# Optimizing a Trainium2 kernel written in Bass

```python
import math
import jax, jax.numpy as jnp
from jax import lax
import numpy as np

D_MODEL = 1024
BATCH = 1
SEQ = 256
DEPTH = 1

MEM_LEN = 256
DA_HEADS = 8
DA_DK = D_MODEL // (2 * DA_HEADS)
DA_DV = 2 * DA_DK
Q_BLOCK = 128
RET_HEADS = 4
RET_DV = D_MODEL // RET_HEADS
RET_DK = RET_DV // 2
RET_CHUNK = 128
MEM_HEADS = 4
MEM_DH = D_MODEL // MEM_HEADS
N_BRANCH = 3
BRANCH_W = D_MODEL
N_GROUPS = 4
EXPERTS_PER_GROUP = 4
N_EXPERTS = N_GROUPS * EXPERTS_PER_GROUP
EXPERT_TOPK = 2
D_FF_EXPERT = D_MODEL // 2
DEEPNORM_ALPHA = (2.0 * DEPTH) ** 0.25
DEEPNORM_BETA = (8.0 * DEPTH) ** -0.25
EPS = 1e-5

SPLIT_SIZES = (DA_HEADS * 2 * DA_DK, DA_HEADS * 2 * DA_DK, DA_HEADS * DA_DV,
               RET_HEADS * RET_DK, RET_HEADS * RET_DK, RET_HEADS * RET_DV, RET_HEADS * RET_DV,
               MEM_HEADS * MEM_DH, N_BRANCH * D_MODEL)
SPLIT_POINTS = tuple(int(v) for v in np.cumsum(SPLIT_SIZES)[:-1])
IN_WIDTH = int(sum(SPLIT_SIZES))
VALUE_SLOTS = (2, 5)


def layer_norm(x, g, b):
    xf = x.astype(jnp.float32)
    mu = jnp.mean(xf, axis=-1, keepdims=True)
    var = jnp.mean(jnp.square(xf - mu), axis=-1, keepdims=True)
    return ((xf - mu) * lax.rsqrt(var + EPS) * g + b).astype(x.dtype)

def diff_attention(q, k, v, lam_vecs, norm_g, lambda_init):
    B, S, H = q.shape[0], q.shape[1], q.shape[2]
    lv = lam_vecs.astype(jnp.float32)
    lam = jnp.exp(jnp.sum(lv[0] * lv[1])) - jnp.exp(jnp.sum(lv[2] * lv[3])) + lambda_init
    slopes = 2.0 ** (-8.0 * (jnp.arange(H, dtype=jnp.float32) + 1.0) / H)
    kf = k.astype(jnp.float32)
    vf = v.astype(jnp.float32)
    kpos = jnp.arange(S)
    nblk = S // Q_BLOCK
    qb = q.astype(jnp.float32).reshape(B, nblk, Q_BLOCK, H, 2, DA_DK).transpose(1, 0, 2, 3, 4, 5)
    scale = DA_DK ** -0.5

    def block(args):
        q_blk, i = args
        qpos = i * Q_BLOCK + jnp.arange(Q_BLOCK)
        dist = (qpos[:, None] - kpos[None, :]).astype(jnp.float32)
        s = jnp.einsum('bqhcd,bkhcd->bhcqk', q_blk, kf) * scale
        s = s - slopes[None, :, None, None, None] * dist[None, None, None]
        s = jnp.where(dist[None, None, None] >= 0, s, -jnp.inf)
        p = jax.nn.softmax(s, axis=-1)
        a = p[:, :, 0] - lam * p[:, :, 1]
        return jnp.einsum('bhqk,bkhe->bqhe', a, vf)

    o = lax.map(block, (qb, jnp.arange(nblk)))
    o = o.transpose(1, 0, 2, 3, 4).reshape(B, S, H, DA_DV)
    o = o * lax.rsqrt(jnp.mean(jnp.square(o), axis=-1, keepdims=True) + EPS) * norm_g
    return (o * (1.0 - lambda_init)).reshape(B, S, H * DA_DV)

def retention(q, k, v, gn_g, gn_b):
    B, S, H, dk = q.shape
    dv = v.shape[-1]
    C = RET_CHUNK
    n = S // C
    log_g = jnp.log(1.0 - 2.0 ** (-5.0 - jnp.arange(H, dtype=jnp.float32)))
    idx = jnp.arange(C, dtype=jnp.float32)
    rel = idx[:, None] - idx[None, :]
    intra = jnp.where(rel[None] >= 0, jnp.exp(rel[None] * log_g[:, None, None]), 0.0)
    q_decay = jnp.exp((idx[:, None] + 1.0) * log_g[None, :])
    k_decay = jnp.exp((C - 1.0 - idx[:, None]) * log_g[None, :])
    chunk_decay = jnp.exp(C * log_g)
    qf = q.astype(jnp.float32)
    kf = k.astype(jnp.float32) * dk ** -0.5
    vf = v.astype(jnp.float32)
    qc = qf.reshape(B, n, C, H, dk).transpose(1, 0, 2, 3, 4)
    kc = kf.reshape(B, n, C, H, dk).transpose(1, 0, 2, 3, 4)
    vc = vf.reshape(B, n, C, H, dv).transpose(1, 0, 2, 3, 4)

    def step(state, inp):
        qi, ki, vi = inp
        s = jnp.einsum('bqhd,bkhd->bhqk', qi, ki) * intra[None]
        o = (jnp.einsum('bhqk,bkhe->bqhe', s, vi)
             + jnp.einsum('bqhd,bhde->bqhe', qi, state) * q_decay[None, :, :, None])
        new_state = (state * chunk_decay[None, :, None, None]
                     + jnp.einsum('bkhd,bkhe->bhde', ki * k_decay[None, :, :, None], vi))
        return new_state, o

    state0 = jnp.zeros((B, H, dk, dv), jnp.float32)
    _, o = lax.scan(step, state0, (qc, kc, vc))
    o = o.transpose(1, 0, 2, 3, 4).reshape(B, S, H, dv)
    mu = jnp.mean(o, axis=-1, keepdims=True)
    var = jnp.mean(jnp.square(o - mu), axis=-1, keepdims=True)
    o = ((o - mu) * lax.rsqrt(var + EPS)).reshape(B, S, H * dv)
    return o * gn_g + gn_b

def memory_attention(q, k, v):
    B, S = q.shape[0], q.shape[1]
    s = jnp.einsum('bshd,bmhd->bhsm', q.astype(jnp.float32), k.astype(jnp.float32)) * MEM_DH ** -0.5
    p = jax.nn.softmax(s, axis=-1)
    o = jnp.einsum('bhsm,bmhd->bshd', p, v.astype(jnp.float32))
    return o.reshape(B, S, MEM_HEADS * MEM_DH)

def hier_moe(x, w_rg, b_rg, w_re, b_re, w1, w3, w2):
    B, S, D = x.shape
    t = x.reshape(B * S, D)
    p_grp = jax.nn.softmax((t @ w_rg + b_rg).astype(jnp.float32), axis=-1)
    p_top, g_idx = lax.top_k(p_grp, 1)
    e_logits = (t @ w_re + b_re).astype(jnp.float32).reshape(B * S, N_GROUPS, EXPERTS_PER_GROUP)
    sel = jnp.take_along_axis(e_logits, g_idx[:, :, None], axis=1)[:, 0]
    p_exp = jax.nn.softmax(sel, axis=-1)
    pe_top, e_idx = lax.top_k(p_exp, EXPERT_TOPK)
    pe_top = pe_top / jnp.sum(pe_top, axis=-1, keepdims=True)
    w_tok = p_top * pe_top
    flat_idx = g_idx * EXPERTS_PER_GROUP + e_idx
    combine = jnp.sum(jax.nn.one_hot(flat_idx, N_EXPERTS, dtype=jnp.float32) * w_tok[..., None], axis=1)
    out = jnp.zeros((B * S, D), jnp.float32)
    for e in range(N_EXPERTS):
        h = jax.nn.silu(t @ w1[e]) * (t @ w3[e])
        out = out + combine[:, e:e + 1] * (h @ w2[e])
    return out.reshape(B, S, D).astype(x.dtype)

def first_inputs(seed: int = 0) -> dict:
    key = jax.random.key(seed)
    ks = jax.random.split(key, 24)
    D = D_MODEL

    def nrm(k, shape, scale):
        return jax.random.normal(k, shape, jnp.float32) * scale

    col_scale = np.concatenate([np.full(sz, DEEPNORM_BETA if i in VALUE_SLOTS else 1.0, np.float32)
                                for i, sz in enumerate(SPLIT_SIZES)])
    mem_scale = np.concatenate([np.ones(D, np.float32), np.full(D, DEEPNORM_BETA, np.float32)])
    return {
        'x': nrm(ks[0], (BATCH, SEQ, D), 1.0),
        'mem': nrm(ks[1], (BATCH, MEM_LEN, D), 1.0),
        'w_in': nrm(ks[2], (DEPTH, D, IN_WIDTH), D ** -0.5) * jnp.asarray(col_scale),
        'b_gate': nrm(ks[3], (DEPTH, N_BRANCH * D), 0.02),
        'w_mem_kv': nrm(ks[4], (DEPTH, D, 2 * D), D ** -0.5) * jnp.asarray(mem_scale),
        'da_lambda': nrm(ks[5], (DEPTH, 4, DA_DK), 0.1),
        'da_norm_g': 1.0 + nrm(ks[6], (DEPTH, DA_DV), 0.02),
        'ret_gn_g': 1.0 + nrm(ks[7], (DEPTH, RET_HEADS * RET_DV), 0.02),
        'ret_gn_b': nrm(ks[8], (DEPTH, RET_HEADS * RET_DV), 0.02),
        'w_branch': nrm(ks[9], (DEPTH, N_BRANCH, BRANCH_W, D), BRANCH_W ** -0.5),
        'w_o': nrm(ks[10], (DEPTH, D, D), D ** -0.5 * DEEPNORM_BETA),
        'ln1_g': 1.0 + nrm(ks[11], (DEPTH, D), 0.02),
        'ln1_b': nrm(ks[12], (DEPTH, D), 0.02),
        'w_rg': nrm(ks[13], (DEPTH, D, N_GROUPS), D ** -0.5),
        'b_rg': nrm(ks[14], (DEPTH, N_GROUPS), 0.01),
        'w_re': nrm(ks[15], (DEPTH, D, N_EXPERTS), D ** -0.5),
        'b_re': nrm(ks[16], (DEPTH, N_EXPERTS), 0.01),
        'w1': nrm(ks[17], (DEPTH, N_EXPERTS, D, D_FF_EXPERT), D ** -0.5),
        'w3': nrm(ks[18], (DEPTH, N_EXPERTS, D, D_FF_EXPERT), D ** -0.5),
        'w2': nrm(ks[19], (DEPTH, N_EXPERTS, D_FF_EXPERT, D), D_FF_EXPERT ** -0.5 * DEEPNORM_BETA),
        'ln2_g': 1.0 + nrm(ks[20], (DEPTH, D), 0.02),
        'ln2_b': nrm(ks[21], (DEPTH, D), 0.02),
    }

def first_block(x, mem, w_in, b_gate, w_mem_kv, da_lambda, da_norm_g, ret_gn_g, ret_gn_b,
              w_branch, w_o, ln1_g, ln1_b, w_rg, b_rg, w_re, b_re, w1, w3, w2, ln2_g, ln2_b):
    B, S, D = x.shape
    M = mem.shape[1]
    for l in range(DEPTH):
        lambda_init = 0.8 - 0.6 * math.exp(-0.3 * l)
        proj = x @ w_in[l]
        da_q, da_k, da_v, r_q, r_k, r_v, r_g, m_q, gate_logits = jnp.split(proj, SPLIT_POINTS, axis=-1)

        y_da = diff_attention(da_q.reshape(B, S, DA_HEADS, 2, DA_DK),
                              da_k.reshape(B, S, DA_HEADS, 2, DA_DK),
                              da_v.reshape(B, S, DA_HEADS, DA_DV),
                              da_lambda[l], da_norm_g[l], lambda_init).astype(x.dtype)

        y_ret = retention(r_q.reshape(B, S, RET_HEADS, RET_DK),
                          r_k.reshape(B, S, RET_HEADS, RET_DK),
                          r_v.reshape(B, S, RET_HEADS, RET_DV),
                          ret_gn_g[l], ret_gn_b[l])
        y_ret = (jax.nn.silu(r_g.astype(jnp.float32)) * y_ret).astype(x.dtype)

        m_k, m_v = jnp.split(mem @ w_mem_kv[l], 2, axis=-1)
        y_mem = memory_attention(m_q.reshape(B, S, MEM_HEADS, MEM_DH),
                                 m_k.reshape(B, M, MEM_HEADS, MEM_DH),
                                 m_v.reshape(B, M, MEM_HEADS, MEM_DH)).astype(x.dtype)

        gates = jax.nn.sigmoid(gate_logits + b_gate[l]).reshape(B, S, N_BRANCH, D)
        branches = jnp.stack([y_da, y_ret, y_mem], axis=2)
        branch_d = jnp.einsum('bsnc,ncd->bsnd', branches, w_branch[l])
        merged = jnp.sum(gates * branch_d, axis=2)
        x = layer_norm(DEEPNORM_ALPHA * x + merged @ w_o[l], ln1_g[l], ln1_b[l])

        y_moe = hier_moe(x, w_rg[l], b_rg[l], w_re[l], b_re[l], w1[l], w3[l], w2[l])
        x = layer_norm(DEEPNORM_ALPHA * x + y_moe, ln2_g[l], ln2_b[l])
    return x


_first_inputs = first_inputs


def first_inputs(seed=0):
    import zlib

    import numpy as np

    out = dict(_first_inputs(seed))
    spreads = {}
    factors = {'mem': 2.814,
     'b_gate': 8.0,
     'w_mem_kv': 2.715,
     'da_lambda': 3.501,
     'da_norm_g': 74.833,
     'ret_gn_g': 106.684,
     'ret_gn_b': 108.9,
     'b_rg': 18.856,
     'b_re': 26.31,
     'ln2_g': 26.042,
     'ln2_b': 24.107}
    for name, (base, spread) in spreads.items():
        noise = np.random.default_rng([zlib.crc32(name.encode()), seed]).standard_normal(out[name].shape)
        drawn = base * np.exp(spread * noise) if base else spread * noise
        out[name] = __import__('jax').numpy.asarray(drawn.astype(out[name].dtype))
    for name, factor in factors.items():
        out[name] = (out[name] * factor).astype(out[name].dtype)
    return out


_narrow_inputs = first_inputs


def first_inputs(seed=0):

    out = dict(_narrow_inputs(seed))
    wider = {'da_norm_g': 3.74, 'ret_gn_g': 3.54, 'ret_gn_b': 3.53, 'ln2_g': 3.34, 'ln2_b': 3.34}
    for name, times in wider.items():
        mean = out[name].mean()
        out[name] = (mean + times * (out[name] - mean)).astype(out[name].dtype)
    return out


DEPTH_2 = 2

N_EVEN = (DEPTH_2 + 1) // 2
N_ODD = DEPTH_2 // 2
ALPHA = (2.0 * DEPTH_2) ** 0.25
BETA = (8.0 * DEPTH_2) ** -0.25
LN_EPS = 1e-5

POOL_WINDOWS = (2, 4, 8, 16)
POOL_GROUPS = len(POOL_WINDOWS)
POOL_CH = D_MODEL // 8
POOL_WIDTH = POOL_GROUPS * POOL_CH
HEAD_DIM = 64
N_Q_HEADS = D_MODEL // 128
N_KV_HEADS = 2
Q_GROUP = N_Q_HEADS // N_KV_HEADS
ATTN_WIDTH = N_Q_HEADS * HEAD_DIM
KV_WIDTH = N_KV_HEADS * HEAD_DIM
WINDOW = 128
BLOCK = 128
EVEN_IN = POOL_WIDTH + ATTN_WIDTH + 2 * KV_WIDTH
EVEN_MIX = POOL_WIDTH + ATTN_WIDTH

CHUNK = 128
SG_WIDTH = D_MODEL
SG_GROUPS = 8
SG_CH = SG_WIDTH // SG_GROUPS

D_FF = ((8 * D_MODEL // 3 + 127) // 128) * 128
N_EXPERTS_2 = 8
TOP_K = 2
D_FF_EXPERT_2 = 7 * D_MODEL // 2


def layer_norm_2(x, g, b):
    xf = x.astype(jnp.float32)
    mu = jnp.mean(xf, axis=-1, keepdims=True)
    var = jnp.mean(jnp.square(xf - mu), axis=-1, keepdims=True)
    return ((xf - mu) * lax.rsqrt(var + LN_EPS) * g + b).astype(x.dtype)

def pool_mixer(p, w_pool, pool_scale):
    B_, S, _ = p.shape
    pf = p.astype(jnp.float32)
    cs = jnp.concatenate([jnp.zeros((B_, 1, POOL_WIDTH), jnp.float32), jnp.cumsum(pf, axis=1)], axis=1)
    t = jnp.arange(S)
    outs = []
    for g, w in enumerate(POOL_WINDOWS):
        r = w // 2
        lo = jnp.maximum(t - r, 0)
        hi = jnp.minimum(t + r + 1, S)
        sl = slice(g * POOL_CH, (g + 1) * POOL_CH)
        csg = cs[..., sl]
        cnt = (hi - lo).astype(jnp.float32)[None, :, None]
        outs.append((csg[:, hi] - csg[:, lo]) / cnt - pf[..., sl])
    pooled = jnp.stack(outs, axis=2).astype(p.dtype)
    y = jnp.einsum('bsgc,gcd->bsgd', pooled, w_pool)
    return y.reshape(B_, S, POOL_WIDTH) * pool_scale

def windowed_gqa(q, k, v, sink):
    B_, S, _, _ = q.shape
    nb = S // BLOCK
    qb = q.reshape(B_, nb, BLOCK, N_KV_HEADS, Q_GROUP, HEAD_DIM)
    pad = ((0, 0), (BLOCK, BLOCK), (0, 0), (0, 0))
    kp = jnp.pad(k, pad).reshape(B_, nb + 2, BLOCK, N_KV_HEADS, HEAD_DIM)
    vp = jnp.pad(v, pad).reshape(B_, nb + 2, BLOCK, N_KV_HEADS, HEAD_DIM)
    kw = jnp.concatenate([kp[:, :-2], kp[:, 1:-1], kp[:, 2:]], axis=2)
    vw = jnp.concatenate([vp[:, :-2], vp[:, 1:-1], vp[:, 2:]], axis=2)
    scores = jnp.einsum('bnqhgd,bnshd->bnhgqs', qb, kw).astype(jnp.float32) * (HEAD_DIM ** -0.5)
    i = jnp.arange(BLOCK)[:, None]
    j = jnp.arange(3 * BLOCK)[None, :]
    dist = jnp.abs(j - BLOCK - i)
    key_pos = jnp.arange(nb)[:, None] * BLOCK - BLOCK + jnp.arange(3 * BLOCK)[None, :]
    valid = (key_pos >= 0) & (key_pos < S)
    mask = (dist <= WINDOW)[None] & valid[:, None, :]
    slopes = 2.0 ** (-8.0 * jnp.arange(1, N_Q_HEADS + 1, dtype=jnp.float32) / N_Q_HEADS)
    alibi = -slopes.reshape(N_KV_HEADS, Q_GROUP)[:, :, None, None] * dist.astype(jnp.float32)
    scores = jnp.where(mask[None, :, None, None], scores + alibi, -1e30)
    sink_b = sink.astype(jnp.float32).reshape(N_KV_HEADS, Q_GROUP)[None, None, :, :, None, None]
    m = jnp.maximum(jnp.max(scores, axis=-1, keepdims=True), sink_b)
    pexp = jnp.exp(scores - m)
    probs = pexp / (jnp.sum(pexp, axis=-1, keepdims=True) + jnp.exp(sink_b - m))
    out = jnp.einsum('bnhgqs,bnshd->bnqhgd', probs.astype(v.dtype), vw)
    return out.reshape(B_, S, ATTN_WIDTH)

def even_mixer(h, w_in, w_pool, pool_scale, sink, w_out):
    B_, S, _ = h.shape
    z = h @ w_in
    p, q, k, v = jnp.split(z, [POOL_WIDTH, POOL_WIDTH + ATTN_WIDTH, POOL_WIDTH + ATTN_WIDTH + KV_WIDTH], axis=-1)
    ya = pool_mixer(p, w_pool, pool_scale)
    yb = windowed_gqa(q.reshape(B_, S, N_Q_HEADS, HEAD_DIM),
                      k.reshape(B_, S, N_KV_HEADS, HEAD_DIM),
                      v.reshape(B_, S, N_KV_HEADS, HEAD_DIM), sink)
    return jnp.concatenate([ya, yb], axis=-1) @ w_out

def spatial_gating_mixer(h, w_in, sg_ln_g, sg_ln_b, w_s, b_s, w_out):
    B_, S, _ = h.shape
    z = jax.nn.gelu(h @ w_in)
    u, v = jnp.split(z, 2, axis=-1)
    v = layer_norm_2(v, sg_ln_g, sg_ln_b)
    vc = v.reshape(B_, S // CHUNK, CHUNK, SG_GROUPS, SG_CH)
    sv = jnp.einsum('gts,bnsgc->bntgc', w_s, vc) + b_s.T[None, None, :, :, None]
    return (u * sv.reshape(B_, S, SG_WIDTH)) @ w_out

def swiglu(h, w_gate, w_up, w_down):
    return (jax.nn.silu(h @ w_gate) * (h @ w_up)) @ w_down

def moe_swiglu(h, w_router, w_gate, w_up, w_down):
    logits = (h @ w_router).astype(jnp.float32)
    top_v, top_i = lax.top_k(logits, TOP_K)
    gates = jax.nn.softmax(top_v, axis=-1)
    dense_gate = jnp.sum(jax.nn.one_hot(top_i, N_EXPERTS_2, dtype=jnp.float32) * gates[..., None], axis=-2)
    y = jnp.zeros_like(h)
    for e in range(N_EXPERTS_2):
        y = y + dense_gate[..., e:e + 1].astype(h.dtype) * swiglu(h, w_gate[e], w_up[e], w_down[e])
    return y

def second_inputs(seed: int = 0) -> dict:
    key = jax.random.key(seed)
    ks = jax.random.split(key, 32)
    f32 = jnp.float32
    D = D_MODEL

    def nrm(k, shape, scale):
        return jax.random.normal(k, shape, f32) * scale

    x = nrm(ks[0], (BATCH, SEQ, D), 1.0)
    c = nrm(ks[1], (BATCH, D), 1.0)
    ada_w = nrm(ks[2], (DEPTH_2, D, 6 * D), 0.1 * D ** -0.5)
    ada_b = nrm(ks[3], (DEPTH_2, 6 * D), 0.01)
    ln_g = 1.0 + nrm(ks[4], (DEPTH_2, 2, D), 0.02)
    ln_b = nrm(ks[5], (DEPTH_2, 2, D), 0.01)

    ev_w_in = nrm(ks[6], (N_EVEN, D, EVEN_IN), D ** -0.5)
    col_scale = jnp.concatenate([jnp.full((EVEN_IN - KV_WIDTH,), 1.0, f32), jnp.full((KV_WIDTH,), BETA, f32)])
    ev_w_in = ev_w_in * col_scale
    ev_pool_w = nrm(ks[7], (N_EVEN, POOL_GROUPS, POOL_CH, POOL_CH), POOL_CH ** -0.5)
    ev_pool_scale = 1.0 + nrm(ks[8], (N_EVEN, POOL_WIDTH), 0.02)
    ev_sink = nrm(ks[9], (N_EVEN, N_Q_HEADS), 0.5)
    ev_w_out = nrm(ks[10], (N_EVEN, EVEN_MIX, D), BETA * EVEN_MIX ** -0.5)

    od_w_in = nrm(ks[11], (N_ODD, D, 2 * SG_WIDTH), D ** -0.5)
    od_sg_ln_g = 1.0 + nrm(ks[12], (N_ODD, SG_WIDTH), 0.02)
    od_sg_ln_b = nrm(ks[13], (N_ODD, SG_WIDTH), 0.01)
    od_w_s = nrm(ks[14], (N_ODD, SG_GROUPS, CHUNK, CHUNK), CHUNK ** -0.5)
    od_b_s = 1.0 + nrm(ks[15], (N_ODD, SG_GROUPS, CHUNK), 0.02)
    od_w_out = nrm(ks[16], (N_ODD, SG_WIDTH, D), BETA * SG_WIDTH ** -0.5)

    ffn_w_gate = nrm(ks[17], (N_EVEN, D, D_FF), BETA * D ** -0.5)
    ffn_w_up = nrm(ks[18], (N_EVEN, D, D_FF), BETA * D ** -0.5)
    ffn_w_down = nrm(ks[19], (N_EVEN, D_FF, D), BETA * D_FF ** -0.5)

    moe_w_router = nrm(ks[20], (N_ODD, D, N_EXPERTS_2), D ** -0.5)
    moe_w_gate = nrm(ks[21], (N_ODD, N_EXPERTS_2, D, D_FF_EXPERT_2), BETA * D ** -0.5)
    moe_w_up = nrm(ks[22], (N_ODD, N_EXPERTS_2, D, D_FF_EXPERT_2), BETA * D ** -0.5)
    moe_w_down = nrm(ks[23], (N_ODD, N_EXPERTS_2, D_FF_EXPERT_2, D), BETA * D_FF_EXPERT_2 ** -0.5)

    return {"x": x, "c": c, "ada_w": ada_w, "ada_b": ada_b, "ln_g": ln_g, "ln_b": ln_b,
            "ev_w_in": ev_w_in, "ev_pool_w": ev_pool_w, "ev_pool_scale": ev_pool_scale,
            "ev_sink": ev_sink, "ev_w_out": ev_w_out,
            "od_w_in": od_w_in, "od_sg_ln_g": od_sg_ln_g, "od_sg_ln_b": od_sg_ln_b,
            "od_w_s": od_w_s, "od_b_s": od_b_s, "od_w_out": od_w_out,
            "ffn_w_gate": ffn_w_gate, "ffn_w_up": ffn_w_up, "ffn_w_down": ffn_w_down,
            "moe_w_router": moe_w_router, "moe_w_gate": moe_w_gate, "moe_w_up": moe_w_up,
            "moe_w_down": moe_w_down}

def second_block(x, c, ada_w, ada_b, ln_g, ln_b,
              ev_w_in, ev_pool_w, ev_pool_scale, ev_sink, ev_w_out,
              od_w_in, od_sg_ln_g, od_sg_ln_b, od_w_s, od_b_s, od_w_out,
              ffn_w_gate, ffn_w_up, ffn_w_down,
              moe_w_router, moe_w_gate, moe_w_up, moe_w_down):
    cond = jax.nn.silu(c)
    for l in range(DEPTH_2):
        mod = (cond @ ada_w[l] + ada_b[l])[:, None, :]
        sh_m, sc_m, g_m, sh_f, sc_f, g_f = jnp.split(mod, 6, axis=-1)
        e = l // 2
        h = x * (1.0 + sc_m) + sh_m
        if l % 2 == 0:
            y = even_mixer(h, ev_w_in[e], ev_pool_w[e], ev_pool_scale[e], ev_sink[e], ev_w_out[e])
        else:
            y = spatial_gating_mixer(h, od_w_in[e], od_sg_ln_g[e], od_sg_ln_b[e], od_w_s[e], od_b_s[e], od_w_out[e])
        x = layer_norm_2(ALPHA * x + (1.0 + g_m) * y, ln_g[l, 0], ln_b[l, 0])
        h = x * (1.0 + sc_f) + sh_f
        if l % 2 == 0:
            y = swiglu(h, ffn_w_gate[e], ffn_w_up[e], ffn_w_down[e])
        else:
            y = moe_swiglu(h, moe_w_router[e], moe_w_gate[e], moe_w_up[e], moe_w_down[e])
        x = layer_norm_2(ALPHA * x + (1.0 + g_f) * y, ln_g[l, 1], ln_b[l, 1])
    return x


_first_inputs_2 = second_inputs


def second_inputs(seed=0):
    import zlib

    import numpy as np

    out = dict(_first_inputs_2(seed))
    spreads = {}
    factors = {'ada_b': 6.856,
     'ev_pool_scale': 8.0,
     'ev_sink': 8.0,
     'od_sg_ln_g': 8.0,
     'od_sg_ln_b': 8.0,
     'od_b_s': 8.0}
    for name, (base, spread) in spreads.items():
        noise = np.random.default_rng([zlib.crc32(name.encode()), seed]).standard_normal(out[name].shape)
        drawn = base * np.exp(spread * noise) if base else spread * noise
        out[name] = __import__('jax').numpy.asarray(drawn.astype(out[name].dtype))
    for name, factor in factors.items():
        out[name] = (out[name] * factor).astype(out[name].dtype)
    return out


_narrow_inputs_2 = second_inputs


def second_inputs(seed=0):

    out = dict(_narrow_inputs_2(seed))
    wider = {'ev_sink': 6.32, 'od_sg_ln_g': 4.78, 'od_sg_ln_b': 9.05, 'od_b_s': 5.03}
    for name, times in wider.items():
        mean = out[name].mean()
        out[name] = (mean + times * (out[name] - mean)).astype(out[name].dtype)
    return out


def setup_inputs(seed=0):
    out = dict(first_inputs(seed))
    for name, value in second_inputs(seed + 1).items():
        if name != "x":
            out[name + "_2"] = value
    return out


def reference(
    x, mem, w_in, b_gate, w_mem_kv, da_lambda, da_norm_g, ret_gn_g, ret_gn_b, w_branch, w_o,
    ln1_g, ln1_b, w_rg, b_rg, w_re, b_re, w1, w3, w2, ln2_g, ln2_b, c_2, ada_w_2, ada_b_2,
    ln_g_2, ln_b_2, ev_w_in_2, ev_pool_w_2, ev_pool_scale_2, ev_sink_2, ev_w_out_2, od_w_in_2,
    od_sg_ln_g_2, od_sg_ln_b_2, od_w_s_2, od_b_s_2, od_w_out_2, ffn_w_gate_2, ffn_w_up_2,
    ffn_w_down_2, moe_w_router_2, moe_w_gate_2, moe_w_up_2, moe_w_down_2,
):
    x = first_block(
        x, mem, w_in, b_gate, w_mem_kv, da_lambda, da_norm_g, ret_gn_g, ret_gn_b, w_branch, w_o,
        ln1_g, ln1_b, w_rg, b_rg, w_re, b_re, w1, w3, w2, ln2_g, ln2_b,
    )
    return second_block(
        x, c_2, ada_w_2, ada_b_2, ln_g_2, ln_b_2, ev_w_in_2, ev_pool_w_2, ev_pool_scale_2,
        ev_sink_2, ev_w_out_2, od_w_in_2, od_sg_ln_g_2, od_sg_ln_b_2, od_w_s_2, od_b_s_2,
        od_w_out_2, ffn_w_gate_2, ffn_w_up_2, ffn_w_down_2, moe_w_router_2, moe_w_gate_2,
        moe_w_up_2, moe_w_down_2,
    )


_drawn_inputs = setup_inputs


def setup_inputs(seed=0):
    import zlib

    import numpy as np

    out = dict(_drawn_inputs(seed))
    spreads = {}
    factors = {}
    for name, (base, spread) in spreads.items():
        noise = np.random.default_rng([zlib.crc32(name.encode()), seed]).standard_normal(out[name].shape)
        drawn = base * np.exp(spread * noise) if base else spread * noise
        out[name] = __import__('jax').numpy.asarray(drawn.astype(out[name].dtype))
    for name, factor in factors.items():
        out[name] = (out[name] * factor).astype(out[name].dtype)
    return out
```

```python
from contextlib import ExitStack

import numpy as np
import concourse.bass as bass
from concourse import mybir

F32 = mybir.dt.float32
I32 = mybir.dt.int32
ALU = mybir.AluOpType
ACT = mybir.ActivationFunctionType
AX = mybir.AxisListType

P = 128
D = 1024
KT = D // P
T = 256
TB = T // P
PANEL = 512
SLOT = KT * PANEL
SLOTS = 7
DENSE_SLOTS = 5
LATER_SLOTS = 6
BANKS = 8
EPS = 1e-5
NEG = -1e30

DA_H, RET_H, MEM_H = 8, 4, 4
LAMBDA_INIT = 0.2
ALPHA1 = 2.0 ** 0.25
ALPHA2 = 4.0 ** 0.25
G1, E1, N1 = 4, 4, 16
N2 = 8
FF1 = 512
FF2 = 3584
FFN = 2816
POOL_W = (2, 4, 8, 16)
GQA_H, GQA_KV, GQA_D = 8, 2, 64
WIN = 128
SG_G = 8

TIERS = ((P, T), (P, T))
VEC_A = {}
VEC_B = {}
for _table, _rows in ((VEC_A, (("b_gate", 24), ("gn_g", 8), ("gn_b", 8), ("ln1_g", 8), ("ln1_b", 8), ("da_g", 1),
                               ("ln2_g", 8), ("ln2_b", 8), ("lng_2", 32), ("c", 8), ("pool_scale", 4))),
                      (VEC_B, (("ada_b", 96), ("lnb_2", 32)))):
    _at = 0
    for _name, _n in _rows:
        _table[_name] = (_at, _n)
        _at += _n

C_IDENT, C_USTRICT, C_IOTA = 0, 128, 256
C_COMMON = 512
C_PHASE = 2560


def shape_constants():
    out = np.zeros((P, C_COMMON + 2 * C_PHASE), np.float32)
    i = np.arange(P)
    out[:, C_IDENT:C_IDENT + P] = np.eye(P)
    out[:, C_USTRICT:C_USTRICT + P] = i[:, None] < i[None, :]
    out[:, C_IOTA:C_IOTA + T] = np.arange(T)
    t = np.arange(T)
    dist = (t[:, None] - t[None, :]).astype(np.float64)
    causal = np.where(dist >= 0, -dist, NEG)
    window = np.where(np.abs(dist) <= WIN, -np.abs(dist), NEG)
    for b in range(TB):
        out[:, C_COMMON + b * T:C_COMMON + (b + 1) * T] = causal[b * P:(b + 1) * P]
        out[:, C_COMMON + C_PHASE + b * T:C_COMMON + C_PHASE + (b + 1) * T] = window[b * P:(b + 1) * P]
    for h in range(RET_H):
        log_g = np.log(1.0 - 2.0 ** (-5.0 - h))
        m = np.where(dist.T <= 0, 0.0, 0.0)
        m = np.where(dist >= 0, np.exp(np.maximum(dist, 0) * log_g), 0.0).T * (128.0 ** -0.5)
        for b in range(TB):
            at = C_COMMON + 2 * T + (h * TB + b) * T
            out[:, at:at + T] = m[b * P:(b + 1) * P]
    for g, w in enumerate(POOL_W):
        r = w // 2
        lo, hi = np.maximum(t - r, 0), np.minimum(t + r + 1, T)
        m = ((t[:, None] >= lo[None]) & (t[:, None] < hi[None])) / (hi - lo)[None] - np.eye(T)
        for b in range(TB):
            at = C_COMMON + C_PHASE + 2 * T + (g * TB + b) * T
            out[:, at:at + T] = m[b * P:(b + 1) * P]
    return out


def mixer1_steps():
    s = [("turn_x", i, 0) for i in range(4)]
    s += [("gemm", "da_q", i) for i in range(4)] + [("gemm", "da_k", i) for i in range(4)]
    s += [("vec", 0, 0), ("vec", 1, 0)]
    s += [("turn_mem", i, 0) for i in range(4)]
    s += [("gemm", "da_v", i) for i in range(4)]
    fill = [("gemm", n, i) for n, k in (("r_q", 2), ("r_k", 2), ("r_v", 4), ("r_g", 4), ("gate0", 4)) for i in range(k)]
    for h in range(DA_H):
        s += [("da_score", h, 0), ("da_score", h, 1), fill.pop(0)]
        if h:
            s += [("da_norm", h - 1, 0)]
        s += [fill.pop(0), ("da_turn", h, 0), ("ada", 0, h), ("da_out", h, 0)]
    s += [("ret_score", 0, 0), ("da_norm", DA_H - 1, 0)]
    s += [("gemm", "branch0", i) for i in range(4)]
    fill = [("gemm", n, i) for n, k in (("m_q", 4), ("m_k", 4), ("m_v", 4)) for i in range(k)]
    for h in range(RET_H):
        if h:
            s += [("ret_score", h, 0), fill.pop(0)]
        s += [("ret_out", h, 0), fill.pop(0), ("ada", 0, DA_H + h), ("ret_mean", h, 0), fill.pop(0), ("ret_var", h, 0)]
    s += fill
    fill = [("gemm", n, i) for n, k in (("gate1", 4), ("branch1", 4)) for i in range(k)]
    for h in range(MEM_H):
        s += [("mem_score", h, 0), fill.pop(0), ("mem_turn", h, 0), fill.pop(0), ("mem_out", h, 0), ("ada", 1, h)]
    for n in ("gate2", "branch2"):
        for i in range(4):
            s += [("gemm", n, i)] + [("ada", 1, MEM_H + (4 if n == "branch2" else 0) + i)]
    s += [("gemm", "w_o", i) for i in range(4)]
    s += [("ln_sum", 0, 0), ("ln_sq", 0, 0), ("logits", 0, 0)]
    s += [("turn_tok", 0, i) for i in range(4)]
    return s + [("rank", 0, 0)]


def mixer2_steps():
    s = [("ln_sum", 1, 0), ("ln_sq", 1, 0)]
    s += [("gemm", "ev_p", i) for i in range(2)] + [("gemm", "ev_q", i) for i in range(2)]
    s += [("ev_k", 0, 0), ("ev_v", 0, 0)]
    fill = [("pool", 0, 0), ("pool", 1, 0), ("pool_map", 0, 0), ("pool_map", 1, 0)]
    s += [("gqa_score", 0, 0), ("gqa_score", 1, 0)] + fill
    for h in range(GQA_H):
        s += [("gqa_turn", h, 0)]
        if h + 2 < GQA_H:
            s += [("gqa_score", h + 2, 0)]
        s += [("gqa_out", h, 0)]
    s += [("gemm", "ev_o", i) for i in range(4)]
    return s + [("ln_sum", 2, 0), ("ln_sq", 2, 0)]


def mixer3_steps():
    s = [("ln_sum", 3, 0), ("ln_sq", 3, 0), ("turn_ws", 0, 0), ("turn_ws", 1, 0)]
    s += [("gemm", "od_v", i) for i in range(4)] + [("gemm", "od_u", i) for i in range(4)]
    s += [("gate_s", i, 0) for i in range(4)]
    s += [("gemm", "od_o", i) for i in range(4)]
    s += [("ln_sum", 4, 0), ("ln_sq", 4, 0), ("logits", 1, 0)]
    s += [("turn_tok", 1, i) for i in range(4)]
    return s + [("rank", 1, 0)]


def last_steps():
    return [("ln_sum", 5, 0), ("ln_sq", 5, 0)] + [("turn_out", i, 0) for i in range(4)]


A_CONST, A_PHASE, A_COLA, A_COLB, A_MOD, A_SMALL = 0, 640, 3200, 3328, 3456, 3584
R_X, R_MEM, R_Q, R_K, R_V, R_RQ, R_RK, R_RV, R_RG, R_YDA, R_TAIL = (
    4096, 6144, 8192, 10240, 12288, 14336, 15360, 16384, 18432, 20480, 22528)
ARENA = 23936
W_TURN, W_ROWS, W_BIAS = SLOT * LATER_SLOTS, SLOT * LATER_SLOTS + 1024, SLOT * LATER_SLOTS + 3072
S_LOGIT, S_E, S_A, S_AT, S_OSQ, S_RSTD, S_RSQ, S_GATE, S_MERGED = 0, 512, 1024, 1536, 2048, 2304, 2560, 3072, 5120


def build(nc, w, out):
    ctx = ExitStack()

    def sem(name):
        return ctx.enter_context(nc.semaphore(name))

    ring = ctx.enter_context(nc.sbuf_tensor("ring", [P, SLOTS * SLOT], F32))
    arena = ctx.enter_context(nc.sbuf_tensor("arena", [P, ARENA], F32))
    counts_i = ctx.enter_context(nc.sbuf_tensor("counts_i", [P, N1], I32))
    psum = ctx.enter_context(nc.psum_tensor("psum", [P, BANKS, 512], F32))

    def region(at, *shape):
        n = int(np.prod(shape))
        v = arena[:, at:at + n]
        if len(shape) == 2:
            return v.rearrange("p (a b) -> p a b", b=shape[1])
        if len(shape) == 3:
            return v.rearrange("p (a b c) -> p a b c", b=shape[1], c=shape[2])
        return v

    def scratch(at, *shape):
        n = int(np.prod(shape))
        v = ring[:, DENSE_SLOTS * SLOT + at:DENSE_SLOTS * SLOT + at + n]
        return v.rearrange("p (a b) -> p a b", b=shape[1]) if len(shape) == 2 else v

    def slot(s, a):
        return ring[:, s * SLOT:(s + 1) * SLOT].rearrange("p (a b) -> p a b", a=a)

    def bank(b, *shape):
        v = psum[:, b, :]
        return v.rearrange("p (a b) -> p a b", b=shape[1]) if shape else v

    def over(v, n):
        return v.unsqueeze(1).to_broadcast([v.shape[0], n, v.shape[1]])

    def along(v, n):
        return v.unsqueeze(2).to_broadcast([v.shape[0], v.shape[1], n])

    ident = region(A_CONST + C_IDENT, P)
    ustrict = region(A_CONST + C_USTRICT, P)
    iota = region(A_CONST + C_IOTA, T)
    ones = region(A_CONST + 512, P)
    causal = region(A_PHASE, TB, T)
    decay = region(A_PHASE + 2 * T, RET_H * TB, T)
    wbias = region(A_PHASE, TB, T)
    pool_m = region(A_PHASE + 2 * T, len(POOL_W) * TB, T)
    vec_a = scratch(S_LOGIT, P)
    vec_b = scratch(S_E, P)
    cols_a, cols_b = region(A_COLA, P), region(A_COLB, P)
    vec_rows = [sum(n for _, n in table.values()) for table in (VEC_A, VEC_B)]
    mod = region(A_MOD, 2 * 48)
    small = region(A_SMALL, 512)
    lam_rows, lam_prod, lam_sum = scratch(S_A, 4 * 64), scratch(S_AT, 2, 64), small[:, 0:2]
    lam_exp, neg_lam = small[:, 2:4], small[:, 4:5]
    cond = small[:, 8:16]
    sink = small[:, 16:24]
    bias_r1 = small[:, 24:44]
    dmax, dsum, drec = small[:, 44:46], small[:, 46:48], small[:, 48:50]
    da_gain = small[:, 50:51]
    eps = small[:, 51:52]
    esink = small[:, 52:54]
    modp1 = small[:, 64:64 + 2 * 48]

    def col_a(name, k=0):
        at = VEC_A[name][0] + k
        return cols_a[:, at:at + 1]

    def col_b(name, k=0):
        at = VEC_B[name][0] + k
        return cols_b[:, at:at + 1]

    xT, memT, yda = region(R_X, KT, T), region(R_MEM, KT, T), region(R_YDA, KT, T)
    x_tok, mem_tok = region(R_Q, TB, D), region(R_RV, TB, D)
    daq, dak, dav = region(R_Q, KT, T), region(R_K, KT, T), region(R_V, TB, D)
    rq, rk, rv, rg = region(R_RQ, RET_H, T), region(R_RK, RET_H, T), region(R_RV, TB, D), region(R_RG, KT, T)
    mq, mk, mv = daq, dak, dav
    ymem, yret = memT, rg
    gate, merged = scratch(S_GATE, KT, T), scratch(S_MERGED, KT, T)
    logit, e_prob, a_prob, a_turn = (scratch(S_LOGIT, 2, T), scratch(S_E, 2, T), scratch(S_A, TB, T),
                                     scratch(S_AT, 2, T))
    osq, rstd = scratch(S_OSQ, T), scratch(S_RSTD, T)
    ret_s, ret_o, ret_stat, ret_sq = (region(R_TAIL, 2, T), region(R_TAIL + 512, 2, T), region(R_TAIL + 1024, T),
                                      scratch(S_RSQ, 2, T))
    gtmp = ret_sq
    z, z_sq = region(R_Q, KT, T), region(R_K, KT, T)
    ln_stat = region(R_TAIL + 1024, T)
    ada_sum = scratch(7168, 2, PANEL)
    router = (small[:, 160:320].rearrange("p (k e) -> p k e", e=G1 + N1),
              small[:, 320:384].rearrange("p (k e) -> p k e", e=N2))

    acc, hT = region(R_X, KT, T), region(R_MEM, KT, T)
    tok = region(R_V, TB, D)
    xe = region(R_MEM, KT, T)
    h_tile = (region(R_Q, 4, T), region(R_Q + 1024, 4, T))
    s_tile = region(R_K, 4, T)
    perm, perm_w = region(R_K + 1024, TB, T), region(R_K + 1536, TB, T)
    ye = region(R_RQ, KT, T)
    ye_tok = region(R_RV, 2, D)
    spread = region(R_RG, 2, T)
    w_pool = region(R_RG + 1024, 4, P)
    later_sq = region(R_YDA, KT, T)
    mix = region(R_RQ, KT, T)
    p_tok, pooled = region(R_Q, TB, 4 * P), region(R_Q + 1024, 4, T)
    q2, k2, v2 = region(R_K, 4, T), region(R_K + 1024, GQA_KV, T), region(R_K + 1536, TB, P)
    logit2, e2, a2, at2 = (region(R_V, TB, T), region(R_V + 512, TB, T), region(R_V + 1024, TB, T),
                           region(R_V + 1536, TB, T))
    v_tok = region(R_Q, TB, D)
    ws_t = region(R_K, SG_G, P)
    w_s = ring[:, W_TURN:W_TURN + SG_G * P].rearrange("p (g s) -> p g s", s=P)
    sg_rows = ring[:, W_ROWS:W_ROWS + 2 * D].rearrange("p (a d) -> p a d", d=D)
    bs_rows = ring[:, W_BIAS:W_BIAS + D].rearrange("p (g t) -> p g t", t=P)
    out_tok = region(R_V, TB, D)

    def route(at, *shape):
        return region(R_TAIL + at, *shape)

    lg, top_v, top_e, top_1, top_2, sel, hot_g = (route(0, TB, G1 + N1), route(40, TB, N1), route(72, TB, N1),
                                                  route(104, TB, N1), route(136, TB, N1), route(168, TB, N1),
                                                  route(200, TB, G1))
    peak, peak_1, peak_2, ratio, wt_1, wt_2, p_top = (route(208 + 2 * k, TB) for k in range(7))
    desc = route(224, N1)
    ex_g = route(240, TB, G1)
    bn_s, bn_a = route(256, TB, 4 * 6), route(304, TB, 2)
    table = region(R_TAIL + 320, 3 * TB, N1 + 1)
    mine = region(R_TAIL + 432, 3 * TB)

    job_done = sem("job_done")
    bank_free = [sem(f"bank_free{b}") for b in range(BANKS)]
    slot_full = [sem(f"slot_full{s}") for s in range(SLOTS)]
    const_in, x_in, mem_in, vec_in, row_in = (sem("const_in"), sem("x_in"), sem("mem_in"), sem("vec_in"),
                                              sem("row_in"))
    phase_in = sem("phase_in")
    ones_set = sem("ones_set")
    dve_step, act_step = sem("dve_step"), sem("act_step")
    lam_summed, lam_exped, neg_lam_set, cond_set = (sem("lam_summed"), sem("lam_exped"), sem("neg_lam_set"),
                                                    sem("cond_set"))
    da_logits, da_exped, da_probs, da_squared, da_y = (sem("da_logits"), sem("da_exped"), sem("da_probs"),
                                                       sem("da_squared"), sem("da_y"))
    ret_scored, ret_centred, ret_squared, ret_normed, ret_scaled, ret_y = (
        sem("ret_scored"), sem("ret_centred"), sem("ret_squared"), sem("ret_normed"), sem("ret_scaled"), sem("ret_y"))
    mem_max, mem_probs = sem("mem_max"), sem("mem_probs")
    gated, merged_set = sem("gated"), sem("merged_set")
    ln_centred, ln_squared, ln_normed, ln_out = sem("ln_centred"), sem("ln_squared"), sem("ln_normed"), sem("ln_out")
    ada_summed = sem("ada_summed")
    router_in, small_in, modp1_set, modulated, acc_scaled = (sem("router_in"), sem("small_in"), sem("modp1_set"),
                                                             sem("modulated"), sem("acc_scaled"))
    route_diff, route_exp, masks_set, counts_set = sem("route_diff"), sem("route_exp"), sem("masks_set"), sem("counts_set")
    gqa_logits, gqa_exped, gqa_probs = sem("gqa_logits"), sem("gqa_exped"), sem("gqa_probs")
    v_normed, sg_gated, z_set = sem("v_normed"), sem("sg_gated"), sem("z_set")
    mine_set = sem("mine_set")
    perm_set, xe_set, spread_set, silu_set, h_set = (sem("perm_set"), sem("xe_set"), sem("spread_set"),
                                                     sem("silu_set"), sem("h_set"))
    ye_copied, ye_turned, added = sem("ye_copied"), sem("ye_turned"), sem("added")
    out_staged, out_stored = sem("out_staged"), sem("out_stored")

    plans = (mixer1_steps(), mixer2_steps(), mixer3_steps(), last_steps())
    EXPERT1, EXPERT2 = 5 + 5 + 6, 5 + 5 * (FF2 // PANEL) + 6
    FFN_P = [(c, min(PANEL, FFN - c)) for c in range(0, FFN, PANEL)]
    FFN_JOBS = sum(n // P + 1 for _, n in FFN_P)
    index, done, plan_end = {}, {}, []
    at = 0
    for plan, between in zip(plans, (EXPERT1 * N1, FFN_JOBS, EXPERT2 * N2, 0)):
        for s in plan:
            at += 1
            index[s], done[s] = len(index), at
        plan_end.append(at)
        at += between
    EX1, FF0, EX2 = plan_end[0], plan_end[1], plan_end[2]
    H1, HF, H2 = 0, 4 * N1, 4 * N1 + FFN // P
    Y1, YF, Y2 = 0, 4 * N1, 4 * N1 + 4

    def job_bank(s):
        return index[s] % BANKS

    def bank_through(s):
        return bank_free[index[s] % BANKS], index[s] // BANKS + 1

    gemm_src = {}
    at = 0
    for name, cols in (("da_q", 1024), ("da_k", 1024), ("da_v", 1024), ("r_q", 512), ("r_k", 512), ("r_v", 1024),
                       ("r_g", 1024), ("m_q", 1024), ("gate0", 1024), ("gate1", 1024), ("gate2", 1024)):
        gemm_src[name] = (w["w_in"][0], at)
        at += cols
    gemm_src["m_k"], gemm_src["m_v"] = (w["w_mem_kv"][0], 0), (w["w_mem_kv"][0], D)
    for n in range(3):
        gemm_src[f"branch{n}"] = (w["w_branch"][0, n], 0)
    gemm_src["w_o"] = (w["w_o"][0], 0)
    gemm_src["ev_p"], gemm_src["ev_q"] = (w["ev_w_in_2"][0], 0), (w["ev_w_in_2"][0], 512)
    gemm_src["ev_o"] = (w["ev_w_out_2"][0], 0)
    gemm_src["od_u"], gemm_src["od_v"] = (w["od_w_in_2"][0], 0), (w["od_w_in_2"][0], D)
    gemm_src["od_o"] = (w["od_w_out_2"][0], 0)
    token_major = ("da_v", "r_v", "m_v", "ev_p", "od_v")

    def cols(src, c0, n=PANEL):
        return src[:, c0:c0 + n].rearrange("(k p) n -> p k n", p=P)

    fills = [0] * SLOTS
    freed = [None] * SLOTS
    loads = {0: [], 1: [], 2: [], 3: []}
    panel = {}

    def fill_slot(where, key, s, words, src, free):
        loads[where].append((s, words, src, freed[s]))
        fills[s] += 1
        freed[s] = free
        panel[key] = (s, fills[s])

    def plan_loads(n, count, start=0):
        at = start
        for s in plans[n]:
            key, words = s, SLOT
            if s[0] == "gemm" and s[2] % 2 == 0:
                src, c0 = gemm_src[s[1]]
                src, free = cols(src, c0 + s[2] // 2 * PANEL), (job_done, done[("gemm", s[1], s[2] + 1)])
            elif s[0] == "ev_k":
                src, words = cols(w["ev_w_in_2"][0], 1024, 256), KT * 256
                free = (job_done, done[("ev_v", 0, 0)])
            elif s[0] == "ada":
                src, free = cols(w["ada_w_2"][s[1]], s[2] * PANEL), (ada_summed, 12 * s[1] + s[2] + 1)
            else:
                continue
            fill_slot(n, key, at % count, words, src, free)
            at += 1
        return at

    plan_loads(0, DENSE_SLOTS)
    freed[5] = (job_done, done[("gemm", "w_o", 3)])
    BASE1 = list(fills)
    first1 = list(freed)
    for s in range(LATER_SLOTS):
        fills[s] += N1 // 2
        freed[s] = (job_done, EX1 + EXPERT1 * (N1 - 2 + s // 3) + (9 if s % 3 < 2 else 10))
    at = plan_loads(1, LATER_SLOTS)
    jobs = FF0
    for n, (c0, width) in enumerate(FFN_P):
        jobs += width // P
        for name, free in (("gate", jobs), ("up", jobs), ("down", jobs + 1)):
            if name == "down":
                src = w["ffn_w_down_2"][0][c0:c0 + width, :].rearrange("(j p) d -> p j d", p=P)
            else:
                src = cols(w[f"ffn_w_{name}_2"][0], c0, width)
            fill_slot(3, (name, n), at % LATER_SLOTS, KT * width, src, (job_done, free))
            at += 1
        jobs += 1
    plan_loads(2, LATER_SLOTS, at)
    freed[6] = (job_done, done[("gemm", "od_o", 3)])
    BASE2 = list(fills)

    def panel_of(s):
        return panel[("gemm", s[1], s[2] - s[2] % 2) if s[0] == "gemm" else s]

    def layer_norm_scalar(act, n, z, z_sq, sq_done, sq_bank, sq_free, gain_bias, dst):
        for half in range(2):
            act.wait_ge(ln_centred, 2 * n + half + 1)
            act.activation(z_sq[:, 4 * half:4 * half + 4, :], z[:, 4 * half:4 * half + 4, :],
                           ACT.Square).then_inc(ln_squared, 1)
        act.wait_ge(job_done, sq_done)
        act.activation(ln_stat, psum[:, sq_bank, 0:T], ACT.Sqrt, bias=eps, scale=1.0 / D).then_inc(sq_free, 1)
        for k in range(KT):
            if k % 4 == 0:
                act.wait_ge(ln_normed, 2 * n + k // 4 + 1)
            g, b = gain_bias(k)
            act.activation(dst[:, k, :], z[:, k, :], ACT.Identity, bias=b, scale=g).then_inc(ln_out, 1)

    def layer_norm_vector(dve, settle, n, z, sum_done, sum_bank, sum_free, sq_read):
        dve.wait_ge(job_done, sum_done)
        dve.tensor_scalar(ln_stat, psum[:, sum_bank, 0:T], 1.0 / D, None, ALU.mult).then_inc(sum_free[0], 1)
        dve.wait_ge(*sum_free)
        for half in range(2):
            zh = z[:, 4 * half:4 * half + 4, :]
            dve.tensor_tensor(zh, zh, over(ln_stat, 4), ALU.subtract).then_inc(ln_centred, 1)
        dve.wait_ge(ln_centred, 2 * n + 2)
        dve.wait_ge(*sq_read)
        settle(dve.reciprocal(ln_stat, ln_stat))
        for half in range(2):
            zh = z[:, 4 * half:4 * half + 4, :]
            dve.wait_ge(ln_squared, 2 * n + half + 1)
            dve.tensor_tensor(zh, zh, over(ln_stat, 4), ALU.mult).then_inc(ln_normed, 1)

    def by_width(eng, count, widths, body):
        if len(widths) == 1:
            body(widths[0])
            return
        with eng.If(count < widths[0] + 1):
            body(widths[0])
        with eng.Else():
            by_width(eng, count, widths[1:], body)

    def mod_cols(tile, layer, part, k):
        at = layer * 48 + part * KT + k
        return tile[:, at:at + 1]

    def chunks(width):
        return [(c, min(P, width - c * P)) for c in range((width + P - 1) // P)]

    mixtures = (
        dict(n=N1, pairs=1, gain=None, jobs=EXPERT1, at=EX1, h=H1, y=0, add=Y1, turned=0, perm=0, base=BASE1,
             slots=lambda x, t: 3 * (x % 2)),
        dict(n=N2, pairs=FF2 // PANEL, gain=(1, 5), jobs=EXPERT2, at=EX2, h=H2, y=4 * N1, add=Y2, turned=2 * N1,
             perm=N1 + 1, base=BASE2, slots=None),
    )

    block = ctx.enter_context(nc.Block())

    @block.sync
    def _(sp):
        sp.dma_start(x_tok, w["x"][0].rearrange("(b p) d -> p b d", p=P)).then_inc(x_in, 16)
        sp.dma_start(arena[:, 0:C_COMMON], w["consts"][:, 0:C_COMMON]).then_inc(const_in, 16)

        def load(s, words, src, wait):
            if wait:
                sp.wait_ge(*wait)
            dst = ring[:, s * SLOT:s * SLOT + words].rearrange("p (a b) -> p a b", a=src.shape[1])
            sp.dma_start(dst, src).then_inc(slot_full[s], 16)

        def expert_sources(names, x, t):
            gate_w, up_w, down_w = names
            c = slice(t * PANEL, (t + 1) * PANEL)
            return (gate_w[x][:, c].rearrange("(k p) n -> p k n", p=P), up_w[x][:, c].rearrange("(k p) n -> p k n", p=P),
                    down_w[x][c, :].rearrange("(j p) d -> p j d", p=P))

        for one in loads[0]:
            load(*one)
        names1 = (w["w1"][0], w["w3"][0], w["w2"][0])
        for e in range(2):
            for n, src in enumerate(expert_sources(names1, e, 0)):
                load(3 * e + n, SLOT, src, first1[3 * e + n])
        with sp.Fori(1, N1 // 2) as it:
            for e in range(2):
                for n, src in enumerate(expert_sources(names1, it * 2 + e, 0)):
                    load(3 * e + n, SLOT, src,
                         (job_done, it * (2 * EXPERT1) + (EX1 + EXPERT1 * (e - 2) + (9 if n < 2 else 10))))
        for one in loads[1] + loads[3] + loads[2]:
            load(*one)
        names2 = (w["moe_w_gate_2"][0], w["moe_w_up_2"][0], w["moe_w_down_2"][0])

        def freed_in_expert(q):
            return 5 + 5 * (q // 3) + (4 if q % 3 < 2 else 5)

        for q in range(21):
            wait = freed[q] if q < SLOTS else (job_done, EX2 + freed_in_expert(q - SLOTS))
            load(q % SLOTS, SLOT, expert_sources(names2, 0, q // 3)[q % 3], wait)
        with sp.Fori(1, N2) as it:
            for q in range(21):
                before = freed_in_expert(q - SLOTS) if q >= SLOTS else freed_in_expert(q + 14) - EXPERT2
                load(q % SLOTS, SLOT, expert_sources(names2, it, q // 3)[q % 3],
                     (job_done, it * EXPERT2 + (EX2 + before)))
        for i in range(4):
            sp.wait_ge(*bank_through(("turn_out", i, 0)))
            c = slice(i % 2 * 4 * P, (i % 2 + 1) * 4 * P)
            sp.dma_start(out[i // 2 * P:(i // 2 + 1) * P, c], out_tok[:, i // 2, c]).then_inc(out_stored, 16)
        sp.wait_ge(out_stored, 4 * 16)

    @block.gpsimd
    def _(pool):
        nc.gpsimd.memset(ones, 1.0).then_inc(ones_set, 1)
        nc.gpsimd.memset(eps, EPS).then_inc(ones_set, 1)

    @block.scalar
    def _(act):
        step = [0]

        def settle(ins):
            step[0] += 1
            ins.then_inc(act_step, 1)
            act.wait_ge(act_step, step[0])

        def full(s):
            act.wait_ge(job_done, done[s])
            return job_bank(s)

        def evacuated(s):
            act.wait_ge(*bank_through(s))

        for table, tile, names in ((VEC_A, vec_a, {"b_gate": w["b_gate"], "gn_g": w["ret_gn_g"], "gn_b": w["ret_gn_b"],
                                                   "ln1_g": w["ln1_g"], "ln1_b": w["ln1_b"], "da_g": w["da_norm_g"],
                                                   "ln2_g": w["ln2_g"], "ln2_b": w["ln2_b"], "lng_2": w["ln_g_2"],
                                                   "c": w["c_2"], "pool_scale": w["ev_pool_scale_2"]}),
                                   (VEC_B, vec_b, {"ada_b": w["ada_b_2"], "lnb_2": w["ln_b_2"]})):
            for name, src in names.items():
                r0, n = table[name]
                flat = src.rearrange("a b c -> (a b c)") if len(src.shape) == 3 else src.rearrange("a b -> (a b)")
                act.dma_start(tile[r0:r0 + n, :], flat.rearrange("(k p) -> k p", p=P)).then_inc(vec_in, 16)
        act.dma_start(mem_tok, w["mem"][0].rearrange("(b p) d -> p b d", p=P)).then_inc(mem_in, 16)
        act.dma_start(region(A_PHASE, C_PHASE), w["consts"][:, C_COMMON:C_COMMON + C_PHASE]).then_inc(phase_in, 16)
        for dst, src in ((lam_rows, w["da_lambda"][0].rearrange("a b -> (a b)")), (sink, w["ev_sink_2"][0]),
                         (bias_r1[:, 0:G1], w["b_rg"][0]), (bias_r1[:, G1:G1 + N1], w["b_re"][0])):
            act.dma_start(dst, src.partition_broadcast(P)).then_inc(row_in, 16)
        for dst, src in ((router[0][:, :, 0:G1], w["w_rg"][0]), (router[0][:, :, G1:], w["w_re"][0]),
                         (router[1], w["moe_w_router_2"][0])):
            act.dma_start(dst, src.rearrange("(k p) e -> p k e", p=P)).then_inc(router_in, 16)

        def copy(out_, s, view, scale=1.0):
            b = full(s)
            act.activation(out_, view(b), ACT.Copy, scale=scale).then_inc(bank_free[b], 1)

        as_blocks = lambda b: bank(b, 2, T)

        def walk(plan):
            for s in plan:
                kind, a, i = s
                if kind == "vec":
                    n = vec_rows[a]
                    copy((cols_a, cols_b)[a][:, 0:n], s, lambda b: psum[:, b, 0:n])
                    if a == 0:
                        evacuated(s)
                        act.activation(cond, cols_a[:, VEC_A["c"][0]:VEC_A["c"][0] + KT], ACT.Silu).then_inc(cond_set, 1)
                    else:
                        act.wait_ge(lam_summed, 1)
                        act.activation(lam_exp, lam_sum, ACT.Exp).then_inc(lam_exped, 1)
                elif kind == "turn_x":
                    copy(xT[:, 2 * a:2 * a + 2, :], s, as_blocks)
                elif kind == "turn_mem":
                    copy(memT[:, 2 * a:2 * a + 2, :], s, as_blocks)
                elif kind == "gemm" and a in ("da_v", "r_v", "m_v"):
                    if a == "r_v":
                        act.wait_ge(job_done, done[("turn_mem", 3, 0)])
                    dst = {"da_v": dav, "r_v": rv, "m_v": mv}[a]
                    copy(dst[:, i % 2, i // 2 * PANEL:(i // 2 + 1) * PANEL], s, bank)
                elif kind == "gemm" and a in ("da_q", "da_k", "m_q", "m_k", "r_q", "r_k"):
                    dst = {"da_q": daq, "da_k": dak, "m_q": mq, "m_k": mk, "r_q": rq, "r_k": rk}[a]
                    scale = {"da_q": (D // (2 * DA_H)) ** -0.5, "m_q": (D // MEM_H) ** -0.5}.get(a, 1.0)
                    copy(dst[:, 2 * i:2 * i + 2, :], s, as_blocks, scale)
                elif kind == "gemm" and a == "r_g":
                    b = full(s)
                    act.activation(rg[:, 2 * i:2 * i + 2, :], bank(b, 2, T), ACT.Silu).then_inc(bank_free[b], 1)
                elif kind == "gemm" and a.startswith("gate"):
                    n = int(a[-1])
                    if n:
                        evacuated(("gemm", f"branch{n - 1}", i))
                    b = full(s)
                    for k in range(2):
                        ins = act.activation(gate[:, 2 * i + k, :], bank(b, 2, T)[:, k, :], ACT.Sigmoid,
                                             bias=col_a("b_gate", n * KT + 2 * i + k))
                    ins.then_inc(bank_free[b], 1)
                elif kind == "da_score":
                    u = 2 * a + i
                    act.wait_ge(da_logits, u + 1)
                    if u:
                        act.wait_ge(da_probs, u)
                    for c in range(2):
                        ins = act.activation(e_prob[:, c, :], logit[:, c, :], ACT.Exp, bias=dmax[:, c:c + 1],
                                             accum_out=dsum[:, c:c + 1])
                    ins.then_inc(da_exped, 1)
                elif kind == "da_turn":
                    copy(a_turn, s, as_blocks)
                elif kind == "da_out":
                    b = full(s)
                    if a:
                        act.wait_ge(job_done, done[("da_norm", a - 1, 0)])
                    act.activation(osq, psum[:, b, 0:T], ACT.Square).then_inc(da_squared, 1)
                elif kind == "da_norm":
                    b = full(s)
                    if a:
                        evacuated(("da_out", a - 1, 0))
                    act.activation(rstd, psum[:, b, 0:T], ACT.Sqrt, bias=eps, scale=1.0 / P).then_inc(bank_free[b], 1)
                elif kind == "ret_out":
                    if a:
                        act.wait_ge(ret_y, a)
                    copy(ret_o, s, as_blocks)
                elif kind == "ret_mean":
                    act.wait_ge(ret_centred, a + 1)
                    act.activation(ret_sq, ret_o, ACT.Square).then_inc(ret_squared, 1)
                elif kind == "ret_var":
                    b = full(s)
                    act.activation(ret_stat, psum[:, b, 0:T], ACT.Sqrt, bias=eps, scale=1.0 / 256)\
                       .then_inc(bank_free[b], 1)
                    act.wait_ge(ret_normed, a + 1)
                    for k in range(2):
                        n = 2 * a + k
                        ins = act.activation(ret_o[:, k, :], ret_o[:, k, :], ACT.Identity, bias=col_a("gn_b", n),
                                             scale=col_a("gn_g", n))
                    ins.then_inc(ret_scaled, 1)
                elif kind == "mem_score":
                    b = full(s)
                    act.wait_ge(mem_max, a + 1)
                    if a:
                        act.wait_ge(mem_probs, a)
                    for c in range(TB):
                        ins = act.activation(e_prob[:, c, :], bank(b, 2, T)[:, c, :], ACT.Exp, bias=dmax[:, c:c + 1],
                                             accum_out=dsum[:, c:c + 1])
                    ins.then_inc(bank_free[b], 1)
                elif kind == "mem_turn":
                    copy(a_turn, s, as_blocks)
                elif kind == "mem_out":
                    copy(ymem[:, 2 * a:2 * a + 2, :], s, as_blocks)
                elif kind == "turn_tok":
                    copy(tok[:, i // 2, i % 2 * PANEL:(i % 2 + 1) * PANEL], s, bank)
                    if a == 0 and i == 3:
                        later_loads()
                elif kind == "logits":
                    for n in range(2 - a):
                        act.wait_ge(route_diff, 2 * a + n + 1)
                        t = ex_g if (a, n) == (0, 0) else ratio
                        act.activation(t, t, ACT.Exp).then_inc(route_exp, 1)
                elif kind == "gemm" and a == "ev_p":
                    copy(p_tok[:, i, :], s, bank)
                elif kind == "gemm" and a == "ev_q":
                    copy(q2[:, 2 * i:2 * i + 2, :], s, as_blocks, GQA_D ** -0.5)
                elif kind == "ev_k":
                    b = full(s)
                    for g in range(GQA_KV):
                        for half in range(2):
                            ins = act.activation(k2[64 * half:64 * half + 64, g, :], psum[64 * g:64 * g + 64, b, 0:T],
                                                 ACT.Copy)
                    ins.then_inc(bank_free[b], 1)
                elif kind == "ev_v":
                    copy(v2, s, lambda b: psum[:, b, 0:T].rearrange("p (t c) -> p t c", c=P))
                elif kind == "pool":
                    copy(pooled[:, 2 * a:2 * a + 2, :], s, as_blocks)
                elif kind == "pool_map":
                    b = full(s)
                    for k in range(2):
                        ins = act.activation(mix[:, 2 * a + k, :], bank(b, 2, T)[:, k, :], ACT.Identity,
                                             scale=col_a("pool_scale", 2 * a + k))
                    ins.then_inc(bank_free[b], 1)
                elif kind == "gqa_score":
                    act.wait_ge(gqa_logits, a + 1)
                    if a:
                        act.wait_ge(gqa_probs, a)
                    for t in range(TB):
                        act.activation(e2[:, t, :], logit2[:, t, :], ACT.Exp, bias=dmax[:, t:t + 1],
                                       accum_out=dsum[:, t:t + 1])
                    act.activation(esink, dmax, ACT.Exp, bias=sink[:, a:a + 1]).then_inc(gqa_exped, 1)
                elif kind == "gqa_turn":
                    copy(at2, s, as_blocks)
                elif kind == "gqa_out":
                    p0 = 64 * (a % 2)
                    copy(mix[p0:p0 + 64, 4 + a // 2, :], s, lambda b: psum[p0:p0 + 64, b, 0:T])
                elif kind == "turn_ws":
                    copy(ws_t[:, 4 * a:4 * a + 4, :], s, lambda b: bank(b, 4, P))
                elif kind == "gemm" and a in ("od_u", "od_v"):
                    b = full(s)
                    if a == "od_u":
                        act.activation(mix[:, 2 * i:2 * i + 2, :], bank(b, 2, T), ACT.Gelu_apprx_tanh)\
                           .then_inc(bank_free[b], 1)
                    else:
                        act.activation(v_tok[:, i % 2, i // 2 * PANEL:(i // 2 + 1) * PANEL], bank(b),
                                       ACT.Gelu_apprx_tanh).then_inc(bank_free[b], 1)
                        if i == 3:
                            act.wait_ge(v_normed, 1)
                            act.activation(bn_a[:, :, 1:2], bn_a[:, :, 1:2], ACT.Sqrt, bias=eps).then_inc(v_normed, 1)
                elif kind == "turn_out":
                    copy(out_tok[:, a // 2, a % 2 * PANEL:(a % 2 + 1) * PANEL], s, bank)
                elif kind == "ln_sum":
                    sq = ("ln_sq", a, 0)
                    gain_bias = ((lambda k: (col_a("ln1_g", k), col_a("ln1_b", k))),
                                 (lambda k: (col_a("ln2_g", k), col_a("ln2_b", k))),
                                 *((lambda k, n=n: (col_a("lng_2", 8 * n + k), col_b("lnb_2", 8 * n + k)))
                                   for n in range(4)))[a]
                    src, squares = (z, z_sq) if a == 0 else (acc, later_sq)
                    layer_norm_scalar(act, a, src, squares, done[sq], job_bank(sq), bank_free[job_bank(sq)], gain_bias, acc)
                    if 1 <= a <= 4:
                        layer, part = (a - 1) // 2, 3 * ((a - 1) % 2)
                        act.wait_ge(modp1_set, 1)
                        for k in range(KT):
                            act.wait_ge(ln_out, KT * a + k + 1)
                            act.activation(hT[:, k, :], acc[:, k, :], ACT.Identity, bias=mod_cols(mod, layer, part, k),
                                           scale=mod_cols(modp1, layer, part + 1, k)).then_inc(modulated, 1)

        def later_loads():
            act.wait_ge(da_probs, 2 * DA_H)
            act.wait_ge(ret_y, RET_H)
            act.wait_ge(job_done, done[("gemm", "w_o", 3)])
            act.dma_start(region(A_PHASE, C_PHASE), w["consts"][:, C_COMMON + C_PHASE:]).then_inc(small_in, 16)
            act.dma_start(w_pool, w["ev_pool_w_2"][0].rearrange("g c d -> c g d")).then_inc(small_in, 16)
            act.dma_start(w_s, w["od_w_s_2"][0].rearrange("g t s -> t g s")).then_inc(small_in, 16)
            for dst, src in ((sg_rows[:, 0, :], w["od_sg_ln_g_2"][0]), (sg_rows[:, 1, :], w["od_sg_ln_b_2"][0]),
                             (bs_rows.rearrange("p g t -> p (g t)"), w["od_b_s_2"][0].rearrange("g t -> (g t)"))):
                act.dma_start(dst, src.partition_broadcast(P)).then_inc(small_in, 16)

        def expert(m, x, e):
            jobs, h0 = x * m["jobs"] + m["at"], x * (4 * m["pairs"]) + m["h"]

            def body(width):
                for i in range(4):
                    act.wait_ge(job_done, jobs + (i + 1))
                    act.activation(xe[:, 2 * i:2 * i + 2, 0:width], bank(i, 2, T)[:, :, 0:width],
                                   ACT.Copy).then_inc(xe_set, 1)
                for t in range(m["pairs"]):
                    if t == 0:
                        act.wait_ge(h_set, h0)
                    for j in range(4):
                        act.wait_ge(job_done, jobs + (5 + 5 * t + j + 1))
                        if t:
                            act.wait_ge(h_set, h0 + (4 * t + j - 3))
                        act.activation(s_tile[:, j, 0:width], psum[:, 4 + j, 0:width], ACT.Silu).then_inc(silu_set, 1)
                for i in range(4):
                    if i == 0:
                        act.wait_ge(job_done, jobs + (5 + 5 * m["pairs"]))
                    act.activation(ye[:, 2 * i:2 * i + 2, 0:width], bank(i, 2, T)[:, :, 0:width],
                                   ACT.Copy).then_inc(ye_copied, 1)

            return body

        def mixture(m, n, rank_step):
            evacuated(rank_step)
            if m["n"] == N1:
                with act.Fori(0, N1 // 2) as it:
                    for e in range(2):
                        x = it * 2 + e
                        count = act.value_load(counts_i[0:1, bass.ds(x, 1)], min_val=0, max_val=T)
                        by_width(act, count, TIERS[n], expert(m, x, e))
            else:
                with act.Fori(0, m["n"]) as x:
                    count = act.value_load(counts_i[0:1, bass.ds(x, 1)], min_val=0, max_val=T)
                    by_width(act, count, TIERS[n], expert(m, x, 0))

        walk(plans[0])
        mixture(mixtures[0], 0, ("rank", 0, 0))
        walk(plans[1])
        jobs, q = FF0, HF
        for n, (_, width) in enumerate(FFN_P):
            for j in range(width // P):
                act.wait_ge(job_done, jobs + j + 1)
                act.wait_ge(h_set, q - 4 + j + 1 if n else HF)
                act.activation(s_tile[:, j, :], psum[:, 4 + j, 0:T], ACT.Silu).then_inc(silu_set, 1)
            jobs, q = jobs + width // P + 1, q + width // P
        walk(plans[2])
        mixture(mixtures[1], 1, ("rank", 1, 0))
        walk(plans[3])

    @block.vector
    def _(dve):
        step = [0]

        def settle(ins):
            step[0] += 1
            ins.then_inc(dve_step, 1)
            dve.wait_ge(dve_step, step[0])

        def full(s):
            dve.wait_ge(job_done, done[s])
            return job_bank(s)

        def evacuated(s):
            dve.wait_ge(*bank_through(s))

        dve.wait_ge(row_in, 4 * 16)
        lam4 = lam_rows.rearrange("p (a b) -> p a b", b=64)
        settle(dve.tensor_tensor(lam_prod, lam4[:, 0:4:2, :], lam4[:, 1:4:2, :], ALU.mult))
        dve.tensor_reduce(lam_sum, lam_prod, AX.X, ALU.add).then_inc(lam_summed, 1)
        dve.wait_ge(lam_exped, 1)
        settle(dve.tensor_tensor(neg_lam, lam_exp[:, 1:2], lam_exp[:, 0:1], ALU.subtract))
        settle(dve.tensor_scalar(neg_lam, neg_lam, -LAMBDA_INIT, None, ALU.add))
        evacuated(("vec", 0, 0))
        settle(dve.tensor_scalar(da_gain, col_a("da_g"), 1.0 - LAMBDA_INIT, None, ALU.mult))
        dve.wait_ge(const_in, 16)
        dve.wait_ge(phase_in, 16)
        def sum_modulation(n):
            layer, p = n // 12, n % 12
            at, fill = panel[("ada", layer, p)]
            dve.wait_ge(slot_full[at], 16 * fill)
            if n >= 2:
                dve.wait_ge(job_done, done[("ada", (n - 2) // 12, (n - 2) % 12)])
            tile, wt = ada_sum[:, n % 2, :], slot(at, KT)
            settle(dve.tensor_scalar(tile, wt[:, 0, :], cond[:, 0:1], None, ALU.mult))
            for k in range(1, KT):
                ins = dve.scalar_tensor_tensor(tile, wt[:, k, :], cond[:, k:k + 1], tile, ALU.mult, ALU.add)
                if k < KT - 1:
                    settle(ins)
            ins.then_inc(ada_summed, 1)

        def add_modulation_bias(s):
            b = full(s)
            at = s[1] * 48 + s[2] * 4
            c = VEC_B["ada_b"][0] + at
            dve.tensor_tensor(mod[:, at:at + 4], psum[:, b, 0:4], cols_b[:, c:c + 4], ALU.add)\
               .then_inc(bank_free[b], 1)

        def settled_max_one_hot(values, out_, n, m):
            settle(dve.tensor_reduce(m, values, AX.X, ALU.max))
            settle(dve.tensor_tensor(top_e[:, :, 0:n], values, along(m, n), ALU.is_equal))
            settle(dve.tensor_tensor(top_e[:, :, 0:n], top_e[:, :, 0:n], over(desc[:, 0:n], TB), ALU.mult))
            settle(dve.tensor_reduce(peak, top_e[:, :, 0:n], AX.X, ALU.max))
            settle(dve.tensor_tensor(out_, top_e[:, :, 0:n], along(peak, n), ALU.is_equal))

        def top_two(values, n, told):
            settled_max_one_hot(values, top_1[:, :, 0:n], n, peak_1)
            settle(dve.scalar_tensor_tensor(top_v[:, :, 0:n], top_1[:, :, 0:n], -1e38, values, ALU.mult, ALU.add))
            settled_max_one_hot(top_v[:, :, 0:n], top_2[:, :, 0:n], n, peak_2)
            dve.tensor_tensor(ratio, peak_2, peak_1, ALU.subtract).then_inc(route_diff, 1)
            dve.wait_ge(route_exp, told)
            settle(dve.tensor_scalar(wt_2, ratio, 1.0, None, ALU.add))
            settle(dve.reciprocal(wt_1, wt_2))
            settle(dve.tensor_tensor(wt_2, wt_1, ratio, ALU.mult))

        def routing(m, b, s):
            n = (N1, N2)[m]
            settle(dve.memset(table, 0.0))
            settle(dve.tensor_scalar(desc, iota[:, 0:N1], -1.0, float(N1), ALU.mult, ALU.add))
            logits = psum[:, b, 0:TB * (G1 + N1 if m == 0 else N2)].rearrange("p (t e) -> p t e", t=TB)
            if m == 0:
                dve.tensor_tensor(lg, logits, over(bias_r1, TB), ALU.add).then_inc(bank_free[b], 1)
                evacuated(s)
                group, each = lg[:, :, 0:G1], lg[:, :, G1:].rearrange("p t (g e) -> p t g e", e=E1)
                settled_max_one_hot(group, hot_g, G1, peak_1)
                dve.tensor_tensor(ex_g, group, along(peak_1, G1), ALU.subtract).then_inc(route_diff, 1)
                dve.wait_ge(route_exp, 1)
                settle(dve.tensor_reduce(p_top, ex_g, AX.X, ALU.add))
                settle(dve.reciprocal(p_top, p_top))
                hot4 = hot_g.unsqueeze(3).to_broadcast([P, TB, G1, E1])
                four = lambda v: v.rearrange("p t (g e) -> p t g e", e=E1)
                for t in range(TB):
                    settle(dve.tensor_tensor(four(top_v)[:, t], each[:, t], hot4[:, t], ALU.mult))
                    settle(dve.tensor_reduce(sel[:, t, 0:E1], top_v[:, t, :].rearrange("p (g e) -> p e g", e=E1),
                                             AX.X, ALU.add))
                top_two(sel[:, :, 0:E1], E1, 2)
                settle(dve.tensor_tensor(wt_1, wt_1, p_top, ALU.mult))
                settle(dve.tensor_tensor(wt_2, wt_2, p_top, ALU.mult))
            else:
                dve.tensor_copy(lg[:, :, 0:n], logits).then_inc(bank_free[b], 1)
                evacuated(s)
                top_two(lg[:, :, 0:n], n, 3)
            k = E1 if m == 0 else n
            one, two = top_1[:, :, 0:k], top_2[:, :, 0:k]
            w_k, m_k = sel[:, :, 0:k], top_v[:, :, 0:k]
            settle(dve.tensor_tensor(m_k, one, two, ALU.add))
            settle(dve.tensor_tensor(one, one, along(wt_1, k), ALU.mult))
            settle(dve.tensor_tensor(two, two, along(wt_2, k), ALU.mult))
            settle(dve.tensor_tensor(w_k, one, two, ALU.add))
            for t in range(TB):
                for row, v in ((4 + t, w_k), (2 + t, m_k)):
                    if m == 0:
                        dst = table[:, row, 0:n].rearrange("p (g e) -> p g e", e=E1)
                        ins = dve.tensor_tensor(dst, along(hot_g[:, t, :], E1), over(v[:, t, :], G1), ALU.mult)
                    else:
                        ins = dve.tensor_copy(table[:, row, 0:n], v[:, t, :])
                    if (t, row) != (TB - 1, 2 + t):
                        settle(ins)
            ins.then_inc(masks_set, 1)

        def add_to_result(i, gain, settled):
            if gain is None:
                dve.tensor_tensor(acc[:, 2 * i:2 * i + 2, :], bank(i, 2, T), acc[:, 2 * i:2 * i + 2, :],
                                  ALU.add).then_inc(settled, 1)
                return
            for k in range(2):
                ins = dve.scalar_tensor_tensor(acc[:, 2 * i + k, :], bank(i, 2, T)[:, k, :],
                                               mod_cols(modp1, *gain, 2 * i + k), acc[:, 2 * i + k, :],
                                               ALU.mult, ALU.add)
            ins.then_inc(settled, 1)

        owed = []

        def walk(plan):
            for s in plan:
                kind, a, i = s
                if owed and index[s] >= index[owed[0]] + 2:
                    add_modulation_bias(owed.pop())
                if kind == "da_score":
                    u = 2 * a + i
                    b = full(s)
                    if u:
                        dve.wait_ge(da_exped, u)
                    dve.scalar_tensor_tensor(logit, causal, 2.0 ** -(a + 1), bank(b, 2, T), ALU.mult,
                                             ALU.add).then_inc(bank_free[b], 1)
                    evacuated(s)
                    dve.tensor_reduce(dmax, logit, AX.X, ALU.max, negate=True).then_inc(da_logits, 1)
                    dve.wait_ge(da_exped, u + 1)
                    settle(dve.reciprocal(drec, dsum))
                    if i == 0:
                        if a:
                            dve.wait_ge(job_done, done[("da_turn", a - 1, 0)])
                        dve.tensor_tensor(a_prob, e_prob, along(drec, T), ALU.mult).then_inc(da_probs, 1)
                    else:
                        settle(dve.tensor_scalar(drec, drec, neg_lam, None, ALU.mult))
                        settle(dve.tensor_tensor(e_prob, e_prob, along(drec, T), ALU.mult))
                        dve.wait_ge(da_probs, u)
                        dve.tensor_tensor(a_prob, a_prob, e_prob, ALU.add).then_inc(da_probs, 1)
                elif kind == "da_norm":
                    evacuated(s)
                    settle(dve.reciprocal(rstd, rstd))
                    bo = job_bank(("da_out", a, 0))
                    dve.scalar_tensor_tensor(yda[:, a, :], psum[:, bo, 0:T], da_gain, rstd, ALU.mult,
                                             ALU.mult).then_inc(bank_free[bo], 1)
                elif kind == "ret_score":
                    b = full(s)
                    if a:
                        dve.wait_ge(job_done, done[("ret_out", a - 1, 0)])
                    dve.tensor_tensor(ret_s, bank(b, 2, T), decay[:, 2 * a:2 * a + 2, :], ALU.mult).then_inc(bank_free[b], 1)
                elif kind == "ret_mean":
                    b = full(s)
                    dve.tensor_scalar(ret_stat, psum[:, b, 0:T], 1.0 / 256, None, ALU.mult).then_inc(bank_free[b], 1)
                    evacuated(s)
                    evacuated(("ret_out", a, 0))
                    dve.tensor_tensor(ret_o, ret_o, over(ret_stat, 2), ALU.subtract).then_inc(ret_centred, 1)
                elif kind == "ret_var":
                    evacuated(s)
                    settle(dve.reciprocal(ret_stat, ret_stat))
                    dve.tensor_tensor(ret_o, ret_o, over(ret_stat, 2), ALU.mult).then_inc(ret_normed, 1)
                    dve.wait_ge(ret_scaled, a + 1)
                    for k in range(1):
                        evacuated(("gemm", "r_g", a))
                        dve.tensor_tensor(yret[:, 2 * a:2 * a + 2, :], ret_o, rg[:, 2 * a:2 * a + 2, :],
                                          ALU.mult).then_inc(ret_y, 1)
                elif kind == "mem_score":
                    b = full(s)
                    dve.tensor_reduce(dmax, bank(b, 2, T), AX.X, ALU.max, negate=True).then_inc(mem_max, 1)
                    evacuated(s)
                    settle(dve.reciprocal(drec, dsum))
                    if a:
                        dve.wait_ge(job_done, done[("mem_turn", a - 1, 0)])
                    dve.tensor_tensor(a_prob, e_prob, along(drec, T), ALU.mult).then_inc(mem_probs, 1)
                elif kind == "gemm" and a.startswith("branch"):
                    n = int(a[-1])
                    b = full(s)
                    evacuated(("gemm", f"gate{n}", i))
                    mg = merged[:, 2 * i:2 * i + 2, :]
                    gt = gate[:, 2 * i:2 * i + 2, :]
                    if n == 0:
                        dve.tensor_tensor(mg, gt, bank(b, 2, T), ALU.mult).then_inc(bank_free[b], 1)
                    else:
                        dve.tensor_tensor(gtmp, gt, bank(b, 2, T), ALU.mult).then_inc(bank_free[b], 1)
                        evacuated(s)
                        evacuated(("gemm", f"branch{n - 1}", i))
                        settle(dve.tensor_tensor(mg, mg, gtmp, ALU.add))
                        if n == 2 and i == 3:
                            dve.sem_inc(merged_set, 1)
                elif kind == "gemm" and a == "w_o":
                    b = full(s)
                    dve.scalar_tensor_tensor(z[:, 2 * i:2 * i + 2, :], xT[:, 2 * i:2 * i + 2, :], ALPHA1, bank(b, 2, T),
                                             ALU.mult, ALU.add).then_inc(bank_free[b], 1)
                elif kind == "ada":
                    owed.append(s)
                    n = 12 * a + i + 1
                    if n < 24:
                        sum_modulation(n)
                    else:
                        add_modulation_bias(owed.pop())
                        evacuated(s)
                        evacuated(("ada", 1, 10))
                        dve.tensor_scalar(modp1, mod, 1.0, None, ALU.add).then_inc(modp1_set, 1)
                elif kind == "gemm" and a in ("ev_o", "od_o"):
                    b = full(s)
                    dve.wait_ge(acc_scaled, 2 if a == "ev_o" else 4)
                    for k in range(2):
                        n = 2 * i + k
                        ins = dve.scalar_tensor_tensor(acc[:, n, :], bank(b, 2, T)[:, k, :],
                                                       mod_cols(modp1, 0 if a == "ev_o" else 1, 2, n), acc[:, n, :],
                                                       ALU.mult, ALU.add)
                    ins.then_inc(bank_free[b], 1)
                elif kind == "gqa_score":
                    b = full(s)
                    if a == 0:
                        dve.wait_ge(small_in, 6 * 16)
                    if a:
                        dve.wait_ge(gqa_exped, a)
                    dve.scalar_tensor_tensor(logit2, wbias, 2.0 ** -(a + 1), bank(b, 2, T), ALU.mult,
                                             ALU.add).then_inc(bank_free[b], 1)
                    evacuated(s)
                    settle(dve.tensor_reduce(dmax, logit2, AX.X, ALU.max))
                    dve.tensor_scalar(dmax, dmax, sink[:, a:a + 1], -1.0, ALU.max, ALU.mult).then_inc(gqa_logits, 1)
                    dve.wait_ge(gqa_exped, a + 1)
                    settle(dve.tensor_tensor(dsum, dsum, esink, ALU.add))
                    settle(dve.reciprocal(drec, dsum))
                    if a:
                        dve.wait_ge(job_done, done[("gqa_turn", a - 1, 0)])
                    dve.tensor_tensor(a2, e2, along(drec, T), ALU.mult).then_inc(gqa_probs, 1)
                elif s == ("gemm", "od_v", 3):
                    for n in range(4):
                        evacuated(("gemm", "od_v", n))
                    for t in range(TB):
                        for c in range(2):
                            settle(dve.bn_stats(bn_s[:, t, 6 * c:6 * c + 6], v_tok[:, t, c * 512:(c + 1) * 512]))
                        ins = dve.bn_aggr(bn_a[:, t, :], bn_s[:, t, 0:12])
                        if t == 0:
                            settle(ins)
                    ins.then_inc(v_normed, 1)
                    dve.wait_ge(v_normed, 2)
                    settle(dve.reciprocal(bn_a[:, :, 1:2], bn_a[:, :, 1:2]))
                    for t in range(TB):
                        settle(dve.tensor_scalar(v_tok[:, t, :], v_tok[:, t, :], bn_a[:, t, 0:1], bn_a[:, t, 1:2],
                                                 ALU.subtract, ALU.mult))
                    settle(dve.tensor_tensor(v_tok, v_tok, over(sg_rows[:, 0, :], TB), ALU.mult))
                    dve.tensor_tensor(v_tok, v_tok, over(sg_rows[:, 1, :], TB), ALU.add).then_inc(v_normed, 1)
                elif kind == "gate_s":
                    b = full(s)
                    evacuated(("gemm", "od_u", a))
                    for k in range(2):
                        ins = dve.tensor_tensor(e2[:, k, :].rearrange("p (c t) -> p c t", t=P), bank(b, 4, P)[:, 2 * k:2 * k + 2, :],
                                                over(bs_rows[:, 2 * a + k, :], 2), ALU.add)
                    ins.then_inc(bank_free[b], 1)
                    evacuated(s)
                    dve.tensor_tensor(mix[:, 2 * a:2 * a + 2, :], mix[:, 2 * a:2 * a + 2, :], e2,
                                      ALU.mult).then_inc(sg_gated, 1)
                    dve.wait_ge(sg_gated, a + 1)
                elif kind == "logits":
                    routing(a, full(s), s)
                elif kind == "turn_tok" and i == 3:
                    if a == 0:
                        dve.wait_ge(job_done, done[s])
                        dve.tensor_scalar(acc, acc, ALPHA1, None, ALU.mult).then_inc(acc_scaled, 1)
                elif kind == "rank":
                    b = full(s)
                    n = (N1, N2)[a]
                    settle(dve.tensor_copy(table[:, 0:2, 0:n], psum[:, b, 0:2 * n].rearrange("p (t e) -> p t e", e=n)))
                    dve.tensor_copy(counts_i[:, 0:n], psum[:, b, 2 * n:3 * n]).then_inc(bank_free[b], 1)
                elif kind == "ln_sum":
                    if a == 0:
                        for k in range(4):
                            evacuated(("gemm", "w_o", k))
                    src = z if a == 0 else acc
                    layer_norm_vector(dve, settle, a, src, done[s], job_bank(s), bank_through(s),
                                      bank_through(("ln_sq", a, 0)))
                    if 1 <= a <= 4:
                        dve.wait_ge(modulated, KT * a)
                        dve.tensor_scalar(acc, acc, ALPHA2, None, ALU.mult).then_inc(acc_scaled, 1)
                        dve.wait_ge(acc_scaled, a + 1)

        def own_tokens(m, x):
            dve.tensor_copy(mine.unsqueeze(2), table[:, :, bass.ds(x, 1)]).then_inc(mine_set, 1)
            dve.wait_ge(mine_set, x + (m["perm"] + 1))
            for t in range(TB):
                rank, is_in, weight = mine[:, t:t + 1], mine[:, 2 + t:3 + t], mine[:, 4 + t:5 + t]
                dve.tensor_scalar(perm[:, t, :], iota, rank, is_in, ALU.is_equal, ALU.mult)
                ins = dve.tensor_scalar(perm_w[:, t, :], iota, rank, weight, ALU.is_equal, ALU.mult)
            ins.then_inc(perm_set, 1)

        def expert(m, x):
            jobs, h0 = x * m["jobs"] + m["at"], x * (4 * m["pairs"]) + m["h"]

            def body(width):
                dve.wait_ge(job_done, jobs + 5)
                w0 = min(width, P)
                dve.tensor_copy(spread[0:w0, 0:len(chunks(width)), :], bank(4, 2, T)[0:w0, 0:len(chunks(width)), :])\
                   .then_inc(spread_set, 1)
                for t in range(m["pairs"]):
                    for j in range(4):
                        dve.wait_ge(silu_set, h0 + (4 * t + j + 1))
                        dve.tensor_tensor(h_tile[t % 2][:, j, 0:width], s_tile[:, j, 0:width],
                                          psum[:, 4 + j, T:T + width], ALU.mult).then_inc(h_set, 1)
                    if t == 0:
                        dve.wait_ge(perm_set, x + (m["perm"] + 1))
                        own_tokens(m, x + 1)
                for half in range(2):
                    dve.wait_ge(job_done, jobs + (5 + 5 * m["pairs"] + half + 1))
                    for c, n in chunks(width):
                        ins = dve.tensor_copy(ye_tok[0:n, c, half * 512:half * 512 + 512],
                                              psum[0:n, 4 + 2 * c + half, :])
                    ins.then_inc(ye_turned, 1)
                for i in range(4):
                    dve.wait_ge(job_done, jobs + (5 + 5 * m["pairs"] + 2 + i + 1))
                    if i == 0:
                        dve.wait_ge(added, x * 4 + m["add"])
                    add_to_result(i, m["gain"], added)

            return body

        def mixture(m, n, rank_step):
            evacuated(rank_step)
            own_tokens(m, 0)
            if m["n"] == N1:
                with dve.Fori(0, N1 // 2) as it:
                    for e in range(2):
                        x = it * 2 + e
                        count = dve.value_load(counts_i[0:1, bass.ds(x, 1)], min_val=0, max_val=T)
                        by_width(dve, count, TIERS[n], expert(m, x))
            else:
                with dve.Fori(0, m["n"]) as x:
                    count = dve.value_load(counts_i[0:1, bass.ds(x, 1)], min_val=0, max_val=T)
                    by_width(dve, count, TIERS[n], expert(m, x))

        dve.wait_ge(cond_set, 1)
        sum_modulation(0)
        walk(plans[0])
        dve.wait_ge(acc_scaled, 1)
        mixture(mixtures[0], 0, ("rank", 0, 0))
        dve.wait_ge(added, Y1 + 4 * N1)
        walk(plans[1])
        q = HF
        for n, (_, width) in enumerate(FFN_P):
            for j in range(width // P):
                dve.wait_ge(silu_set, q + j + 1)
                dve.tensor_tensor(h_tile[n % 2][:, j, :], s_tile[:, j, :], psum[:, 4 + j, T:2 * T],
                                  ALU.mult).then_inc(h_set, 1)
            q += width // P
        dve.wait_ge(job_done, FF0 + FFN_JOBS)
        for i in range(4):
            add_to_result(i, (0, 5), added)
        dve.wait_ge(added, Y2)
        walk(plans[2])
        mixture(mixtures[1], 1, ("rank", 1, 0))
        dve.wait_ge(added, Y2 + 4 * N2)
        walk(plans[3])

    @block.tensor
    def _(pe):
        def open_bank(s):
            n = index[s]
            if n >= BANKS:
                pe.wait_ge(bank_free[n % BANKS], n // BANKS)
            return n % BANKS

        def evacuated(s):
            pe.wait_ge(*bank_through(s))

        def turn4(s, pairs):
            b = open_bank(s)
            for n, (src, col) in enumerate(pairs):
                ins = pe.transpose(psum[0:src.shape[1], b, col:col + src.shape[0]], src,
                                   ident[0:src.shape[0], 0:src.shape[0]])
            ins.then_inc(job_done, 1)

        rhs_of = {"m_k": memT, "m_v": memT, "branch0": yda, "branch1": yret, "branch2": ymem, "w_o": merged,
                  "ev_p": hT, "ev_q": hT, "ev_o": mix, "od_u": hT, "od_v": hT, "od_o": mix}
        pe.wait_ge(const_in, 16)
        pe.wait_ge(ones_set, 2)
        def walk(plan):
            for s in plan:
                kind, a, i = s
                if kind == "vec":
                    pe.wait_ge(vec_in, 16 * 13)
                    rows = (vec_a, vec_b)[a]
                    n = vec_rows[a]
                    b = open_bank(s)
                    pe.transpose(psum[:, b, 0:n], rows[0:n, :], ident[0:n, 0:n]).then_inc(job_done, 1)
                elif kind in ("turn_x", "turn_mem"):
                    pe.wait_ge(*((x_in, 16) if kind == "turn_x" else (mem_in, 16)))
                    src = x_tok if kind == "turn_x" else mem_tok
                    turn4(s, [(src[:, t, (2 * a + k) * P:(2 * a + k + 1) * P], k * T + t * P)
                              for k in range(2) for t in range(TB)])
                elif kind == "gemm":
                    at, fills = panel_of(s)
                    if i == 0:
                        if a == "da_q":
                            for n in range(4):
                                evacuated(("turn_x", n, 0))
                        elif a == "m_k":
                            for n in range(4):
                                evacuated(("turn_mem", n, 0))
                        elif a == "branch0":
                            evacuated(("da_out", DA_H - 1, 0))
                            for n in range(DA_H):
                                evacuated(("da_out", n, 0))
                        elif a == "branch1":
                            pe.wait_ge(ret_y, RET_H)
                        elif a == "branch2":
                            for n in range(MEM_H):
                                evacuated(("mem_out", n, 0))
                        elif a == "w_o":
                            pe.wait_ge(merged_set, 1)
                        elif a == "ev_p":
                            pe.wait_ge(modulated, KT)
                        elif a == "ev_o":
                            evacuated(("pool_map", 0, 0))
                            evacuated(("pool_map", 1, 0))
                            for n in range(GQA_H):
                                evacuated(("gqa_out", n, 0))
                        elif a == "od_v":
                            pe.wait_ge(modulated, 3 * KT)
                        elif a == "od_o":
                            pe.wait_ge(sg_gated, 4)
                    pe.wait_ge(slot_full[at], 16 * fills)
                    rhs = rhs_of.get(a, xT)
                    b = open_bank(s)
                    wt = slot(at, KT)
                    if a in token_major:
                        for k in range(KT):
                            ins = pe.matmul(bank(b), rhs[:, k, i % 2 * P:(i % 2 + 1) * P], wt[:, k, :],
                                            start=(k == 0), stop=(k == KT - 1))
                    else:
                        for m in range(2):
                            c = (i % 2 * 2 + m) * P
                            for k in range(KT):
                                ins = pe.matmul(bank(b, 2, T)[:, m, :], wt[:, k, c:c + P], rhs[:, k, :],
                                                start=(k == 0), stop=(k == KT - 1))
                    ins.then_inc(job_done, 1)
                elif kind == "da_score":
                    b = open_bank(s)
                    if a % 2 == 0 and i == 0:
                        evacuated(("gemm", "da_q", a // 2))
                        evacuated(("gemm", "da_k", a // 2))
                    for t in range(TB):
                        ins = pe.matmul(bank(b, 2, T)[:, t, :], daq[64 * i:64 * i + 64, a, t * P:(t + 1) * P],
                                        dak[64 * i:64 * i + 64, a, :], start=True, stop=True)
                    ins.then_inc(job_done, 1)
                elif kind == "da_turn":
                    pe.wait_ge(da_probs, 2 * a + 2)
                    turn4(s, [(a_prob[:, t, k * P:(k + 1) * P], k * T + t * P) for k in range(2) for t in range(TB)])
                elif kind == "da_out":
                    evacuated(("da_turn", a, 0))
                    if a == 0:
                        for n in range(4):
                            evacuated(("gemm", "da_v", n))
                    b = open_bank(s)
                    for k in range(TB):
                        ins = pe.matmul(psum[:, b, 0:T], dav[:, k, a * P:(a + 1) * P], a_turn[:, k, :], start=(k == 0),
                                        stop=(k == TB - 1))
                    ins.then_inc(job_done, 1)
                elif kind == "da_norm":
                    pe.wait_ge(da_squared, a + 1)
                    b = open_bank(s)
                    pe.matmul(psum[:, b, 0:T], ones, osq, start=True, stop=True).then_inc(job_done, 1)
                elif kind == "ret_score":
                    if a == 0:
                        for n, k in (("r_q", 2), ("r_k", 2), ("r_v", 4)):
                            for m in range(k):
                                evacuated(("gemm", n, m))
                    b = open_bank(s)
                    for k in range(TB):
                        ins = pe.matmul(bank(b, 2, T)[:, k, :], rk[:, a, k * P:(k + 1) * P], rq[:, a, :], start=True,
                                        stop=True)
                    ins.then_inc(job_done, 1)
                elif kind == "ret_out":
                    evacuated(("ret_score", a, 0))
                    b = open_bank(s)
                    for m in range(2):
                        for k in range(TB):
                            c = (2 * a + m) * P
                            ins = pe.matmul(bank(b, 2, T)[:, m, :], rv[:, k, c:c + P], ret_s[:, k, :], start=(k == 0),
                                            stop=(k == TB - 1))
                    ins.then_inc(job_done, 1)
                elif kind in ("ret_mean", "ret_var"):
                    if kind == "ret_mean":
                        evacuated(("ret_out", a, 0))
                    else:
                        pe.wait_ge(ret_squared, a + 1)
                    src = ret_o if kind == "ret_mean" else ret_sq
                    b = open_bank(s)
                    for k in range(2):
                        ins = pe.matmul(psum[:, b, 0:T], ones, src[:, k, :], start=(k == 0), stop=(k == 1))
                    ins.then_inc(job_done, 1)
                elif kind == "mem_score":
                    if a == 0:
                        for n in ("m_q", "m_k"):
                            for m in range(4):
                                evacuated(("gemm", n, m))
                    b = open_bank(s)
                    for t in range(TB):
                        for k in range(2):
                            ins = pe.matmul(bank(b, 2, T)[:, t, :], mq[:, 2 * a + k, t * P:(t + 1) * P],
                                            mk[:, 2 * a + k, :], start=(k == 0), stop=(k == 1))
                    ins.then_inc(job_done, 1)
                elif kind == "mem_turn":
                    pe.wait_ge(mem_probs, a + 1)
                    turn4(s, [(a_prob[:, t, k * P:(k + 1) * P], k * T + t * P) for k in range(2) for t in range(TB)])
                elif kind == "mem_out":
                    evacuated(("mem_turn", a, 0))
                    if a == 0:
                        for n in range(4):
                            evacuated(("gemm", "m_v", n))
                    b = open_bank(s)
                    for m in range(2):
                        for k in range(TB):
                            c = (2 * a + m) * P
                            ins = pe.matmul(bank(b, 2, T)[:, m, :], mv[:, k, c:c + P], a_turn[:, k, :], start=(k == 0),
                                            stop=(k == TB - 1))
                    ins.then_inc(job_done, 1)
                elif kind in ("ln_sum", "ln_sq"):
                    if kind == "ln_sum" and a == 0:
                        for n in range(4):
                            evacuated(("gemm", "w_o", n))
                    elif kind == "ln_sum" and a in (2, 4):
                        for n in range(4):
                            evacuated(("gemm", "ev_o" if a == 2 else "od_o", n))
                    b = open_bank(s)
                    src = (z if a == 0 else acc) if kind == "ln_sum" else (z_sq if a == 0 else later_sq)
                    for k in range(KT):
                        if kind == "ln_sq" and k % 4 == 0:
                            pe.wait_ge(ln_squared, 2 * a + k // 4 + 1)
                        ins = pe.matmul(psum[:, b, 0:T], ones, src[:, k, :], start=(k == 0), stop=(k == KT - 1))
                    ins.then_inc(job_done, 1)
                elif kind == "ada":
                    pe.wait_ge(ada_summed, 12 * a + i + 1)
                    b = open_bank(s)
                    for m in range(4):
                        ins = pe.matmul(psum[:, b, m:m + 1], ada_sum[:, (12 * a + i) % 2, m * P:(m + 1) * P],
                                        ones[:, 0:1], start=True, stop=True)
                    ins.then_inc(job_done, 1)
                elif kind == "logits":
                    if a == 0:
                        pe.wait_ge(router_in, 3 * 16)
                        pe.wait_ge(ln_out, KT)
                    else:
                        pe.wait_ge(modulated, 4 * KT)
                    b = open_bank(s)
                    n = router[a].shape[2]
                    for t in range(TB):
                        for k in range(KT):
                            ins = pe.matmul(psum[:, b, t * n:(t + 1) * n], (acc, hT)[a][:, k, t * P:(t + 1) * P],
                                            router[a][:, k, :], start=(k == 0), stop=(k == KT - 1))
                    ins.then_inc(job_done, 1)
                elif kind == "turn_tok":
                    src, t, k0 = (acc, hT)[a], i // 2, i % 2 * 4
                    turn4(s, [(src[:, k0 + k, t * P:(t + 1) * P], k * P) for k in range(4)])
                elif kind == "turn_out":
                    if a == 0:
                        pe.wait_ge(ln_out, 6 * KT)
                    t, k0 = a // 2, a % 2 * 4
                    turn4(s, [(acc[:, k0 + k, t * P:(t + 1) * P], k * P) for k in range(4)])
                elif kind == "rank":
                    pe.wait_ge(masks_set, a + 1)
                    b = open_bank(s)
                    n = (N1, N2)[a]
                    mask = [table[:, 2 + t, 0:n] for t in range(TB)]
                    for c, terms in enumerate((((ustrict, 0),), ((ustrict, 1), (ones, 0)), ((ones, 0), (ones, 1)))):
                        for k, (lhs, t) in enumerate(terms):
                            ins = pe.matmul(psum[:, b, c * n:(c + 1) * n], lhs, mask[t], start=(k == 0),
                                            stop=(k == len(terms) - 1))
                    ins.then_inc(job_done, 1)
                elif kind in ("ev_k", "ev_v"):
                    at, fill = panel[("ev_k", 0, 0)]
                    pe.wait_ge(slot_full[at], 16 * fill)
                    wt = ring[:, at * SLOT:at * SLOT + KT * 256].rearrange("p (k n) -> p k n", k=KT)
                    b = open_bank(s)
                    if kind == "ev_k":
                        for k in range(KT):
                            ins = pe.matmul(psum[:, b, 0:T], wt[:, k, 0:P], hT[:, k, :], start=(k == 0),
                                            stop=(k == KT - 1))
                    else:
                        for t in range(TB):
                            for k in range(KT):
                                ins = pe.matmul(psum[:, b, t * P:(t + 1) * P], hT[:, k, t * P:(t + 1) * P],
                                                wt[:, k, P:2 * P], start=(k == 0), stop=(k == KT - 1))
                    ins.then_inc(job_done, 1)
                elif kind in ("pool", "pool_map"):
                    if kind == "pool":
                        pe.wait_ge(small_in, 6 * 16)
                        evacuated(("gemm", "ev_p", 0))
                        evacuated(("gemm", "ev_p", 1))
                    else:
                        evacuated(("pool", a, 0))
                    b = open_bank(s)
                    for m in range(2):
                        g = 2 * a + m
                        if kind == "pool":
                            for t in range(TB):
                                ins = pe.matmul(bank(b, 2, T)[:, m, :], p_tok[:, t, g * P:(g + 1) * P],
                                                pool_m[:, 2 * g + t, :], start=(t == 0), stop=(t == 1))
                        else:
                            ins = pe.matmul(bank(b, 2, T)[:, m, :], w_pool[:, g, :], pooled[:, g, :], start=True,
                                            stop=True)
                    ins.then_inc(job_done, 1)
                elif kind == "gqa_score":
                    if a == 0:
                        for n in (("gemm", "ev_q", 0), ("gemm", "ev_q", 1), ("ev_k", 0, 0)):
                            evacuated(n)
                    b = open_bank(s)
                    p0 = 64 * (a % 2)
                    for t in range(TB):
                        ins = pe.matmul(bank(b, 2, T)[:, t, :], q2[p0:p0 + 64, a // 2, t * P:(t + 1) * P],
                                        k2[p0:p0 + 64, a // 4, :], start=True, stop=True)
                    ins.then_inc(job_done, 1)
                elif kind == "gqa_turn":
                    pe.wait_ge(gqa_probs, a + 1)
                    turn4(s, [(a2[:, t, k * P:(k + 1) * P], k * T + t * P) for k in range(2) for t in range(TB)])
                elif kind == "gqa_out":
                    evacuated(("gqa_turn", a, 0))
                    if a == 0:
                        evacuated(("ev_v", 0, 0))
                    b = open_bank(s)
                    p0, c0 = 64 * (a % 2), 64 * (a // 4)
                    for k in range(TB):
                        ins = pe.matmul(psum[p0:p0 + 64, b, 0:T], v2[:, k, c0:c0 + 64], at2[:, k, :],
                                        start=(k == 0), stop=(k == TB - 1))
                    ins.then_inc(job_done, 1)
                elif kind == "turn_ws":
                    turn4(s, [(w_s[:, 4 * a + k, :], k * P) for k in range(4)])
                elif kind == "gate_s":
                    if a == 0:
                        pe.wait_ge(v_normed, 3)
                        evacuated(("turn_ws", 0, 0))
                        evacuated(("turn_ws", 1, 0))
                    b = open_bank(s)
                    for m in range(2):
                        for t in range(TB):
                            g = 2 * a + m
                            ins = pe.matmul(bank(b, 4, P)[:, 2 * m + t, :], v_tok[:, t, g * P:(g + 1) * P],
                                            ws_t[:, g, :], start=True, stop=True)
                    ins.then_inc(job_done, 1)

        def pair(width, rhs, panels, blocks, h_first, tile, first, last, h_free):
            (gs, gf), (us, uf), (ds, df) = panels
            pe.wait_ge(slot_full[gs], gf)
            pe.wait_ge(slot_full[us], uf)
            n = blocks * P
            sides = [ring[:, k * SLOT:k * SLOT + KT * n].rearrange("p (k n) -> p k n", k=KT) for k in (gs, us)]
            for j in range(blocks):
                if h_free is not None:
                    pe.wait_ge(h_set, h_free + j)
                for side, wt in enumerate(sides):
                    for k in range(KT):
                        ins = pe.matmul(psum[:, 4 + j, side * T:side * T + width], wt[:, k, j * P:(j + 1) * P],
                                        rhs[:, k, 0:width], start=(k == 0), stop=(k == KT - 1))
                ins.then_inc(job_done, 1)
            pe.wait_ge(slot_full[ds], df)
            wd = ring[:, ds * SLOT:ds * SLOT + blocks * D].rearrange("p (j d) -> p j d", d=D)
            for j in range(blocks):
                pe.wait_ge(h_set, h_first + (j + 1))
                for k in range(KT):
                    ins = pe.matmul(bank(k // 2, 2, T)[:, k % 2, 0:width], wd[:, j, k * P:(k + 1) * P],
                                    tile[:, j, 0:width], start=(first and j == 0 and k % 2 == 0),
                                    stop=(last and j == blocks - 1), skip_group_check=True)
            ins.then_inc(job_done, 1)

        def expert(m, x, e, it):
            h0 = x * (4 * m["pairs"]) + m["h"]

            def body(width):
                pe.wait_ge(perm_set, x + (m["perm"] + 1))
                pe.wait_ge(added, x * 4 + m["add"])
                for i in range(4):
                    for k in range(2):
                        for t in range(TB):
                            ins = pe.matmul(bank(i, 2, T)[:, k, 0:width], tok[:, t, (2 * i + k) * P:(2 * i + k + 1) * P],
                                            perm[:, t, 0:width], start=(t == 0), stop=(t == TB - 1))
                    ins.then_inc(job_done, 1)
                pe.wait_ge(ye_turned, x * 2 + m["turned"])
                for c, n in chunks(width):
                    for t in range(TB):
                        ins = pe.transpose(bank(4, 2, T)[:, c, t * P:(t + 1) * P], perm_w[:, t, c * P:(c + 1) * P],
                                           ident)
                ins.then_inc(job_done, 1)
                pe.wait_ge(xe_set, x * 4 + (4 * (N1 if m["n"] == N2 else 0) + 4))
                pe.wait_ge(spread_set, x + ((N1 if m["n"] == N2 else 0) + 1))
                for t in range(m["pairs"]):
                    if m["n"] == N1:
                        panels = [(3 * e + k, it * 16 + 16 * (m["base"][3 * e + k] + 1)) for k in range(3)]
                    else:
                        panels = [((3 * t + k) % SLOTS,
                                   x * 48 + 16 * (m["base"][(3 * t + k) % SLOTS] + (3 * t + k) // SLOTS + 1))
                                  for k in range(3)]
                    pair(width, xe, panels, 4, h0 + 4 * t, h_tile[t % 2], t == 0, t == m["pairs"] - 1,
                         h0 + (4 * t - 3) if t else None)
                pe.wait_ge(ye_copied, x * 4 + (m["y"] + 4))
                pe.wait_ge(h_set, h0 + 4 * m["pairs"])
                for half in range(2):
                    for c, n in chunks(width):
                        for k in range(4):
                            dst, src = psum[0:n, 4 + 2 * c + half, k * P:(k + 1) * P], ye[:, 4 * half + k, c * P:c * P + n]
                            if (half, c, k) == (0, 0, 0):
                                ins = pe.matmul(dst, src, ident, start=True, stop=True)
                            else:
                                ins = pe.transpose(dst, src, ident)
                    ins.then_inc(job_done, 1)
                pe.wait_ge(ye_turned, x * 2 + (m["turned"] + 2))
                for i in range(4):
                    for k in range(2):
                        for c, n in chunks(width):
                            f = 2 * i + k
                            ins = pe.matmul(bank(i, 2, T)[:, k, :], ye_tok[0:n, c, f * P:(f + 1) * P],
                                            spread[0:n, c, :], start=(c == 0), stop=(c == len(chunks(width)) - 1))
                    ins.then_inc(job_done, 1)

            return body

        def mixture(m, n, rank_step):
            evacuated(rank_step)
            for s in plans[2 * n][-8:]:
                evacuated(s)
            if m["n"] == N1:
                with pe.Fori(0, N1 // 2) as it:
                    for e in range(2):
                        x = it * 2 + e
                        count = pe.value_load(counts_i[0:1, bass.ds(x, 1)], min_val=0, max_val=T)
                        by_width(pe, count, TIERS[n], expert(m, x, e, it))
            else:
                with pe.Fori(0, m["n"]) as x:
                    count = pe.value_load(counts_i[0:1, bass.ds(x, 1)], min_val=0, max_val=T)
                    by_width(pe, count, TIERS[n], expert(m, x, 0, None))
            pe.wait_ge(added, m["add"] + 4 * m["n"])
            pe.wait_ge(ye_turned, m["turned"] + 2 * m["n"])

        walk(plans[0])
        mixture(mixtures[0], 0, ("rank", 0, 0))
        walk(plans[1])
        pe.wait_ge(modulated, 2 * KT)
        for s in plans[1][-8:]:
            evacuated(s)
        q = HF
        for n, (_, width) in enumerate(FFN_P):
            pair(T, hT, [(panel[(name, n)][0], 16 * panel[(name, n)][1]) for name in ("gate", "up", "down")],
                 width // P, q, h_tile[n % 2], n == 0, n == len(FFN_P) - 1, q - 3 if n else None)
            q += width // P
        pe.wait_ge(added, Y2)
        pe.wait_ge(h_set, H2)
        walk(plans[2])
        mixture(mixtures[1], 1, ("rank", 1, 0))
        walk(plans[3])

    ctx.close()


_OUT = (1, T, D)


def kernel(**inputs):
    import concourse.bacc as bacc
    from concourse.bass_utils import run_bass_kernel_spmd

    nc = bacc.Bacc("TRN2", target_bir_lowering=False, num_devices=1)
    arrays, w = {}, {}
    for name, value in {**inputs, "consts": shape_constants()}.items():
        a = np.ascontiguousarray(value)
        arrays[name + "_in"] = a
        w[name] = nc.dram_tensor(name + "_in", a.shape, mybir.dt.from_np(a.dtype), kind="ExternalInput").ap()
    out = nc.dram_tensor("out", (T, D), F32, kind="ExternalOutput").ap()
    build(nc, w, out)
    return run_bass_kernel_spmd(nc, [arrays], core_ids=[0]).results[0]["out"].reshape(_OUT)
```

```python
from contextlib import ExitStack

import numpy as np
import concourse.bass as bass
from concourse import mybir

F32 = mybir.dt.float32
F32R = mybir.dt.float32r
I32 = mybir.dt.int32
ALU = mybir.AluOpType
ACT = mybir.ActivationFunctionType
AX = mybir.AxisListType

P = 128
D = 1024
KT = D // P
T = 256
TB = T // P
PANEL = 512
SLOT = KT * PANEL
SLOTS = 5
FF_SLOTS = 3
STAGES = 6
BANKS = 8
EPS = 1e-5
NEG = -1e30

DA_H, RET_H, MEM_H = 8, 4, 4
LAMBDA_INIT = 0.2
ALPHA1 = 2.0 ** 0.25
ALPHA2 = 4.0 ** 0.25
G1, E1, N1 = 4, 4, 16
N2 = 8
FF1 = 512
assert FF1 == PANEL
FF2 = 3584
FFN = 2816
POOL_W = (2, 4, 8, 16)
GQA_H, GQA_KV, GQA_D = 8, 2, 64
WIN = 128
SG_G = 8

WIDTHS = (P, T)
VEC_A = {}
VEC_B = {}
for _table, _rows in ((VEC_A, (("b_gate", 24), ("gn_g", 8), ("gn_b", 8), ("ln1_g", 8), ("ln1_b", 8), ("da_g", 1),
                               ("ln2_g", 8), ("ln2_b", 8), ("lng_2", 32), ("c", 8), ("pool_scale", 4))),
                      (VEC_B, (("ada_b", 96), ("lnb_2", 32)))):
    _at = 0
    for _name, _n in _rows:
        _table[_name] = (_at, _n)
        _at += _n

C_IDENT, C_USTRICT, C_IOTA = 0, 128, 256
C_COMMON = 512
C_PHASE = 2560


def shape_constants():
    out = np.zeros((P, C_COMMON + 2 * C_PHASE), np.float32)
    i = np.arange(P)
    out[:, C_IDENT:C_IDENT + P] = np.eye(P)
    out[:, C_USTRICT:C_USTRICT + P] = i[:, None] < i[None, :]
    out[:, C_IOTA:C_IOTA + T] = np.arange(T)
    t = np.arange(T)
    dist = (t[:, None] - t[None, :]).astype(np.float64)
    causal = np.where(dist >= 0, -dist, NEG)
    window = np.where(np.abs(dist) <= WIN, -np.abs(dist), NEG)
    for b in range(TB):
        out[:, C_COMMON + b * T:C_COMMON + (b + 1) * T] = causal[b * P:(b + 1) * P]
        out[:, C_COMMON + C_PHASE + b * T:C_COMMON + C_PHASE + (b + 1) * T] = window[b * P:(b + 1) * P]
    for h in range(RET_H):
        log_g = np.log(1.0 - 2.0 ** (-5.0 - h))
        m = np.where(dist.T <= 0, 0.0, 0.0)
        m = np.where(dist >= 0, np.exp(np.maximum(dist, 0) * log_g), 0.0).T * (128.0 ** -0.5)
        for b in range(TB):
            at = C_COMMON + 2 * T + (h * TB + b) * T
            out[:, at:at + T] = m[b * P:(b + 1) * P]
    for g, w in enumerate(POOL_W):
        r = w // 2
        lo, hi = np.maximum(t - r, 0), np.minimum(t + r + 1, T)
        m = ((t[:, None] >= lo[None]) & (t[:, None] < hi[None])) / (hi - lo)[None] - np.eye(T)
        for b in range(TB):
            at = C_COMMON + C_PHASE + 2 * T + (g * TB + b) * T
            out[:, at:at + T] = m[b * P:(b + 1) * P]
    return out


def mixer1_steps():
    s = [("turn_x", i, 0) for i in range(4)]
    s += [("gemm", "da_q", i) for i in range(4)] + [("gemm", "da_k", i) for i in range(4)]
    s += [("vec", 0, 0), ("vec", 1, 0)]
    s += [("turn_mem", i, 0) for i in range(4)]
    s += [("gemm", "da_v", i) for i in range(4)]
    fill = [("gemm", n, i) for n, k in (("r_q", 2), ("r_k", 2), ("r_v", 4), ("r_g", 4), ("gate0", 4)) for i in range(k)]
    for h in range(DA_H):
        s += [("da_score", h, 0), ("da_score", h, 1), fill.pop(0)]
        if h:
            s += [("da_norm", h - 1, 0)]
        s += [fill.pop(0), ("da_turn", h, 0), ("ada", 0, h), ("da_out", h, 0)]
    s += [("ret_score", 0, 0), ("da_norm", DA_H - 1, 0)]
    s += [("gemm", "branch0", i) for i in range(4)]
    fill = [("gemm", n, i) for n, k in (("m_q", 4), ("m_k", 4), ("m_v", 4)) for i in range(k)]
    for h in range(RET_H):
        if h:
            s += [("ret_score", h, 0), fill.pop(0)]
        s += [("ret_out", h, 0), fill.pop(0), ("ada", 0, DA_H + h), ("ret_mean", h, 0), fill.pop(0), ("ret_var", h, 0)]
    s += fill
    fill = [("gemm", n, i) for n, k in (("gate1", 4), ("branch1", 4)) for i in range(k)]
    for h in range(MEM_H):
        s += [("mem_score", h, 0), fill.pop(0), ("mem_turn", h, 0), fill.pop(0), ("mem_out", h, 0), ("ada", 1, h)]
    for n in ("gate2", "branch2"):
        for i in range(4):
            s += [("gemm", n, i)] + [("ada", 1, MEM_H + (4 if n == "branch2" else 0) + i)]
    s += [("gemm", "w_o", i) for i in range(4)]
    s += [("ln_sum", 0, 0), ("ln_sq", 0, 0), ("logits", 0, 0)]
    s += [("turn_tok", 0, i) for i in range(4)]
    return s + [("rank", 0, 0)]


def mixer2_steps():
    s = [("ln_sum", 1, 0), ("ln_sq", 1, 0)]
    s += [("gemm", "ev_p", i) for i in range(2)] + [("gemm", "ev_q", i) for i in range(2)]
    s += [("ev_k", 0, 0), ("ev_v", 0, 0)]
    fill = [("pool", 0, 0), ("pool", 1, 0), ("pool_map", 0, 0), ("pool_map", 1, 0)]
    s += [("gqa_score", 0, 0), ("gqa_score", 1, 0)] + fill
    for h in range(GQA_H):
        s += [("gqa_turn", h, 0)]
        if h + 2 < GQA_H:
            s += [("gqa_score", h + 2, 0)]
        s += [("gqa_out", h, 0)]
    s += [("gemm", "ev_o", i) for i in range(4)]
    return s + [("ln_sum", 2, 0), ("ln_sq", 2, 0)]


def mixer3_steps():
    s = [("ln_sum", 3, 0), ("ln_sq", 3, 0), ("turn_ws", 0, 0), ("turn_ws", 1, 0)]
    s += [("gemm", "od_v", i) for i in range(4)] + [("gemm", "od_u", i) for i in range(4)]
    s += [("gate_s", i, 0) for i in range(4)]
    s += [("gemm", "od_o", i) for i in range(4)]
    s += [("ln_sum", 4, 0), ("ln_sq", 4, 0), ("logits", 1, 0)]
    s += [("turn_tok", 1, i) for i in range(4)]
    return s + [("rank", 1, 0)]


def last_steps():
    return [("ln_sum", 5, 0), ("ln_sq", 5, 0)] + [("turn_out", i, 0) for i in range(4)]


A_CONST, A_PHASE, A_COLA, A_COLB, A_MOD, A_SMALL = 0, 640, 3200, 3328, 3456, 3584
R_X, R_MEM, R_Q, R_K, R_V, R_TAIL = 4096, 6144, 8192, 10240, 12288, 14336
ARENA = 15744
OVER_SLOTS = 2 * SLOT
M_RQ, M_RK, M_RV, M_RG, M_YDA = (OVER_SLOTS + n for n in (0, 1024, 2048, 4096, 6144))
M_LOGIT, M_E, M_A, M_AT, M_OSQ, M_RSTD, M_RSQ, M_GATE, M_MERGED, M_ADA = (
    OVER_SLOTS + 8192 + n for n in (0, 512, 1024, 1536, 2048, 2304, 2560, 3072, 5120, 7168))
M_MIX, M_WPOOL, M_WS, M_ROWS, M_BIAS = (OVER_SLOTS + n for n in (0, 2048, 2560, 3584, 5632))
OVER = OVER_SLOTS + 16384


def build(nc, w, out):
    ctx = ExitStack()

    def sem(name):
        return ctx.enter_context(nc.semaphore(name))

    ring = ctx.enter_context(nc.sbuf_tensor("ring", [P, FF_SLOTS * SLOT], F32))
    arena = ctx.enter_context(nc.sbuf_tensor("arena", [P, ARENA], F32))
    counts_i = ctx.enter_context(nc.sbuf_tensor("counts_i", [P, N1], I32))
    psum = ctx.enter_context(nc.psum_tensor("psum", [P, BANKS, 512], F32))
    with nc.sbuf_tensor("mixer_tiles", [P, OVER], F32) as over_mixers:
        pass
    stage_hi = ctx.enter_context(nc.sbuf_tensor("stage_hi", [P, STAGES, 1024], F32R))
    stage_lo = ctx.enter_context(nc.sbuf_tensor("stage_lo", [P, STAGES, 1024], F32R))
    x_hi = ctx.enter_context(nc.sbuf_tensor("x_hi", [P, KT, T], F32R))
    x_lo = ctx.enter_context(nc.sbuf_tensor("x_lo", [P, KT, T], F32R))
    h_hi = ctx.enter_context(nc.sbuf_tensor("h_hi", [P, 4, T], F32R))
    h_lo = ctx.enter_context(nc.sbuf_tensor("h_lo", [P, 4, T], F32R))
    y_tok = ctx.enter_context(nc.sbuf_tensor("y_tok", [P, TB, D], F32))

    def region(at, *shape):
        n = int(np.prod(shape))
        v = arena[:, at:at + n]
        if len(shape) == 2:
            return v.rearrange("p (a b) -> p a b", b=shape[1])
        if len(shape) == 3:
            return v.rearrange("p (a b c) -> p a b c", b=shape[1], c=shape[2])
        return v

    def scratch(at, *shape):
        n = int(np.prod(shape))
        v = over_mixers[:, at:at + n]
        return v.rearrange("p (a b) -> p a b", b=shape[1]) if len(shape) == 2 else v

    def slot(s, a, words=SLOT):
        v = ring[:, s * SLOT:s * SLOT + words] if s < FF_SLOTS else scratch((s - FF_SLOTS) * SLOT, words)
        return v.rearrange("p (a b) -> p a b", a=a)

    def bank(b, *shape):
        v = psum[:, b, :]
        return v.rearrange("p (a b) -> p a b", b=shape[1]) if shape else v

    def over(v, n):
        return v.unsqueeze(1).to_broadcast([v.shape[0], n, v.shape[1]])

    def along(v, n):
        return v.unsqueeze(2).to_broadcast([v.shape[0], v.shape[1], n])

    ident = region(A_CONST + C_IDENT, P)
    ustrict = region(A_CONST + C_USTRICT, P)
    iota = region(A_CONST + C_IOTA, T)
    ones = region(A_CONST + 512, P)
    causal = region(A_PHASE, TB, T)
    decay = region(A_PHASE + 2 * T, RET_H * TB, T)
    wbias = region(A_PHASE, TB, T)
    pool_m = region(A_PHASE + 2 * T, len(POOL_W) * TB, T)
    vec_a = scratch(M_LOGIT, P)
    vec_b = scratch(M_E, P)
    cols_a, cols_b = region(A_COLA, P), region(A_COLB, P)
    vec_rows = [sum(n for _, n in table.values()) for table in (VEC_A, VEC_B)]
    mod = region(A_MOD, 2 * 48)
    small = region(A_SMALL, 512)
    lam_rows, lam_prod, lam_sum = scratch(M_A, 4 * 64), scratch(M_AT, 2, 64), small[:, 0:2]
    lam_exp, neg_lam = small[:, 2:4], small[:, 4:5]
    cond = small[:, 8:16]
    sink = small[:, 16:24]
    bias_r1 = small[:, 24:44]
    dmax, dsum, drec = small[:, 44:46], small[:, 46:48], small[:, 48:50]
    da_gain = small[:, 50:51]
    eps = small[:, 51:52]
    esink = small[:, 52:54]
    modp1 = small[:, 64:64 + 2 * 48]

    def col_a(name, k=0):
        at = VEC_A[name][0] + k
        return cols_a[:, at:at + 1]

    def col_b(name, k=0):
        at = VEC_B[name][0] + k
        return cols_b[:, at:at + 1]

    xT, memT, yda = region(R_X, KT, T), region(R_MEM, KT, T), scratch(M_YDA, KT, T)
    x_tok, mem_tok = region(R_Q, TB, D), scratch(M_RV, TB, D)
    daq, dak, dav = region(R_Q, KT, T), region(R_K, KT, T), region(R_V, TB, D)
    rq, rk, rv, rg = scratch(M_RQ, RET_H, T), scratch(M_RK, RET_H, T), scratch(M_RV, TB, D), scratch(M_RG, KT, T)
    mq, mk, mv = daq, dak, dav
    ymem, yret = memT, rg
    gate, merged = scratch(M_GATE, KT, T), scratch(M_MERGED, KT, T)
    logit, e_prob, a_prob, a_turn = (scratch(M_LOGIT, 2, T), scratch(M_E, 2, T), scratch(M_A, TB, T),
                                     scratch(M_AT, 2, T))
    osq, rstd = scratch(M_OSQ, T), scratch(M_RSTD, T)
    ret_s, ret_o, ret_stat, ret_sq = (region(R_TAIL, 2, T), region(R_TAIL + 512, 2, T), region(R_TAIL + 1024, T),
                                      scratch(M_RSQ, 2, T))
    gtmp = ret_sq
    z, z_sq = region(R_Q, KT, T), region(R_K, KT, T)
    ln_stat = region(R_TAIL + 1024, T)
    ada_sum = scratch(M_ADA, 2, PANEL)
    router = (small[:, 160:320].rearrange("p (k e) -> p k e", e=G1 + N1),
              small[:, 320:384].rearrange("p (k e) -> p k e", e=N2))

    acc, hT = region(R_X, KT, T), region(R_MEM, KT, T)
    tok = region(R_V, TB, D)
    s_tile, h_tile = region(R_Q, TB, PANEL), region(R_Q + 1024, TB, PANEL)
    perm, spread = region(R_K, TB, T), region(R_K + 512, TB, T)
    w_pool = scratch(M_WPOOL, 4, P)
    later_sq = region(R_MEM, KT, T)
    mix = scratch(M_MIX, KT, T)
    p_tok, pooled = region(R_Q, TB, 4 * P), region(R_Q + 1024, 4, T)
    q2, k2, v2 = region(R_K, 4, T), region(R_K + 1024, GQA_KV, T), region(R_K + 1536, TB, P)
    logit2, e2, a2, at2 = (region(R_V, TB, T), region(R_V + 512, TB, T), region(R_V + 1024, TB, T),
                           region(R_V + 1536, TB, T))
    v_tok = region(R_Q, TB, D)
    ws_t = region(R_K, SG_G, P)
    w_s, sg_rows, bs_rows = scratch(M_WS, SG_G, P), scratch(M_ROWS, 2, D), scratch(M_BIAS, SG_G, P)
    out_tok = region(R_V, TB, D)

    def route(at, *shape):
        return region(R_TAIL + at, *shape)

    lg, top_v, top_e, top_1, top_2, sel, hot_g = (route(0, TB, G1 + N1), route(40, TB, N1), route(72, TB, N1),
                                                  route(104, TB, N1), route(136, TB, N1), route(168, TB, N1),
                                                  route(200, TB, G1))
    peak, peak_1, peak_2, ratio, wt_1, wt_2, p_top = (route(208 + 2 * k, TB) for k in range(7))
    desc = route(224, N1)
    ex_g = route(240, TB, G1)
    bn_s, bn_a = route(256, TB, 4 * 6), route(304, TB, 2)
    table = region(R_TAIL + 320, 2 * TB, N2 + 1)
    weights = region(R_TAIL + 360, TB, N1 + 4)
    mine, mine_w, own_w = route(400, 2 * TB), route(404, TB, 4), route(412, TB, 4)
    job_done = sem("job_done")
    bank_free = [sem(f"bank_free{b}") for b in range(BANKS)]
    slot_full = [sem(f"slot_full{s}") for s in range(SLOTS)]
    const_in, x_in, mem_in, vec_in, row_in = (sem("const_in"), sem("x_in"), sem("mem_in"), sem("vec_in"),
                                              sem("row_in"))
    phase_in = sem("phase_in")
    ones_set = sem("ones_set")
    dve_step, act_step = sem("dve_step"), sem("act_step")
    lam_summed, lam_exped, neg_lam_set, cond_set = (sem("lam_summed"), sem("lam_exped"), sem("neg_lam_set"),
                                                    sem("cond_set"))
    da_logits, da_exped, da_probs, da_squared, da_y = (sem("da_logits"), sem("da_exped"), sem("da_probs"),
                                                       sem("da_squared"), sem("da_y"))
    ret_scored, ret_centred, ret_squared, ret_normed, ret_scaled, ret_y = (
        sem("ret_scored"), sem("ret_centred"), sem("ret_squared"), sem("ret_normed"), sem("ret_scaled"), sem("ret_y"))
    mem_max, mem_probs = sem("mem_max"), sem("mem_probs")
    gated, merged_set = sem("gated"), sem("merged_set")
    ln_centred, ln_squared, ln_normed, ln_out = sem("ln_centred"), sem("ln_squared"), sem("ln_normed"), sem("ln_out")
    ada_summed = sem("ada_summed")
    router_in, small_in, modp1_set, modulated, acc_scaled = (sem("router_in"), sem("small_in"), sem("modp1_set"),
                                                             sem("modulated"), sem("acc_scaled"))
    route_diff, route_exp, masks_set, counts_set = sem("route_diff"), sem("route_exp"), sem("masks_set"), sem("counts_set")
    gqa_logits, gqa_exped, gqa_probs = sem("gqa_logits"), sem("gqa_exped"), sem("gqa_probs")
    v_normed, sg_gated, z_set = sem("v_normed"), sem("sg_gated"), sem("z_set")
    mine_set = sem("mine_set")
    perm_set, x_hi_set, x_lo_set, spread_set = sem("perm_set"), sem("x_hi_set"), sem("x_lo_set"), sem("spread_set")
    chunk_hi, chunk_lo = sem("chunk_hi"), sem("chunk_lo")
    silu_set, h_set, h_hi_set, h_lo_set = sem("silu_set"), sem("h_set"), sem("h_hi_set"), sem("h_lo_set")
    y_copied, added = sem("y_copied"), sem("added")
    out_staged, out_stored = sem("out_staged"), sem("out_stored")

    plans = (mixer1_steps(), mixer2_steps(), mixer3_steps(), last_steps())
    def unit_steps(pairs, routed):
        s = [("gather", i) for i in range(4)] + [("spread",)] if routed else []
        chunk = lambda side, p: [("chunk", side, p, c) for c in range(4 if side != "D" else pairs[p] // P)]
        s += chunk("G", 0) + chunk("U", 0)
        for p in range(1, len(pairs)):
            g = chunk("G", p)
            s += g[:2] + [("turn", p - 1)] + g[2:] + chunk("D", p - 1) + chunk("U", p)
        return s + [("turn", len(pairs) - 1)] + chunk("D", len(pairs) - 1) + [("scatter", i) for i in range(4)]

    FFN_P = [min(PANEL, FFN - c) for c in range(0, FFN, PANEL)]
    feeds = [dict(pairs=[FF1] * E1, n=G1, routed=True, gain=None, weights=E1),
             dict(pairs=FFN_P, n=1, routed=False, gain=(0, 5), weights=0),
             dict(pairs=[PANEL] * (FF2 // PANEL), n=N2, routed=True, gain=(1, 5), weights=1)]
    chunks_before = pairs_before = routed_before = units_before = 0
    for f in feeds:
        f["steps"] = unit_steps(f["pairs"], f["routed"])
        f["jobs"] = len(f["steps"])
        f["pos"] = {q: n + 1 for n, q in enumerate(f["steps"])}
        f["order"] = [q for q in f["steps"] if q[0] == "chunk"]
        f["chunks"] = len(f["order"])
        f["count"] = {q: n for n, q in enumerate(f["order"])}
        f["c0"], f["p0"], f["r0"], f["u0"] = chunks_before, pairs_before, routed_before, units_before
        chunks_before += f["chunks"] * f["n"]
        pairs_before += len(f["pairs"]) * f["n"]
        routed_before += f["n"] if f["routed"] else 0
        units_before += f["n"]
    index, done, plan_end = {}, {}, []
    at = 0
    for n, plan in enumerate(plans):
        for s in plan:
            at += 1
            index[s], done[s] = len(index), at
        plan_end.append(at)
        if n < 3:
            feeds[n]["at"] = at
            at += feeds[n]["jobs"] * feeds[n]["n"]
    def job_bank(s):
        return index[s] % BANKS

    def bank_through(s):
        return bank_free[index[s] % BANKS], index[s] // BANKS + 1

    gemm_src = {}
    at = 0
    for name, cols in (("da_q", 1024), ("da_k", 1024), ("da_v", 1024), ("r_q", 512), ("r_k", 512), ("r_v", 1024),
                       ("r_g", 1024), ("m_q", 1024), ("gate0", 1024), ("gate1", 1024), ("gate2", 1024)):
        gemm_src[name] = (w["w_in"][0], at)
        at += cols
    gemm_src["m_k"], gemm_src["m_v"] = (w["w_mem_kv"][0], 0), (w["w_mem_kv"][0], D)
    for n in range(3):
        gemm_src[f"branch{n}"] = (w["w_branch"][0, n], 0)
    gemm_src["w_o"] = (w["w_o"][0], 0)
    gemm_src["ev_p"], gemm_src["ev_q"] = (w["ev_w_in_2"][0], 0), (w["ev_w_in_2"][0], 512)
    gemm_src["ev_o"] = (w["ev_w_out_2"][0], 0)
    gemm_src["od_u"], gemm_src["od_v"] = (w["od_w_in_2"][0], 0), (w["od_w_in_2"][0], D)
    gemm_src["od_o"] = (w["od_w_out_2"][0], 0)
    token_major = ("da_v", "r_v", "m_v", "ev_p", "od_v")

    def cols(src, c0, n=PANEL):
        return src[:, c0:c0 + n].rearrange("(k p) n -> p k n", p=P)

    fills = [0] * SLOTS
    freed = [None] * SLOTS
    loads = {0: [], 1: [], 2: []}
    panel = {}

    def fill_slot(where, key, s, words, src, free):
        loads[where].append((s, words, src, freed[s]))
        fills[s] += 1
        freed[s] = free
        panel[key] = (s, fills[s])

    def plan_loads(n, count, start=0):
        at = start
        for s in plans[n]:
            key, words = s, SLOT
            if s[0] == "gemm" and s[2] % 2 == 0:
                src, c0 = gemm_src[s[1]]
                src, free = cols(src, c0 + s[2] // 2 * PANEL), (job_done, done[("gemm", s[1], s[2] + 1)])
            elif s[0] == "ev_k":
                src, words = cols(w["ev_w_in_2"][0], 1024, 256), KT * 256
                free = (job_done, done[("ev_v", 0, 0)])
            elif s[0] == "ada":
                src, free = cols(w["ada_w_2"][s[1]], s[2] * PANEL), (ada_summed, 12 * s[1] + s[2] + 1)
            else:
                continue
            fill_slot(n, key, at % count, words, src, free)
            at += 1
        return at

    def panel_order(f):
        return [q[1:3] for q in f["order"] if q[3] == 0]

    for n in range(3):
        plan_loads(n, SLOTS)
        f = feeds[n]
        f["freed"], f["base"] = freed[:FF_SLOTS], fills[:FF_SLOTS]
        order = panel_order(f)
        for k in range(len(order)):
            fills[k % FF_SLOTS] += f["n"]
            if k >= len(order) - FF_SLOTS:
                last = ("chunk", *order[k], 3 if order[k][0] != "D" else f["pairs"][order[k][1]] // P - 1)
                freed[k % FF_SLOTS] = (chunk_lo, f["c0"] + f["chunks"] * (f["n"] - 1) + f["count"][last] + 1)
        for k in range(FF_SLOTS, SLOTS):
            freed[k] = (job_done, f["at"] + f["jobs"] * f["n"])

    def panel_of(s):
        return panel[("gemm", s[1], s[2] - s[2] % 2) if s[0] == "gemm" else s]

    def layer_norm_scalar(act, n, z, z_sq, sq_done, sq_bank, sq_free, gain_bias, dst):
        for half in range(2):
            act.wait_ge(ln_centred, 2 * n + half + 1)
            act.activation(z_sq[:, 4 * half:4 * half + 4, :], z[:, 4 * half:4 * half + 4, :],
                           ACT.Square).then_inc(ln_squared, 1)
        act.wait_ge(job_done, sq_done)
        act.activation(ln_stat, psum[:, sq_bank, 0:T], ACT.Sqrt, bias=eps, scale=1.0 / D).then_inc(sq_free, 1)
        for k in range(KT):
            if k % 4 == 0:
                act.wait_ge(ln_normed, 2 * n + k // 4 + 1)
            g, b = gain_bias(k)
            act.activation(dst[:, k, :], z[:, k, :], ACT.Identity, bias=b, scale=g).then_inc(ln_out, 1)

    def layer_norm_vector(dve, settle, n, z, sum_done, sum_bank, sum_free, sq_read):
        dve.wait_ge(job_done, sum_done)
        dve.tensor_scalar(ln_stat, psum[:, sum_bank, 0:T], 1.0 / D, None, ALU.mult).then_inc(sum_free[0], 1)
        dve.wait_ge(*sum_free)
        for half in range(2):
            zh = z[:, 4 * half:4 * half + 4, :]
            dve.tensor_tensor(zh, zh, over(ln_stat, 4), ALU.subtract).then_inc(ln_centred, 1)
        dve.wait_ge(ln_centred, 2 * n + 2)
        dve.wait_ge(*sq_read)
        settle(dve.reciprocal(ln_stat, ln_stat))
        for half in range(2):
            zh = z[:, 4 * half:4 * half + 4, :]
            dve.wait_ge(ln_squared, 2 * n + half + 1)
            dve.tensor_tensor(zh, zh, over(ln_stat, 4), ALU.mult).then_inc(ln_normed, 1)

    def by_width(eng, count, body):
        with eng.If(count < P + 1):
            body(P)
        with eng.Else():
            body(T)

    def units(eng, f, u_body):
        if not f["routed"]:
            u_body(0)(T)
            return
        with eng.Fori(0, f["n"]) as u:
            count = eng.value_load(counts_i[0:1, bass.ds(u, 1)], min_val=0, max_val=T)
            by_width(eng, count, u_body(u))

    def at_unit(u, per_unit, value):
        return u * per_unit + value

    def pair_width(f, side, p):
        return f["pairs"][p] if side != "D" else D

    def chunk_view(tensor, f, side, p, c):
        n = f["count"][("chunk", side, p, c)] % STAGES
        rows, width = (2, f["pairs"][p]) if side != "D" else (1, D)
        return tensor[:, n, 0:rows * width].rearrange("p (a b) -> p a b", b=width)

    def chunk_source(f, side, p, c):
        k = panel_order(f).index((side, p)) % FF_SLOTS
        rows, width = (2, f["pairs"][p]) if side != "D" else (1, D)
        words = KT * f["pairs"][p]
        return slot(k, words // width, words)[:, rows * c:rows * (c + 1), :]

    def h_point(f):
        make, split = {}, {}
        last = len(f["pairs"]) - 1
        for p in range(last):
            make[("chunk", "G", p + 1, 0)] = p
            split[("chunk", "G", p + 1, 3)] = p
        make[("chunk", "D", last, 0)] = last
        split[("chunk", "D", last, 1)] = last
        return make, split

    def mod_cols(tile, layer, part, k):
        at = layer * 48 + part * KT + k
        return tile[:, at:at + 1]

    block = ctx.enter_context(nc.Block())

    @block.sync
    def _(sp):
        sp.dma_start(x_tok, w["x"][0].rearrange("(b p) d -> p b d", p=P)).then_inc(x_in, 16)
        sp.dma_start(arena[:, 0:C_COMMON], w["consts"][:, 0:C_COMMON]).then_inc(const_in, 16)

        def load(s, words, src, wait):
            if wait:
                sp.wait_ge(*wait)
            sp.dma_start(slot(s, src.shape[1], words), src).then_inc(slot_full[s], 16)

        def source(f, n, u, side, p):
            if n == 0:
                gate_w, up_w, down_w = w["w1"][0][u * E1 + p], w["w3"][0][u * E1 + p], w["w2"][0][u * E1 + p]
                c0 = 0
            elif n == 1:
                gate_w, up_w, down_w = w["ffn_w_gate_2"][0], w["ffn_w_up_2"][0], w["ffn_w_down_2"][0]
                c0 = p * PANEL
            else:
                gate_w, up_w, down_w = w["moe_w_gate_2"][0][u], w["moe_w_up_2"][0][u], w["moe_w_down_2"][0][u]
                c0 = p * PANEL
            width = f["pairs"][p]
            if side == "D":
                return down_w[c0:c0 + width, :].rearrange("(j p) d -> p j d", p=P)
            return cols(gate_w if side == "G" else up_w, c0, width)

        def unit_loads(f, n, u):
            for k, (side, p) in enumerate(panel_order(f)):
                wait = (chunk_lo, at_unit(u, f["chunks"], f["c0"] + 4 * (k - FF_SLOTS + 1)))
                if isinstance(u, int) and k < FF_SLOTS:
                    wait = f["freed"][k]
                load(k % FF_SLOTS, KT * f["pairs"][p], source(f, n, u, side, p), wait)

        for n, f in enumerate(feeds):
            for one in loads[n]:
                load(*one)
            unit_loads(f, n, 0)
            if f["n"] > 1:
                with sp.Fori(1, f["n"]) as u:
                    unit_loads(f, n, u)
        for i in range(4):
            sp.wait_ge(*bank_through(("turn_out", i, 0)))
            c = slice(i % 2 * 4 * P, (i % 2 + 1) * 4 * P)
            sp.dma_start(out[i // 2 * P:(i // 2 + 1) * P, c], out_tok[:, i // 2, c]).then_inc(out_stored, 16)
        sp.wait_ge(out_stored, 4 * 16)

    @block.gpsimd
    def _(pool):
        nc.gpsimd.memset(ones, 1.0).then_inc(ones_set, 1)
        nc.gpsimd.memset(eps, EPS).then_inc(ones_set, 1)

    @block.scalar
    def _(act):
        step = [0]

        def settle(ins):
            step[0] += 1
            ins.then_inc(act_step, 1)
            act.wait_ge(act_step, step[0])

        def full(s):
            act.wait_ge(job_done, done[s])
            return job_bank(s)

        def evacuated(s):
            act.wait_ge(*bank_through(s))

        for table, tile, names in ((VEC_A, vec_a, {"b_gate": w["b_gate"], "gn_g": w["ret_gn_g"], "gn_b": w["ret_gn_b"],
                                                   "ln1_g": w["ln1_g"], "ln1_b": w["ln1_b"], "da_g": w["da_norm_g"],
                                                   "ln2_g": w["ln2_g"], "ln2_b": w["ln2_b"], "lng_2": w["ln_g_2"],
                                                   "c": w["c_2"], "pool_scale": w["ev_pool_scale_2"]}),
                                   (VEC_B, vec_b, {"ada_b": w["ada_b_2"], "lnb_2": w["ln_b_2"]})):
            for name, src in names.items():
                r0, n = table[name]
                flat = src.rearrange("a b c -> (a b c)") if len(src.shape) == 3 else src.rearrange("a b -> (a b)")
                act.dma_start(tile[r0:r0 + n, :], flat.rearrange("(k p) -> k p", p=P)).then_inc(vec_in, 16)
        act.dma_start(mem_tok, w["mem"][0].rearrange("(b p) d -> p b d", p=P)).then_inc(mem_in, 16)
        act.dma_start(region(A_PHASE, C_PHASE), w["consts"][:, C_COMMON:C_COMMON + C_PHASE]).then_inc(phase_in, 16)
        for dst, src in ((lam_rows, w["da_lambda"][0].rearrange("a b -> (a b)")), (sink, w["ev_sink_2"][0]),
                         (bias_r1[:, 0:G1], w["b_rg"][0]), (bias_r1[:, G1:G1 + N1], w["b_re"][0])):
            act.dma_start(dst, src.partition_broadcast(P)).then_inc(row_in, 16)
        for dst, src in ((router[0][:, :, 0:G1], w["w_rg"][0]), (router[0][:, :, G1:], w["w_re"][0]),
                         (router[1], w["moe_w_router_2"][0])):
            act.dma_start(dst, src.rearrange("(k p) e -> p k e", p=P)).then_inc(router_in, 16)

        def copy(out_, s, view, scale=1.0):
            b = full(s)
            act.activation(out_, view(b), ACT.Copy, scale=scale).then_inc(bank_free[b], 1)

        as_blocks = lambda b: bank(b, 2, T)

        def walk(plan):
            for s in plan:
                kind, a, i = s
                if kind == "vec":
                    n = vec_rows[a]
                    copy((cols_a, cols_b)[a][:, 0:n], s, lambda b: psum[:, b, 0:n])
                    if a == 0:
                        evacuated(s)
                        act.activation(cond, cols_a[:, VEC_A["c"][0]:VEC_A["c"][0] + KT], ACT.Silu).then_inc(cond_set, 1)
                    else:
                        act.wait_ge(lam_summed, 1)
                        act.activation(lam_exp, lam_sum, ACT.Exp).then_inc(lam_exped, 1)
                elif kind == "turn_x":
                    copy(xT[:, 2 * a:2 * a + 2, :], s, as_blocks)
                elif kind == "turn_mem":
                    copy(memT[:, 2 * a:2 * a + 2, :], s, as_blocks)
                elif kind == "gemm" and a in ("da_v", "r_v", "m_v"):
                    if a == "r_v":
                        act.wait_ge(job_done, done[("turn_mem", 3, 0)])
                    dst = {"da_v": dav, "r_v": rv, "m_v": mv}[a]
                    copy(dst[:, i % 2, i // 2 * PANEL:(i // 2 + 1) * PANEL], s, bank)
                elif kind == "gemm" and a in ("da_q", "da_k", "m_q", "m_k", "r_q", "r_k"):
                    dst = {"da_q": daq, "da_k": dak, "m_q": mq, "m_k": mk, "r_q": rq, "r_k": rk}[a]
                    scale = {"da_q": (D // (2 * DA_H)) ** -0.5, "m_q": (D // MEM_H) ** -0.5}.get(a, 1.0)
                    copy(dst[:, 2 * i:2 * i + 2, :], s, as_blocks, scale)
                elif kind == "gemm" and a == "r_g":
                    b = full(s)
                    act.activation(rg[:, 2 * i:2 * i + 2, :], bank(b, 2, T), ACT.Silu).then_inc(bank_free[b], 1)
                elif kind == "gemm" and a.startswith("gate"):
                    n = int(a[-1])
                    if n:
                        evacuated(("gemm", f"branch{n - 1}", i))
                    b = full(s)
                    for k in range(2):
                        ins = act.activation(gate[:, 2 * i + k, :], bank(b, 2, T)[:, k, :], ACT.Sigmoid,
                                             bias=col_a("b_gate", n * KT + 2 * i + k))
                    ins.then_inc(bank_free[b], 1)
                elif kind == "da_score":
                    u = 2 * a + i
                    act.wait_ge(da_logits, u + 1)
                    if u:
                        act.wait_ge(da_probs, u)
                    for c in range(2):
                        ins = act.activation(e_prob[:, c, :], logit[:, c, :], ACT.Exp, bias=dmax[:, c:c + 1],
                                             accum_out=dsum[:, c:c + 1])
                    ins.then_inc(da_exped, 1)
                elif kind == "da_turn":
                    copy(a_turn, s, as_blocks)
                elif kind == "da_out":
                    b = full(s)
                    if a:
                        act.wait_ge(job_done, done[("da_norm", a - 1, 0)])
                    act.activation(osq, psum[:, b, 0:T], ACT.Square).then_inc(da_squared, 1)
                elif kind == "da_norm":
                    b = full(s)
                    if a:
                        evacuated(("da_out", a - 1, 0))
                    act.activation(rstd, psum[:, b, 0:T], ACT.Sqrt, bias=eps, scale=1.0 / P).then_inc(bank_free[b], 1)
                elif kind == "ret_out":
                    if a:
                        act.wait_ge(ret_y, a)
                    copy(ret_o, s, as_blocks)
                elif kind == "ret_mean":
                    act.wait_ge(ret_centred, a + 1)
                    act.activation(ret_sq, ret_o, ACT.Square).then_inc(ret_squared, 1)
                elif kind == "ret_var":
                    b = full(s)
                    act.activation(ret_stat, psum[:, b, 0:T], ACT.Sqrt, bias=eps, scale=1.0 / 256)\
                       .then_inc(bank_free[b], 1)
                    act.wait_ge(ret_normed, a + 1)
                    for k in range(2):
                        n = 2 * a + k
                        ins = act.activation(ret_o[:, k, :], ret_o[:, k, :], ACT.Identity, bias=col_a("gn_b", n),
                                             scale=col_a("gn_g", n))
                    ins.then_inc(ret_scaled, 1)
                elif kind == "mem_score":
                    b = full(s)
                    act.wait_ge(mem_max, a + 1)
                    if a:
                        act.wait_ge(mem_probs, a)
                    for c in range(TB):
                        ins = act.activation(e_prob[:, c, :], bank(b, 2, T)[:, c, :], ACT.Exp, bias=dmax[:, c:c + 1],
                                             accum_out=dsum[:, c:c + 1])
                    ins.then_inc(bank_free[b], 1)
                elif kind == "mem_turn":
                    copy(a_turn, s, as_blocks)
                elif kind == "mem_out":
                    copy(ymem[:, 2 * a:2 * a + 2, :], s, as_blocks)
                elif kind == "turn_tok":
                    copy(tok[:, i // 2, i % 2 * PANEL:(i % 2 + 1) * PANEL], s, bank)
                    if a == 0 and i == 3:
                        later_loads()
                elif kind == "logits":
                    for n in range(2 - a):
                        act.wait_ge(route_diff, 2 * a + n + 1)
                        t = ex_g if (a, n) == (0, 0) else ratio
                        act.activation(t, t, ACT.Exp).then_inc(route_exp, 1)
                elif kind == "gemm" and a == "ev_p":
                    copy(p_tok[:, i, :], s, bank)
                elif kind == "gemm" and a == "ev_q":
                    copy(q2[:, 2 * i:2 * i + 2, :], s, as_blocks, GQA_D ** -0.5)
                elif kind == "ev_k":
                    b = full(s)
                    for g in range(GQA_KV):
                        for half in range(2):
                            ins = act.activation(k2[64 * half:64 * half + 64, g, :], psum[64 * g:64 * g + 64, b, 0:T],
                                                 ACT.Copy)
                    ins.then_inc(bank_free[b], 1)
                elif kind == "ev_v":
                    copy(v2, s, lambda b: psum[:, b, 0:T].rearrange("p (t c) -> p t c", c=P))
                elif kind == "pool":
                    copy(pooled[:, 2 * a:2 * a + 2, :], s, as_blocks)
                elif kind == "pool_map":
                    b = full(s)
                    for k in range(2):
                        ins = act.activation(mix[:, 2 * a + k, :], bank(b, 2, T)[:, k, :], ACT.Identity,
                                             scale=col_a("pool_scale", 2 * a + k))
                    ins.then_inc(bank_free[b], 1)
                elif kind == "gqa_score":
                    act.wait_ge(gqa_logits, a + 1)
                    if a:
                        act.wait_ge(gqa_probs, a)
                    for t in range(TB):
                        act.activation(e2[:, t, :], logit2[:, t, :], ACT.Exp, bias=dmax[:, t:t + 1],
                                       accum_out=dsum[:, t:t + 1])
                    act.activation(esink, dmax, ACT.Exp, bias=sink[:, a:a + 1]).then_inc(gqa_exped, 1)
                elif kind == "gqa_turn":
                    copy(at2, s, as_blocks)
                elif kind == "gqa_out":
                    p0 = 64 * (a % 2)
                    copy(mix[p0:p0 + 64, 4 + a // 2, :], s, lambda b: psum[p0:p0 + 64, b, 0:T])
                elif kind == "turn_ws":
                    copy(ws_t[:, 4 * a:4 * a + 4, :], s, lambda b: bank(b, 4, P))
                elif kind == "gemm" and a in ("od_u", "od_v"):
                    b = full(s)
                    if a == "od_u":
                        act.activation(mix[:, 2 * i:2 * i + 2, :], bank(b, 2, T), ACT.Gelu_apprx_tanh)\
                           .then_inc(bank_free[b], 1)
                    else:
                        act.activation(v_tok[:, i % 2, i // 2 * PANEL:(i // 2 + 1) * PANEL], bank(b),
                                       ACT.Gelu_apprx_tanh).then_inc(bank_free[b], 1)
                        if i == 3:
                            act.wait_ge(v_normed, 1)
                            act.activation(bn_a[:, :, 1:2], bn_a[:, :, 1:2], ACT.Sqrt, bias=eps).then_inc(v_normed, 1)
                elif kind == "turn_out":
                    copy(out_tok[:, a // 2, a % 2 * PANEL:(a % 2 + 1) * PANEL], s, bank)
                elif kind == "ln_sum":
                    sq = ("ln_sq", a, 0)
                    gain_bias = ((lambda k: (col_a("ln1_g", k), col_a("ln1_b", k))),
                                 (lambda k: (col_a("ln2_g", k), col_a("ln2_b", k))),
                                 *((lambda k, n=n: (col_a("lng_2", 8 * n + k), col_b("lnb_2", 8 * n + k)))
                                   for n in range(4)))[a]
                    src, squares = (z, z_sq) if a == 0 else (acc, later_sq)
                    layer_norm_scalar(act, a, src, squares, done[sq], job_bank(sq), bank_free[job_bank(sq)], gain_bias, acc)
                    if 1 <= a <= 4:
                        layer, part = (a - 1) // 2, 3 * ((a - 1) % 2)
                        act.wait_ge(modp1_set, 1)
                        for k in range(KT):
                            act.wait_ge(ln_out, KT * a + k + 1)
                            act.activation(hT[:, k, :], acc[:, k, :], ACT.Identity, bias=mod_cols(mod, layer, part, k),
                                           scale=mod_cols(modp1, layer, part + 1, k)).then_inc(modulated, 1)

        def later_loads():
            act.wait_ge(da_probs, 2 * DA_H)
            act.wait_ge(ret_y, RET_H)
            act.dma_start(region(A_PHASE, C_PHASE), w["consts"][:, C_COMMON + C_PHASE:]).then_inc(small_in, 16)

        def pool_loads():
            act.dma_start(w_pool, w["ev_pool_w_2"][0].rearrange("g c d -> c g d")).then_inc(small_in, 16)

        def gate_loads():
            act.dma_start(w_s, w["od_w_s_2"][0].rearrange("g t s -> t g s")).then_inc(small_in, 16)
            for dst, src in ((sg_rows[:, 0, :], w["od_sg_ln_g_2"][0]), (sg_rows[:, 1, :], w["od_sg_ln_b_2"][0]),
                             (bs_rows.rearrange("p g t -> p (g t)"), w["od_b_s_2"][0].rearrange("g t -> (g t)"))):
                act.dma_start(dst, src.partition_broadcast(P)).then_inc(small_in, 16)

        def unit(f):
            pairs, pos, count = f["pairs"], f["pos"], f["count"]
            make, split = h_point(f)

            def split_chunk(q, jobs, c0, u):
                _, side, p, c = q
                n = count[q]
                if c == 0:
                    k = panel_order(f).index((side, p))
                    act.wait_ge(slot_full[k % FF_SLOTS], at_unit(u, 16 * len(pairs), 16 * (f["base"][k % FF_SLOTS] + k // FF_SLOTS + 1)))
                if n >= STAGES:
                    act.wait_ge(job_done, jobs + pos[f["order"][n - STAGES]])
                elif f["n"] > 1:
                    act.wait_ge(job_done, jobs + (pos[f["order"][n - STAGES]] - f["jobs"]))
                act.activation(chunk_view(stage_hi, f, side, p, c), chunk_source(f, side, p, c), ACT.Copy)\
                   .then_inc(chunk_hi, 1)

            def of_unit(u):
                jobs, c0, p0 = (at_unit(u, f["jobs"], f["at"]), at_unit(u, f["chunks"], f["c0"]),
                                at_unit(u, len(pairs), f["p0"]))

                def body(width):
                    nt = width // P
                    for q in f["order"]:
                        split_chunk(q, jobs, c0, u)
                        n = count[q]
                        if n == STAGES - 1:
                            for i in range(4):
                                if f["routed"]:
                                    act.wait_ge(job_done, jobs + pos[("gather", i)])
                                    src = bank(i, 2, T)[:, :, 0:width]
                                else:
                                    src = hT[:, 2 * i:2 * i + 2, :]
                                act.activation(x_hi[:, 2 * i:2 * i + 2, 0:width], src, ACT.Copy).then_inc(x_hi_set, 1)
                        if q in make:
                            p = make[q]
                            act.wait_ge(job_done, jobs + pos[("chunk", "U", p, 3)])
                            act.wait_ge(h_set, p0 + p)
                            g0 = 4 if width == T else 4 + p % 2
                            act.activation(s_tile[:, 0:nt, 0:pairs[p]], psum[:, g0:g0 + nt, 0:pairs[p]], ACT.Silu)\
                               .then_inc(silu_set, 1)
                        if q in split:
                            p = split[q]
                            act.wait_ge(job_done, jobs + pos[("turn", p)])
                            t0, blocks = (6 if width == T else 7), pairs[p] // P
                            for t in range(nt):
                                ins = act.activation(h_hi[:, 0:blocks, t * P:(t + 1) * P],
                                                     bank(t0 + t, 4, P)[:, 0:blocks, :], ACT.Copy)
                            ins.then_inc(h_hi_set, 1)
                    act.wait_ge(job_done, jobs + pos[f["order"][-1]])
                    for t in range(nt):
                        ins = act.activation(y_tok[:, t, :].rearrange("p (a b) -> p a b", a=2),
                                             psum[:, 2 * t:2 * t + 2, :], ACT.Copy)
                    ins.then_inc(y_copied, 1)

                return body

            return of_unit

        for n in range(3):
            if n == 1:
                pool_loads()
            elif n == 2:
                gate_loads()
            walk(plans[n])
            act.wait_ge(job_done, plan_end[n])
            act.wait_ge(ada_summed, 24)
            if feeds[n]["routed"]:
                evacuated(("rank", n // 2, 0))
            else:
                act.wait_ge(modulated, 2 * KT)
            units(act, feeds[n], unit(feeds[n]))
        walk(plans[3])

    @block.vector
    def _(dve):
        step = [0]

        def settle(ins):
            step[0] += 1
            ins.then_inc(dve_step, 1)
            dve.wait_ge(dve_step, step[0])

        def full(s):
            dve.wait_ge(job_done, done[s])
            return job_bank(s)

        def evacuated(s):
            dve.wait_ge(*bank_through(s))

        dve.wait_ge(row_in, 4 * 16)
        lam4 = lam_rows.rearrange("p (a b) -> p a b", b=64)
        settle(dve.tensor_tensor(lam_prod, lam4[:, 0:4:2, :], lam4[:, 1:4:2, :], ALU.mult))
        dve.tensor_reduce(lam_sum, lam_prod, AX.X, ALU.add).then_inc(lam_summed, 1)
        dve.wait_ge(lam_exped, 1)
        settle(dve.tensor_tensor(neg_lam, lam_exp[:, 1:2], lam_exp[:, 0:1], ALU.subtract))
        settle(dve.tensor_scalar(neg_lam, neg_lam, -LAMBDA_INIT, None, ALU.add))
        evacuated(("vec", 0, 0))
        settle(dve.tensor_scalar(da_gain, col_a("da_g"), 1.0 - LAMBDA_INIT, None, ALU.mult))
        dve.wait_ge(const_in, 16)
        dve.wait_ge(phase_in, 16)
        def sum_modulation(n):
            layer, p = n // 12, n % 12
            at, fill = panel[("ada", layer, p)]
            dve.wait_ge(slot_full[at], 16 * fill)
            if n >= 2:
                dve.wait_ge(job_done, done[("ada", (n - 2) // 12, (n - 2) % 12)])
            tile, wt = ada_sum[:, n % 2, :], slot(at, KT)
            settle(dve.tensor_scalar(tile, wt[:, 0, :], cond[:, 0:1], None, ALU.mult))
            for k in range(1, KT):
                ins = dve.scalar_tensor_tensor(tile, wt[:, k, :], cond[:, k:k + 1], tile, ALU.mult, ALU.add)
                if k < KT - 1:
                    settle(ins)
            ins.then_inc(ada_summed, 1)

        def add_modulation_bias(s):
            b = full(s)
            at = s[1] * 48 + s[2] * 4
            c = VEC_B["ada_b"][0] + at
            dve.tensor_tensor(mod[:, at:at + 4], psum[:, b, 0:4], cols_b[:, c:c + 4], ALU.add)\
               .then_inc(bank_free[b], 1)

        def settled_max_one_hot(values, out_, n, m):
            settle(dve.tensor_reduce(m, values, AX.X, ALU.max))
            settle(dve.tensor_tensor(top_e[:, :, 0:n], values, along(m, n), ALU.is_equal))
            settle(dve.tensor_tensor(top_e[:, :, 0:n], top_e[:, :, 0:n], over(desc[:, 0:n], TB), ALU.mult))
            settle(dve.tensor_reduce(peak, top_e[:, :, 0:n], AX.X, ALU.max))
            settle(dve.tensor_tensor(out_, top_e[:, :, 0:n], along(peak, n), ALU.is_equal))

        def top_two(values, n, told):
            settled_max_one_hot(values, top_1[:, :, 0:n], n, peak_1)
            settle(dve.scalar_tensor_tensor(top_v[:, :, 0:n], top_1[:, :, 0:n], -1e38, values, ALU.mult, ALU.add))
            settled_max_one_hot(top_v[:, :, 0:n], top_2[:, :, 0:n], n, peak_2)
            dve.tensor_tensor(ratio, peak_2, peak_1, ALU.subtract).then_inc(route_diff, 1)
            dve.wait_ge(route_exp, told)
            settle(dve.tensor_scalar(wt_2, ratio, 1.0, None, ALU.add))
            settle(dve.reciprocal(wt_1, wt_2))
            settle(dve.tensor_tensor(wt_2, wt_1, ratio, ALU.mult))

        def routing(m, b, s):
            n = (N1, N2)[m]
            settle(dve.memset(region(R_TAIL + 320, 96), 0.0))
            settle(dve.tensor_scalar(desc, iota[:, 0:N1], -1.0, float(N1), ALU.mult, ALU.add))
            logits = psum[:, b, 0:TB * (G1 + N1 if m == 0 else N2)].rearrange("p (t e) -> p t e", t=TB)
            if m == 0:
                dve.tensor_tensor(lg, logits, over(bias_r1, TB), ALU.add).then_inc(bank_free[b], 1)
                evacuated(s)
                group, each = lg[:, :, 0:G1], lg[:, :, G1:].rearrange("p t (g e) -> p t g e", e=E1)
                settled_max_one_hot(group, hot_g, G1, peak_1)
                dve.tensor_tensor(ex_g, group, along(peak_1, G1), ALU.subtract).then_inc(route_diff, 1)
                dve.wait_ge(route_exp, 1)
                settle(dve.tensor_reduce(p_top, ex_g, AX.X, ALU.add))
                settle(dve.reciprocal(p_top, p_top))
                hot4 = hot_g.unsqueeze(3).to_broadcast([P, TB, G1, E1])
                four = lambda v: v.rearrange("p t (g e) -> p t g e", e=E1)
                for t in range(TB):
                    settle(dve.tensor_tensor(four(top_v)[:, t], each[:, t], hot4[:, t], ALU.mult))
                    settle(dve.tensor_reduce(sel[:, t, 0:E1], top_v[:, t, :].rearrange("p (g e) -> p e g", e=E1),
                                             AX.X, ALU.add))
                top_two(sel[:, :, 0:E1], E1, 2)
                settle(dve.tensor_tensor(wt_1, wt_1, p_top, ALU.mult))
                settle(dve.tensor_tensor(wt_2, wt_2, p_top, ALU.mult))
            else:
                dve.tensor_copy(lg[:, :, 0:n], logits).then_inc(bank_free[b], 1)
                evacuated(s)
                top_two(lg[:, :, 0:n], n, 3)
            k = E1 if m == 0 else n
            one, two = top_1[:, :, 0:k], top_2[:, :, 0:k]
            w_k, m_k = sel[:, :, 0:k], table[:, TB:2 * TB, 0:k]
            if m == 1:
                settle(dve.tensor_tensor(m_k, one, two, ALU.add))
            else:
                settle(dve.tensor_copy(table[:, TB:2 * TB, 0:G1], hot_g))
            settle(dve.tensor_tensor(one, one, along(wt_1, k), ALU.mult))
            settle(dve.tensor_tensor(two, two, along(wt_2, k), ALU.mult))
            if m == 1:
                dve.tensor_tensor(weights[:, :, 0:k], one, two, ALU.add).then_inc(masks_set, 1)
            else:
                settle(dve.tensor_tensor(w_k, one, two, ALU.add))
                for t in range(TB):
                    ins = dve.tensor_tensor(weights[:, t, 0:n].rearrange("p (g e) -> p g e", e=E1),
                                            along(hot_g[:, t, :], E1), over(w_k[:, t, :], G1), ALU.mult)
                ins.then_inc(masks_set, 1)

        def add_to_result(i, gain, settled):
            if gain is None:
                dve.tensor_tensor(acc[:, 2 * i:2 * i + 2, :], bank(i, 2, T), acc[:, 2 * i:2 * i + 2, :],
                                  ALU.add).then_inc(settled, 1)
                return
            for k in range(2):
                ins = dve.scalar_tensor_tensor(acc[:, 2 * i + k, :], bank(i, 2, T)[:, k, :],
                                               mod_cols(modp1, *gain, 2 * i + k), acc[:, 2 * i + k, :],
                                               ALU.mult, ALU.add)
            ins.then_inc(settled, 1)

        owed = []

        def walk(plan):
            for s in plan:
                kind, a, i = s
                if owed and index[s] >= index[owed[0]] + 2:
                    add_modulation_bias(owed.pop())
                if kind == "da_score":
                    u = 2 * a + i
                    b = full(s)
                    if u:
                        dve.wait_ge(da_exped, u)
                    dve.scalar_tensor_tensor(logit, causal, 2.0 ** -(a + 1), bank(b, 2, T), ALU.mult,
                                             ALU.add).then_inc(bank_free[b], 1)
                    evacuated(s)
                    dve.tensor_reduce(dmax, logit, AX.X, ALU.max, negate=True).then_inc(da_logits, 1)
                    dve.wait_ge(da_exped, u + 1)
                    settle(dve.reciprocal(drec, dsum))
                    if i == 0:
                        if a:
                            dve.wait_ge(job_done, done[("da_turn", a - 1, 0)])
                        dve.tensor_tensor(a_prob, e_prob, along(drec, T), ALU.mult).then_inc(da_probs, 1)
                    else:
                        settle(dve.tensor_scalar(drec, drec, neg_lam, None, ALU.mult))
                        settle(dve.tensor_tensor(e_prob, e_prob, along(drec, T), ALU.mult))
                        dve.wait_ge(da_probs, u)
                        dve.tensor_tensor(a_prob, a_prob, e_prob, ALU.add).then_inc(da_probs, 1)
                elif kind == "da_norm":
                    evacuated(s)
                    settle(dve.reciprocal(rstd, rstd))
                    bo = job_bank(("da_out", a, 0))
                    dve.scalar_tensor_tensor(yda[:, a, :], psum[:, bo, 0:T], da_gain, rstd, ALU.mult,
                                             ALU.mult).then_inc(bank_free[bo], 1)
                elif kind == "ret_score":
                    b = full(s)
                    if a:
                        dve.wait_ge(job_done, done[("ret_out", a - 1, 0)])
                    dve.tensor_tensor(ret_s, bank(b, 2, T), decay[:, 2 * a:2 * a + 2, :], ALU.mult).then_inc(bank_free[b], 1)
                elif kind == "ret_mean":
                    b = full(s)
                    dve.tensor_scalar(ret_stat, psum[:, b, 0:T], 1.0 / 256, None, ALU.mult).then_inc(bank_free[b], 1)
                    evacuated(s)
                    evacuated(("ret_out", a, 0))
                    dve.tensor_tensor(ret_o, ret_o, over(ret_stat, 2), ALU.subtract).then_inc(ret_centred, 1)
                elif kind == "ret_var":
                    evacuated(s)
                    settle(dve.reciprocal(ret_stat, ret_stat))
                    dve.tensor_tensor(ret_o, ret_o, over(ret_stat, 2), ALU.mult).then_inc(ret_normed, 1)
                    dve.wait_ge(ret_scaled, a + 1)
                    for k in range(1):
                        evacuated(("gemm", "r_g", a))
                        dve.tensor_tensor(yret[:, 2 * a:2 * a + 2, :], ret_o, rg[:, 2 * a:2 * a + 2, :],
                                          ALU.mult).then_inc(ret_y, 1)
                elif kind == "mem_score":
                    b = full(s)
                    dve.tensor_reduce(dmax, bank(b, 2, T), AX.X, ALU.max, negate=True).then_inc(mem_max, 1)
                    evacuated(s)
                    settle(dve.reciprocal(drec, dsum))
                    if a:
                        dve.wait_ge(job_done, done[("mem_turn", a - 1, 0)])
                    dve.tensor_tensor(a_prob, e_prob, along(drec, T), ALU.mult).then_inc(mem_probs, 1)
                elif kind == "gemm" and a.startswith("branch"):
                    n = int(a[-1])
                    b = full(s)
                    evacuated(("gemm", f"gate{n}", i))
                    mg = merged[:, 2 * i:2 * i + 2, :]
                    gt = gate[:, 2 * i:2 * i + 2, :]
                    if n == 0:
                        dve.tensor_tensor(mg, gt, bank(b, 2, T), ALU.mult).then_inc(bank_free[b], 1)
                    else:
                        dve.tensor_tensor(gtmp, gt, bank(b, 2, T), ALU.mult).then_inc(bank_free[b], 1)
                        evacuated(s)
                        evacuated(("gemm", f"branch{n - 1}", i))
                        settle(dve.tensor_tensor(mg, mg, gtmp, ALU.add))
                        if n == 2 and i == 3:
                            dve.sem_inc(merged_set, 1)
                elif kind == "gemm" and a == "w_o":
                    b = full(s)
                    dve.scalar_tensor_tensor(z[:, 2 * i:2 * i + 2, :], xT[:, 2 * i:2 * i + 2, :], ALPHA1, bank(b, 2, T),
                                             ALU.mult, ALU.add).then_inc(bank_free[b], 1)
                elif kind == "ada":
                    owed.append(s)
                    n = 12 * a + i + 1
                    if n < 24:
                        sum_modulation(n)
                    else:
                        add_modulation_bias(owed.pop())
                        evacuated(s)
                        evacuated(("ada", 1, 10))
                        dve.tensor_scalar(modp1, mod, 1.0, None, ALU.add).then_inc(modp1_set, 1)
                elif kind == "gemm" and a in ("ev_o", "od_o"):
                    b = full(s)
                    dve.wait_ge(acc_scaled, 2 if a == "ev_o" else 4)
                    for k in range(2):
                        n = 2 * i + k
                        ins = dve.scalar_tensor_tensor(acc[:, n, :], bank(b, 2, T)[:, k, :],
                                                       mod_cols(modp1, 0 if a == "ev_o" else 1, 2, n), acc[:, n, :],
                                                       ALU.mult, ALU.add)
                    ins.then_inc(bank_free[b], 1)
                elif kind == "gqa_score":
                    b = full(s)
                    if a == 0:
                        dve.wait_ge(small_in, 2 * 16)
                    if a:
                        dve.wait_ge(gqa_exped, a)
                    dve.scalar_tensor_tensor(logit2, wbias, 2.0 ** -(a + 1), bank(b, 2, T), ALU.mult,
                                             ALU.add).then_inc(bank_free[b], 1)
                    evacuated(s)
                    settle(dve.tensor_reduce(dmax, logit2, AX.X, ALU.max))
                    dve.tensor_scalar(dmax, dmax, sink[:, a:a + 1], -1.0, ALU.max, ALU.mult).then_inc(gqa_logits, 1)
                    dve.wait_ge(gqa_exped, a + 1)
                    settle(dve.tensor_tensor(dsum, dsum, esink, ALU.add))
                    settle(dve.reciprocal(drec, dsum))
                    if a:
                        dve.wait_ge(job_done, done[("gqa_turn", a - 1, 0)])
                    dve.tensor_tensor(a2, e2, along(drec, T), ALU.mult).then_inc(gqa_probs, 1)
                elif s == ("gemm", "od_v", 3):
                    dve.wait_ge(small_in, 6 * 16)
                    for n in range(4):
                        evacuated(("gemm", "od_v", n))
                    for t in range(TB):
                        for c in range(2):
                            settle(dve.bn_stats(bn_s[:, t, 6 * c:6 * c + 6], v_tok[:, t, c * 512:(c + 1) * 512]))
                        ins = dve.bn_aggr(bn_a[:, t, :], bn_s[:, t, 0:12])
                        if t == 0:
                            settle(ins)
                    ins.then_inc(v_normed, 1)
                    dve.wait_ge(v_normed, 2)
                    settle(dve.reciprocal(bn_a[:, :, 1:2], bn_a[:, :, 1:2]))
                    for t in range(TB):
                        settle(dve.tensor_scalar(v_tok[:, t, :], v_tok[:, t, :], bn_a[:, t, 0:1], bn_a[:, t, 1:2],
                                                 ALU.subtract, ALU.mult))
                    settle(dve.tensor_tensor(v_tok, v_tok, over(sg_rows[:, 0, :], TB), ALU.mult))
                    dve.tensor_tensor(v_tok, v_tok, over(sg_rows[:, 1, :], TB), ALU.add).then_inc(v_normed, 1)
                elif kind == "gate_s":
                    b = full(s)
                    evacuated(("gemm", "od_u", a))
                    for k in range(2):
                        ins = dve.tensor_tensor(e2[:, k, :].rearrange("p (c t) -> p c t", t=P), bank(b, 4, P)[:, 2 * k:2 * k + 2, :],
                                                over(bs_rows[:, 2 * a + k, :], 2), ALU.add)
                    ins.then_inc(bank_free[b], 1)
                    evacuated(s)
                    dve.tensor_tensor(mix[:, 2 * a:2 * a + 2, :], mix[:, 2 * a:2 * a + 2, :], e2,
                                      ALU.mult).then_inc(sg_gated, 1)
                    dve.wait_ge(sg_gated, a + 1)
                elif kind == "logits":
                    routing(a, full(s), s)
                elif kind == "turn_tok" and i == 3:
                    if a == 0:
                        dve.wait_ge(job_done, done[s])
                        dve.tensor_scalar(acc, acc, ALPHA1, None, ALU.mult).then_inc(acc_scaled, 1)
                elif kind == "rank":
                    b = full(s)
                    n = (G1, N2)[a]
                    settle(dve.tensor_copy(table[:, 0:2, 0:n], psum[:, b, 0:2 * n].rearrange("p (t e) -> p t e", e=n)))
                    dve.tensor_copy(counts_i[:, 0:n], psum[:, b, 2 * n:3 * n]).then_inc(bank_free[b], 1)
                elif kind == "ln_sum":
                    if a == 0:
                        for k in range(4):
                            evacuated(("gemm", "w_o", k))
                    src = z if a == 0 else acc
                    layer_norm_vector(dve, settle, a, src, done[s], job_bank(s), bank_through(s),
                                      bank_through(("ln_sq", a, 0)))
                    if 1 <= a <= 4:
                        dve.wait_ge(modulated, KT * a)
                        dve.tensor_scalar(acc, acc, ALPHA2, None, ALU.mult).then_inc(acc_scaled, 1)
                        dve.wait_ge(acc_scaled, a + 1)

        def own_tokens(f, u):
            k = f["weights"]
            dve.tensor_copy(mine.unsqueeze(2), table[:, :, bass.ds(u, 1)]).then_inc(mine_set, 1)
            dve.tensor_copy(mine_w[:, :, 0:k], weights[:, :, bass.ds(u * k, k)]).then_inc(mine_set, 1)
            dve.wait_ge(mine_set, u * 2 + 2 * (f["r0"] + (f["u0"] > 0) + 1))
            for t in range(TB):
                ins = dve.tensor_scalar(perm[:, t, :], iota, mine[:, t:t + 1], mine[:, TB + t:TB + t + 1],
                                        ALU.is_equal, ALU.mult)
            ins.then_inc(perm_set, 1)

        def unit(f):
            pairs, pos, count = f["pairs"], f["pos"], f["count"]
            make, split = h_point(f)

            def of_unit(u):
                jobs, c0, p0 = (at_unit(u, f["jobs"], f["at"]), at_unit(u, f["chunks"], f["c0"]),
                                at_unit(u, len(pairs), f["p0"]))

                def body(width):
                    nt = width // P
                    for q in f["order"]:
                        _, side, p, c = q
                        n = count[q]
                        dve.wait_ge(chunk_hi, c0 + (n + 1))
                        dve.tensor_tensor(chunk_view(stage_lo, f, side, p, c), chunk_source(f, side, p, c),
                                          chunk_view(stage_hi, f, side, p, c).bitcast(F32), ALU.subtract)\
                           .then_inc(chunk_lo, 1)
                        if n == STAGES - 1:
                            for i in range(4):
                                dve.wait_ge(x_hi_set, at_unit(u, 4, 4 * f["u0"] + i + 1))
                                src = bank(i, 2, T)[:, :, 0:width] if f["routed"] else hT[:, 2 * i:2 * i + 2, :]
                                dve.tensor_tensor(x_lo[:, 2 * i:2 * i + 2, 0:width], src,
                                                  x_hi[:, 2 * i:2 * i + 2, 0:width].bitcast(F32), ALU.subtract)\
                                   .then_inc(x_lo_set, 1)
                            if f["routed"]:
                                dve.wait_ge(job_done, jobs + pos[("spread",)])
                                dve.tensor_copy(spread[:, 0:nt, :], bank(4, 2, T)[:, 0:nt, :])
                                dve.tensor_copy(own_w[:, 0:nt, 0:f["weights"]],
                                                bank(6, 32, 16)[:, 0:nt, 0:f["weights"]]).then_inc(spread_set, 1)
                        if q in make:
                            p = make[q]
                            dve.wait_ge(silu_set, p0 + (p + 1))
                            if p:
                                dve.wait_ge(job_done, jobs + pos[("turn", p - 1)])
                            elif f["routed"]:
                                dve.wait_ge(spread_set, at_unit(u, 1, f["r0"] + 1))
                            for t in range(nt):
                                s_t, u_t, h_t = (s_tile[:, t, 0:pairs[p]], psum[:, 6 + t, 0:pairs[p]],
                                                 h_tile[:, t, 0:pairs[p]])
                                if f["routed"]:
                                    e = p if f["weights"] > 1 else 0
                                    ins = dve.scalar_tensor_tensor(h_t, s_t, own_w[:, t, e:e + 1], u_t, ALU.mult,
                                                                   ALU.mult)
                                else:
                                    ins = dve.tensor_tensor(h_t, s_t, u_t, ALU.mult)
                            ins.then_inc(h_set, 1)
                            if p == 0 and f["routed"]:
                                dve.wait_ge(perm_set, at_unit(u, 1, f["r0"] + (f["u0"] > 0) + 1))
                                own_tokens(f, u + 1)
                        if q in split:
                            p = split[q]
                            dve.wait_ge(h_hi_set, p0 + (p + 1))
                            t0, blocks = (6 if width == T else 7), pairs[p] // P
                            for t in range(nt):
                                ins = dve.tensor_tensor(h_lo[:, 0:blocks, t * P:(t + 1) * P],
                                                        bank(t0 + t, 4, P)[:, 0:blocks, :],
                                                        h_hi[:, 0:blocks, t * P:(t + 1) * P].bitcast(F32), ALU.subtract)
                            ins.then_inc(h_lo_set, 1)
                    for i in range(4):
                        dve.wait_ge(job_done, jobs + pos[("scatter", i)])
                        if i == 0:
                            dve.wait_ge(added, at_unit(u, 4, 4 * f["u0"]))
                        add_to_result(i, f["gain"], added)

                return body

            return of_unit

        dve.wait_ge(cond_set, 1)
        sum_modulation(0)
        for n in range(3):
            f = feeds[n]
            walk(plans[n])
            dve.wait_ge(acc_scaled, (1, 3, 5)[n])
            if f["routed"]:
                evacuated(("rank", n // 2, 0))
                own_tokens(f, 0)
            units(dve, f, unit(f))
            dve.wait_ge(added, 4 * (f["u0"] + f["n"]))
        walk(plans[3])

    @block.tensor
    def _(pe):
        def open_bank(s):
            n = index[s]
            if n >= BANKS:
                pe.wait_ge(bank_free[n % BANKS], n // BANKS)
            return n % BANKS

        def evacuated(s):
            pe.wait_ge(*bank_through(s))

        def turn4(s, pairs):
            b = open_bank(s)
            for n, (src, col) in enumerate(pairs):
                ins = pe.transpose(psum[0:src.shape[1], b, col:col + src.shape[0]], src,
                                   ident[0:src.shape[0], 0:src.shape[0]])
            ins.then_inc(job_done, 1)

        rhs_of = {"m_k": memT, "m_v": memT, "branch0": yda, "branch1": yret, "branch2": ymem, "w_o": merged,
                  "ev_p": hT, "ev_q": hT, "ev_o": mix, "od_u": hT, "od_v": hT, "od_o": mix}
        pe.wait_ge(const_in, 16)
        pe.wait_ge(ones_set, 2)
        def walk(plan):
            for s in plan:
                kind, a, i = s
                if kind == "vec":
                    pe.wait_ge(vec_in, 16 * 13)
                    rows = (vec_a, vec_b)[a]
                    n = vec_rows[a]
                    b = open_bank(s)
                    pe.transpose(psum[:, b, 0:n], rows[0:n, :], ident[0:n, 0:n]).then_inc(job_done, 1)
                elif kind in ("turn_x", "turn_mem"):
                    pe.wait_ge(*((x_in, 16) if kind == "turn_x" else (mem_in, 16)))
                    src = x_tok if kind == "turn_x" else mem_tok
                    turn4(s, [(src[:, t, (2 * a + k) * P:(2 * a + k + 1) * P], k * T + t * P)
                              for k in range(2) for t in range(TB)])
                elif kind == "gemm":
                    at, fills = panel_of(s)
                    if i == 0:
                        if a == "da_q":
                            for n in range(4):
                                evacuated(("turn_x", n, 0))
                        elif a == "m_k":
                            for n in range(4):
                                evacuated(("turn_mem", n, 0))
                        elif a == "branch0":
                            evacuated(("da_out", DA_H - 1, 0))
                            for n in range(DA_H):
                                evacuated(("da_out", n, 0))
                        elif a == "branch1":
                            pe.wait_ge(ret_y, RET_H)
                        elif a == "branch2":
                            for n in range(MEM_H):
                                evacuated(("mem_out", n, 0))
                        elif a == "w_o":
                            pe.wait_ge(merged_set, 1)
                        elif a == "ev_p":
                            pe.wait_ge(modulated, KT)
                        elif a == "ev_o":
                            evacuated(("pool_map", 0, 0))
                            evacuated(("pool_map", 1, 0))
                            for n in range(GQA_H):
                                evacuated(("gqa_out", n, 0))
                        elif a == "od_v":
                            pe.wait_ge(modulated, 3 * KT)
                        elif a == "od_o":
                            pe.wait_ge(sg_gated, 4)
                    pe.wait_ge(slot_full[at], 16 * fills)
                    rhs = rhs_of.get(a, xT)
                    b = open_bank(s)
                    wt = slot(at, KT)
                    if a in token_major:
                        for k in range(KT):
                            ins = pe.matmul(bank(b), rhs[:, k, i % 2 * P:(i % 2 + 1) * P], wt[:, k, :],
                                            start=(k == 0), stop=(k == KT - 1))
                    else:
                        for m in range(2):
                            c = (i % 2 * 2 + m) * P
                            for k in range(KT):
                                ins = pe.matmul(bank(b, 2, T)[:, m, :], wt[:, k, c:c + P], rhs[:, k, :],
                                                start=(k == 0), stop=(k == KT - 1))
                    ins.then_inc(job_done, 1)
                elif kind == "da_score":
                    b = open_bank(s)
                    if a % 2 == 0 and i == 0:
                        evacuated(("gemm", "da_q", a // 2))
                        evacuated(("gemm", "da_k", a // 2))
                    for t in range(TB):
                        ins = pe.matmul(bank(b, 2, T)[:, t, :], daq[64 * i:64 * i + 64, a, t * P:(t + 1) * P],
                                        dak[64 * i:64 * i + 64, a, :], start=True, stop=True)
                    ins.then_inc(job_done, 1)
                elif kind == "da_turn":
                    pe.wait_ge(da_probs, 2 * a + 2)
                    turn4(s, [(a_prob[:, t, k * P:(k + 1) * P], k * T + t * P) for k in range(2) for t in range(TB)])
                elif kind == "da_out":
                    evacuated(("da_turn", a, 0))
                    if a == 0:
                        for n in range(4):
                            evacuated(("gemm", "da_v", n))
                    b = open_bank(s)
                    for k in range(TB):
                        ins = pe.matmul(psum[:, b, 0:T], dav[:, k, a * P:(a + 1) * P], a_turn[:, k, :], start=(k == 0),
                                        stop=(k == TB - 1))
                    ins.then_inc(job_done, 1)
                elif kind == "da_norm":
                    pe.wait_ge(da_squared, a + 1)
                    b = open_bank(s)
                    pe.matmul(psum[:, b, 0:T], ones, osq, start=True, stop=True).then_inc(job_done, 1)
                elif kind == "ret_score":
                    if a == 0:
                        for n, k in (("r_q", 2), ("r_k", 2), ("r_v", 4)):
                            for m in range(k):
                                evacuated(("gemm", n, m))
                    b = open_bank(s)
                    for k in range(TB):
                        ins = pe.matmul(bank(b, 2, T)[:, k, :], rk[:, a, k * P:(k + 1) * P], rq[:, a, :], start=True,
                                        stop=True)
                    ins.then_inc(job_done, 1)
                elif kind == "ret_out":
                    evacuated(("ret_score", a, 0))
                    b = open_bank(s)
                    for m in range(2):
                        for k in range(TB):
                            c = (2 * a + m) * P
                            ins = pe.matmul(bank(b, 2, T)[:, m, :], rv[:, k, c:c + P], ret_s[:, k, :], start=(k == 0),
                                            stop=(k == TB - 1))
                    ins.then_inc(job_done, 1)
                elif kind in ("ret_mean", "ret_var"):
                    if kind == "ret_mean":
                        evacuated(("ret_out", a, 0))
                    else:
                        pe.wait_ge(ret_squared, a + 1)
                    src = ret_o if kind == "ret_mean" else ret_sq
                    b = open_bank(s)
                    for k in range(2):
                        ins = pe.matmul(psum[:, b, 0:T], ones, src[:, k, :], start=(k == 0), stop=(k == 1))
                    ins.then_inc(job_done, 1)
                elif kind == "mem_score":
                    if a == 0:
                        for n in ("m_q", "m_k"):
                            for m in range(4):
                                evacuated(("gemm", n, m))
                    b = open_bank(s)
                    for t in range(TB):
                        for k in range(2):
                            ins = pe.matmul(bank(b, 2, T)[:, t, :], mq[:, 2 * a + k, t * P:(t + 1) * P],
                                            mk[:, 2 * a + k, :], start=(k == 0), stop=(k == 1))
                    ins.then_inc(job_done, 1)
                elif kind == "mem_turn":
                    pe.wait_ge(mem_probs, a + 1)
                    turn4(s, [(a_prob[:, t, k * P:(k + 1) * P], k * T + t * P) for k in range(2) for t in range(TB)])
                elif kind == "mem_out":
                    evacuated(("mem_turn", a, 0))
                    if a == 0:
                        for n in range(4):
                            evacuated(("gemm", "m_v", n))
                    b = open_bank(s)
                    for m in range(2):
                        for k in range(TB):
                            c = (2 * a + m) * P
                            ins = pe.matmul(bank(b, 2, T)[:, m, :], mv[:, k, c:c + P], a_turn[:, k, :], start=(k == 0),
                                            stop=(k == TB - 1))
                    ins.then_inc(job_done, 1)
                elif kind in ("ln_sum", "ln_sq"):
                    if kind == "ln_sum" and a == 0:
                        for n in range(4):
                            evacuated(("gemm", "w_o", n))
                    elif kind == "ln_sum" and a in (2, 4):
                        for n in range(4):
                            evacuated(("gemm", "ev_o" if a == 2 else "od_o", n))
                    b = open_bank(s)
                    src = (z if a == 0 else acc) if kind == "ln_sum" else (z_sq if a == 0 else later_sq)
                    for k in range(KT):
                        if kind == "ln_sq" and k % 4 == 0:
                            pe.wait_ge(ln_squared, 2 * a + k // 4 + 1)
                        ins = pe.matmul(psum[:, b, 0:T], ones, src[:, k, :], start=(k == 0), stop=(k == KT - 1))
                    ins.then_inc(job_done, 1)
                elif kind == "ada":
                    pe.wait_ge(ada_summed, 12 * a + i + 1)
                    b = open_bank(s)
                    for m in range(4):
                        ins = pe.matmul(psum[:, b, m:m + 1], ada_sum[:, (12 * a + i) % 2, m * P:(m + 1) * P],
                                        ones[:, 0:1], start=True, stop=True)
                    ins.then_inc(job_done, 1)
                elif kind == "logits":
                    if a == 0:
                        pe.wait_ge(router_in, 3 * 16)
                        pe.wait_ge(ln_out, KT)
                    else:
                        pe.wait_ge(modulated, 4 * KT)
                    b = open_bank(s)
                    n = router[a].shape[2]
                    for t in range(TB):
                        for k in range(KT):
                            ins = pe.matmul(psum[:, b, t * n:(t + 1) * n], (acc, hT)[a][:, k, t * P:(t + 1) * P],
                                            router[a][:, k, :], start=(k == 0), stop=(k == KT - 1))
                    ins.then_inc(job_done, 1)
                elif kind == "turn_tok":
                    src, t, k0 = (acc, hT)[a], i // 2, i % 2 * 4
                    turn4(s, [(src[:, k0 + k, t * P:(t + 1) * P], k * P) for k in range(4)])
                elif kind == "turn_out":
                    if a == 0:
                        pe.wait_ge(ln_out, 6 * KT)
                    t, k0 = a // 2, a % 2 * 4
                    turn4(s, [(acc[:, k0 + k, t * P:(t + 1) * P], k * P) for k in range(4)])
                elif kind == "rank":
                    pe.wait_ge(masks_set, a + 1)
                    b = open_bank(s)
                    n = (G1, N2)[a]
                    mask = [table[:, 2 + t, 0:n] for t in range(TB)]
                    for c, terms in enumerate((((ustrict, 0),), ((ustrict, 1), (ones, 0)), ((ones, 0), (ones, 1)))):
                        for k, (lhs, t) in enumerate(terms):
                            ins = pe.matmul(psum[:, b, c * n:(c + 1) * n], lhs, mask[t], start=(k == 0),
                                            stop=(k == len(terms) - 1))
                    ins.then_inc(job_done, 1)
                elif kind in ("ev_k", "ev_v"):
                    at, fill = panel[("ev_k", 0, 0)]
                    pe.wait_ge(slot_full[at], 16 * fill)
                    wt = slot(at, KT, KT * 256)
                    b = open_bank(s)
                    if kind == "ev_k":
                        for k in range(KT):
                            ins = pe.matmul(psum[:, b, 0:T], wt[:, k, 0:P], hT[:, k, :], start=(k == 0),
                                            stop=(k == KT - 1))
                    else:
                        for t in range(TB):
                            for k in range(KT):
                                ins = pe.matmul(psum[:, b, t * P:(t + 1) * P], hT[:, k, t * P:(t + 1) * P],
                                                wt[:, k, P:2 * P], start=(k == 0), stop=(k == KT - 1))
                    ins.then_inc(job_done, 1)
                elif kind in ("pool", "pool_map"):
                    if kind == "pool":
                        pe.wait_ge(small_in, 2 * 16)
                        evacuated(("gemm", "ev_p", 0))
                        evacuated(("gemm", "ev_p", 1))
                    else:
                        evacuated(("pool", a, 0))
                    b = open_bank(s)
                    for m in range(2):
                        g = 2 * a + m
                        if kind == "pool":
                            for t in range(TB):
                                ins = pe.matmul(bank(b, 2, T)[:, m, :], p_tok[:, t, g * P:(g + 1) * P],
                                                pool_m[:, 2 * g + t, :], start=(t == 0), stop=(t == 1))
                        else:
                            ins = pe.matmul(bank(b, 2, T)[:, m, :], w_pool[:, g, :], pooled[:, g, :], start=True,
                                            stop=True)
                    ins.then_inc(job_done, 1)
                elif kind == "gqa_score":
                    if a == 0:
                        for n in (("gemm", "ev_q", 0), ("gemm", "ev_q", 1), ("ev_k", 0, 0)):
                            evacuated(n)
                    b = open_bank(s)
                    p0 = 64 * (a % 2)
                    for t in range(TB):
                        ins = pe.matmul(bank(b, 2, T)[:, t, :], q2[p0:p0 + 64, a // 2, t * P:(t + 1) * P],
                                        k2[p0:p0 + 64, a // 4, :], start=True, stop=True)
                    ins.then_inc(job_done, 1)
                elif kind == "gqa_turn":
                    pe.wait_ge(gqa_probs, a + 1)
                    turn4(s, [(a2[:, t, k * P:(k + 1) * P], k * T + t * P) for k in range(2) for t in range(TB)])
                elif kind == "gqa_out":
                    evacuated(("gqa_turn", a, 0))
                    if a == 0:
                        evacuated(("ev_v", 0, 0))
                    b = open_bank(s)
                    p0, c0 = 64 * (a % 2), 64 * (a // 4)
                    for k in range(TB):
                        ins = pe.matmul(psum[p0:p0 + 64, b, 0:T], v2[:, k, c0:c0 + 64], at2[:, k, :],
                                        start=(k == 0), stop=(k == TB - 1))
                    ins.then_inc(job_done, 1)
                elif kind == "turn_ws":
                    pe.wait_ge(small_in, 6 * 16)
                    turn4(s, [(w_s[:, 4 * a + k, :], k * P) for k in range(4)])
                elif kind == "gate_s":
                    if a == 0:
                        pe.wait_ge(v_normed, 3)
                        evacuated(("turn_ws", 0, 0))
                        evacuated(("turn_ws", 1, 0))
                    b = open_bank(s)
                    for m in range(2):
                        for t in range(TB):
                            g = 2 * a + m
                            ins = pe.matmul(bank(b, 4, P)[:, 2 * m + t, :], v_tok[:, t, g * P:(g + 1) * P],
                                            ws_t[:, g, :], start=True, stop=True)
                    ins.then_inc(job_done, 1)

        def unit(f):
            pairs, pos, count = f["pairs"], f["pos"], f["count"]

            def products(dsts, lhs, rhs, first, last):
                (lhs_hi, lhs_lo), terms = lhs, []
                for n, (dst, (rhs_hi, rhs_lo)) in enumerate(zip(dsts, rhs)):
                    terms += [(dst, lhs_hi, rhs_hi, first, False), (dst, lhs_hi, rhs_lo, False, False)]
                for dst, (rhs_hi, _) in zip(dsts, rhs):
                    terms.append((dst, lhs_lo, rhs_hi, False, last))
                for dst, a, b, start, stop in terms:
                    ins = pe.matmul(dst, a, b, start=start, stop=stop)
                return ins

            def of_unit(u):
                jobs, c0, p0 = (at_unit(u, f["jobs"], f["at"]), at_unit(u, f["chunks"], f["c0"]),
                                at_unit(u, len(pairs), f["p0"]))

                def body(width):
                    nt = width // P
                    if f["routed"]:
                        pe.wait_ge(perm_set, at_unit(u, 1, f["r0"] + (f["u0"] > 0) + 1))
                        pe.wait_ge(added, at_unit(u, 4, 4 * f["u0"]))
                        for i in range(4):
                            for k in range(2):
                                for t in range(TB):
                                    c = (2 * i + k) * P
                                    ins = pe.matmul(bank(i, 2, T)[:, k, 0:width], tok[:, t, c:c + P],
                                                    perm[:, t, 0:width], start=(t == 0), stop=(t == TB - 1))
                            ins.then_inc(job_done, 1)
                        for c in range(nt):
                            for t in range(TB):
                                pe.transpose(bank(4, 2, T)[:, c, t * P:(t + 1) * P], perm[:, t, c * P:(c + 1) * P],
                                             ident)
                        for c in range(nt):
                            for t in range(TB):
                                ins = pe.matmul(bank(6, 32, 16)[:, c, 0:f["weights"]], perm[:, t, c * P:(c + 1) * P],
                                                mine_w[:, t, 0:f["weights"]], start=(t == 0), stop=(t == TB - 1))
                        ins.then_inc(job_done, 1)
                        pe.wait_ge(spread_set, at_unit(u, 1, f["r0"] + 1))
                    pe.wait_ge(x_lo_set, at_unit(u, 4, 4 * f["u0"] + 4))
                    for q in f["steps"]:
                        if q[0] == "chunk":
                            _, side, p, c = q
                            n = count[q]
                            pe.wait_ge(chunk_lo, c0 + (n + 1))
                            hi, lo = chunk_view(stage_hi, f, side, p, c), chunk_view(stage_lo, f, side, p, c)
                            if side == "D":
                                if c == 0:
                                    pe.wait_ge(h_lo_set, p0 + (p + 1))
                                for t in range(nt):
                                    part = slice(t * P, (t + 1) * P)
                                    ins = products([psum[:, 2 * t + m, :] for m in range(2)],
                                                   (h_hi[:, c, part], h_lo[:, c, part]),
                                                   [(hi[:, 0, m * PANEL:(m + 1) * PANEL],
                                                     lo[:, 0, m * PANEL:(m + 1) * PANEL]) for m in range(2)],
                                                   p == 0 and c == 0, p == len(pairs) - 1 and c == pairs[p] // P - 1)
                            else:
                                if c == 0 and p:
                                    alternate = side == "G" and width == P
                                    pe.wait_ge(h_set, p0 + (p - 1 if alternate else p))
                                b0 = 6 if side == "U" else 4 if width == T else 4 + p % 2
                                for k in range(2):
                                    for t in range(nt):
                                        part = slice(t * P, (t + 1) * P)
                                        ins = products([psum[:, b0 + t, 0:pairs[p]]],
                                                       (x_hi[:, 2 * c + k, part], x_lo[:, 2 * c + k, part]),
                                                       [(hi[:, k, :], lo[:, k, :])], c == 0 and k == 0,
                                                       c == 3 and k == 1)
                            ins.then_inc(job_done, 1)
                        elif q[0] == "turn":
                            p = q[1]
                            pe.wait_ge(h_set, p0 + (p + 1))
                            t0 = 6 if width == T else 7
                            for t in range(nt):
                                for j in range(pairs[p] // P):
                                    ins = pe.transpose(bank(t0 + t, 4, P)[:, j, :], h_tile[:, t, j * P:(j + 1) * P], ident)
                            ins.then_inc(job_done, 1)
                        elif q == ("scatter", 0):
                            pe.wait_ge(y_copied, at_unit(u, 1, f["u0"] + 1))
                            for i in range(4):
                                for k in range(2):
                                    c0_ = (2 * i + k) * P
                                    for c in range(nt):
                                        src = y_tok[:, c, c0_:c0_ + P]
                                        if f["routed"]:
                                            ins = pe.matmul(bank(i, 2, T)[:, k, :], src, spread[:, c, :],
                                                            start=(c == 0), stop=(c == nt - 1))
                                        else:
                                            ins = pe.transpose(bank(i, 2, T)[:, k, c * P:(c + 1) * P], src, ident)
                                ins.then_inc(job_done, 1)

                return body

            return of_unit

        for n in range(3):
            walk(plans[n])
            if feeds[n]["routed"]:
                evacuated(("rank", n // 2, 0))
            for s in plans[n][-8:]:
                evacuated(s)
            units(pe, feeds[n], unit(feeds[n]))
            pe.wait_ge(added, 4 * (feeds[n]["u0"] + feeds[n]["n"]))
            pe.wait_ge(h_lo_set, feeds[n]["p0"] + len(feeds[n]["pairs"]) * feeds[n]["n"])
        walk(plans[3])

    ctx.close()


_OUT = (1, T, D)


def kernel(**inputs):
    import concourse.bacc as bacc
    from concourse.bass_utils import run_bass_kernel_spmd

    nc = bacc.Bacc("TRN2", target_bir_lowering=False, num_devices=1)
    arrays, w = {}, {}
    for name, value in {**inputs, "consts": shape_constants()}.items():
        a = np.ascontiguousarray(value)
        arrays[name + "_in"] = a
        w[name] = nc.dram_tensor(name + "_in", a.shape, mybir.dt.from_np(a.dtype), kind="ExternalInput").ap()
    out = nc.dram_tensor("out", (T, D), F32, kind="ExternalOutput").ap()
    build(nc, w, out)
    return run_bass_kernel_spmd(nc, [arrays], core_ids=[0]).results[0]["out"].reshape(_OUT)
```

```python
from contextlib import ExitStack

import numpy as np
import concourse.bass as bass
from concourse import mybir

F32 = mybir.dt.float32
F32R = mybir.dt.float32r
I32 = mybir.dt.int32
ALU = mybir.AluOpType
ACT = mybir.ActivationFunctionType
AX = mybir.AxisListType

P = 128
D = 1024
KT = D // P
T = 256
TB = T // P
PANEL = 512
SLOT = KT * PANEL
SLOTS = 5
FF_SLOTS = 3
STAGES = 6
BANKS = 8
EPS = 1e-5
NEG = -1e30

DA_H, RET_H, MEM_H = 8, 4, 4
LAMBDA_INIT = 0.2
ALPHA1 = 2.0 ** 0.25
ALPHA2 = 4.0 ** 0.25
G1, E1, N1 = 4, 4, 16
N2 = 8
FF1 = 512
assert FF1 == PANEL
FF2 = 3584
FFN = 2816
POOL_W = (2, 4, 8, 16)
GQA_H, GQA_KV, GQA_D = 8, 2, 64
WIN = 128
SG_G = 8

VEC_A = {}
VEC_B = {}
for _table, _rows in ((VEC_A, (("b_gate", 24), ("gn_g", 8), ("gn_b", 8), ("ln1_g", 8), ("ln1_b", 8), ("da_g", 1),
                               ("ln2_g", 8), ("ln2_b", 8), ("lng_2", 32), ("c", 8), ("pool_scale", 4))),
                      (VEC_B, (("ada_b", 96), ("lnb_2", 32)))):
    _at = 0
    for _name, _n in _rows:
        _table[_name] = (_at, _n)
        _at += _n

C_IDENT, C_USTRICT, C_IOTA = 0, 128, 256
C_COMMON = 512
C_PHASE = 2560


def shape_constants():
    out = np.zeros((P, C_COMMON + 2 * C_PHASE), np.float32)
    i = np.arange(P)
    out[:, C_IDENT:C_IDENT + P] = np.eye(P)
    out[:, C_USTRICT:C_USTRICT + P] = i[:, None] < i[None, :]
    out[:, C_IOTA:C_IOTA + T] = np.arange(T)
    t = np.arange(T)
    dist = (t[:, None] - t[None, :]).astype(np.float64)
    causal = np.where(dist >= 0, -dist, NEG)
    window = np.where(np.abs(dist) <= WIN, -np.abs(dist), NEG)
    for b in range(TB):
        out[:, C_COMMON + b * T:C_COMMON + (b + 1) * T] = causal[b * P:(b + 1) * P]
        out[:, C_COMMON + C_PHASE + b * T:C_COMMON + C_PHASE + (b + 1) * T] = window[b * P:(b + 1) * P]
    for h in range(RET_H):
        log_g = np.log(1.0 - 2.0 ** (-5.0 - h))
        m = np.where(dist.T <= 0, 0.0, 0.0)
        m = np.where(dist >= 0, np.exp(np.maximum(dist, 0) * log_g), 0.0).T * (128.0 ** -0.5)
        for b in range(TB):
            at = C_COMMON + 2 * T + (h * TB + b) * T
            out[:, at:at + T] = m[b * P:(b + 1) * P]
    for g, w in enumerate(POOL_W):
        r = w // 2
        lo, hi = np.maximum(t - r, 0), np.minimum(t + r + 1, T)
        m = ((t[:, None] >= lo[None]) & (t[:, None] < hi[None])) / (hi - lo)[None] - np.eye(T)
        for b in range(TB):
            at = C_COMMON + C_PHASE + 2 * T + (g * TB + b) * T
            out[:, at:at + T] = m[b * P:(b + 1) * P]
    return out


def mixer1_steps():
    s = [("turn_x", i, 0) for i in range(4)]
    s += [("gemm", "da_q", i) for i in range(4)] + [("gemm", "da_k", i) for i in range(4)]
    s += [("vec", 0, 0), ("vec", 1, 0)]
    s += [("turn_mem", i, 0) for i in range(4)]
    s += [("gemm", "da_v", i) for i in range(4)]
    fill = [("gemm", n, i) for n, k in (("r_q", 2), ("r_k", 2), ("r_v", 4), ("r_g", 4), ("gate0", 4)) for i in range(k)]
    for h in range(DA_H):
        s += [("da_score", h, 0), ("da_score", h, 1), fill.pop(0)]
        if h:
            s += [("da_norm", h - 1, 0)]
        s += [fill.pop(0), ("da_turn", h, 0)] + ([("ada", 0, h)] if h < DA_H - 1 else []) + [("da_out", h, 0)]
    s += [("ret_score", 0, 0), ("da_norm", DA_H - 1, 0)]
    fill = [("gemm", n, i) for n, k in (("m_q", 4), ("m_k", 4), ("m_v", 4)) for i in range(k)]
    s += [fill.pop(0), fill.pop(0)]
    s += [("gemm", "branch0", i) for i in range(4)] + [("ada", 0, DA_H - 1)]
    for h in range(RET_H):
        if h:
            s += [("ret_score", h, 0), fill.pop(0)]
        s += [("ret_out", h, 0), fill.pop(0), ("ada", 0, DA_H + h), ("ret_mean", h, 0)] + fill[:1] + [("ret_var", h, 0)]
        del fill[:1]
    s += fill
    fill = [("gemm", n, i) for n, k in (("gate1", 4), ("branch1", 4)) for i in range(k)]
    for h in range(MEM_H):
        s += [("mem_score", h, 0), fill.pop(0), ("mem_turn", h, 0), fill.pop(0), ("mem_out", h, 0), ("ada", 1, h)]
    for n in ("gate2", "branch2"):
        for i in range(4):
            s += [("gemm", n, i)] + [("ada", 1, MEM_H + (4 if n == "branch2" else 0) + i)]
    s += [("gemm", "w_o", i) for i in range(4)]
    s += [("ln_sum", 0, 0), ("ln_sq", 0, 0), ("logits", 0, 0)]
    s += [("turn_tok", 0, i) for i in range(4)]
    return s + [("rank", 0, 0)]


def mixer2_steps():
    s = [("ln_sum", 1, 0), ("ln_sq", 1, 0)]
    s += [("gemm", "ev_q", i) for i in range(2)]
    s += [("ev_k", 0, 0), ("ev_v", 0, 0), ("gqa_score", 0, 0), ("gqa_score", 1, 0)]
    fill = [("gemm", "ev_p", 0), ("gemm", "ev_p", 1)] + [(n, i, 0) for n in ("pool", "pool_map") for i in range(2)]
    for h in range(GQA_H):
        s += fill[:1] + [("gqa_turn", h, 0)]
        del fill[:1]
        if h + 2 < GQA_H:
            s += [("gqa_score", h + 2, 0)]
        s += [("gqa_out", h, 0)]
    s += [("gemm", "ev_o", i) for i in range(4)]
    return s + [("ln_sum", 2, 0), ("ln_sq", 2, 0)]


def mixer3_steps():
    s = [("ln_sum", 3, 0), ("ln_sq", 3, 0), ("turn_ws", 0, 0), ("turn_ws", 1, 0)]
    s += [("gemm", "od_v", i) for i in range(4)] + [("gemm", "od_u", i) for i in range(4)]
    s += [("gate_s", i, 0) for i in range(4)]
    s += [("gemm", "od_o", i) for i in range(4)]
    s += [("ln_sum", 4, 0), ("ln_sq", 4, 0), ("logits", 1, 0)]
    s += [("turn_tok", 1, i) for i in range(4)]
    return s + [("rank", 1, 0)]


def last_steps():
    return [("ln_sum", 5, 0), ("ln_sq", 5, 0)] + [("turn_out", i, 0) for i in range(4)]


A_CONST, A_PHASE, A_COLA, A_COLB, A_MOD, A_SMALL = 0, 640, 3200, 3328, 3456, 3584
R_X, R_MEM, R_Q, R_K, R_V, R_TAIL = 4096, 6144, 8192, 10240, 12288, 14336
ARENA = 15744
OVER_SLOTS = 2 * SLOT
M_RQ, M_RK, M_RV, M_RG, M_YDA = (OVER_SLOTS + n for n in (0, 1024, 2048, 4096, 6144))
M_LOGIT, M_E, M_A, M_AT, M_OSQ, M_RSTD, M_RSQ, M_GATE, M_MERGED, M_ADA = (
    OVER_SLOTS + 8192 + n for n in (0, 512, 1024, 1536, 2048, 2304, 2560, 3072, 5120, 7168))
M_MIX, M_WPOOL, M_WS, M_ROWS, M_BIAS = (OVER_SLOTS + n for n in (0, 2048, 2560, 3584, 5632))
OVER = OVER_SLOTS + 16384


def build(nc, w, out):
    ctx = ExitStack()

    def sem(name):
        return ctx.enter_context(nc.semaphore(name))

    ring = ctx.enter_context(nc.sbuf_tensor("ring", [P, FF_SLOTS * SLOT], F32))
    arena = ctx.enter_context(nc.sbuf_tensor("arena", [P, ARENA], F32))
    counts_i = ctx.enter_context(nc.sbuf_tensor("counts_i", [P, N1], I32))
    psum = ctx.enter_context(nc.psum_tensor("psum", [P, BANKS, 512], F32))
    with nc.sbuf_tensor("mixer_tiles", [P, OVER], F32) as over_mixers:
        pass
    stage_hi = ctx.enter_context(nc.sbuf_tensor("stage_hi", [P, STAGES, 1024], F32R))
    stage_lo = ctx.enter_context(nc.sbuf_tensor("stage_lo", [P, STAGES, 1024], F32R))
    x_hi = ctx.enter_context(nc.sbuf_tensor("x_hi", [P, KT, T], F32R))
    x_lo = ctx.enter_context(nc.sbuf_tensor("x_lo", [P, KT, T], F32R))
    h_hi = ctx.enter_context(nc.sbuf_tensor("h_hi", [P, 4, T], F32R))
    h_lo = ctx.enter_context(nc.sbuf_tensor("h_lo", [P, 4, T], F32R))
    y_tok = ctx.enter_context(nc.sbuf_tensor("y_tok", [P, TB, D], F32))

    def region(at, *shape):
        n = int(np.prod(shape))
        v = arena[:, at:at + n]
        if len(shape) == 2:
            return v.rearrange("p (a b) -> p a b", b=shape[1])
        if len(shape) == 3:
            return v.rearrange("p (a b c) -> p a b c", b=shape[1], c=shape[2])
        return v

    def scratch(at, *shape):
        n = int(np.prod(shape))
        v = over_mixers[:, at:at + n]
        return v.rearrange("p (a b) -> p a b", b=shape[1]) if len(shape) == 2 else v

    def slot(s, a, words=SLOT):
        v = ring[:, s * SLOT:s * SLOT + words] if s < FF_SLOTS else scratch((s - FF_SLOTS) * SLOT, words)
        return v.rearrange("p (a b) -> p a b", a=a)

    def bank(b, *shape):
        v = psum[:, b, :]
        return v.rearrange("p (a b) -> p a b", b=shape[1]) if shape else v

    def over(v, n):
        return v.unsqueeze(1).to_broadcast([v.shape[0], n, v.shape[1]])

    def along(v, n):
        return v.unsqueeze(2).to_broadcast([v.shape[0], v.shape[1], n])

    ident = region(A_CONST + C_IDENT, P)
    ustrict = region(A_CONST + C_USTRICT, P)
    iota = region(A_CONST + C_IOTA, T)
    ones = region(A_CONST + 512, P)
    causal = region(A_PHASE, TB, T)
    decay = region(A_PHASE + 2 * T, RET_H * TB, T)
    wbias = region(A_PHASE, TB, T)
    pool_m = region(A_PHASE + 2 * T, len(POOL_W) * TB, T)
    vec_a = scratch(M_LOGIT, P)
    vec_b = scratch(M_E, P)
    cols_a, cols_b = region(A_COLA, P), region(A_COLB, P)
    vec_rows = [sum(n for _, n in table.values()) for table in (VEC_A, VEC_B)]
    mod = region(A_MOD, 2 * 48)
    small = region(A_SMALL, 512)
    lam_rows, lam_prod, lam_sum = scratch(M_A, 4 * 64), scratch(M_AT, 2, 64), small[:, 0:2]
    lam_exp, neg_lam = small[:, 2:4], small[:, 4:5]
    cond = small[:, 8:16]
    sink = small[:, 16:24]
    bias_r1 = small[:, 24:44]
    dmax, dsum, drec = small[:, 44:46], small[:, 46:48], small[:, 48:50]
    da_gain = small[:, 50:51]
    eps = small[:, 51:52]
    esink = small[:, 52:54]
    modp1 = small[:, 64:64 + 2 * 48]

    def col_a(name, k=0):
        at = VEC_A[name][0] + k
        return cols_a[:, at:at + 1]

    def col_b(name, k=0):
        at = VEC_B[name][0] + k
        return cols_b[:, at:at + 1]

    xT, memT, yda = region(R_X, KT, T), region(R_MEM, KT, T), scratch(M_YDA, KT, T)
    x_tok, mem_tok = region(R_Q, TB, D), scratch(M_RV, TB, D)
    daq, dak, dav = region(R_Q, KT, T), region(R_K, KT, T), region(R_V, TB, D)
    rq, rk, rv, rg = scratch(M_RQ, RET_H, T), scratch(M_RK, RET_H, T), scratch(M_RV, TB, D), scratch(M_RG, KT, T)
    mq, mk, mv = daq, dak, dav
    ymem, yret = memT, rg
    gate, merged = scratch(M_GATE, KT, T), scratch(M_MERGED, KT, T)
    logit, e_prob, a_prob, a_turn = (scratch(M_LOGIT, 2, T), scratch(M_E, 2, T), scratch(M_A, TB, T),
                                     scratch(M_AT, 2, T))
    osq, rstd = scratch(M_OSQ, T), scratch(M_RSTD, T)
    ret_s, ret_o, ret_stat, ret_sq = (region(R_TAIL, 2, T), region(R_TAIL + 512, 2, T), region(R_TAIL + 1024, T),
                                      scratch(M_RSQ, 2, T))
    gtmp = ret_sq
    z, z_sq = region(R_Q, KT, T), region(R_K, KT, T)
    ln_stat = region(R_TAIL + 1024, T)
    ada_sum = scratch(M_ADA, 2, PANEL)
    router = (small[:, 160:320].rearrange("p (k e) -> p k e", e=G1 + N1),
              small[:, 320:384].rearrange("p (k e) -> p k e", e=N2))

    acc, hT = region(R_X, KT, T), region(R_MEM, KT, T)
    tok = region(R_V, TB, D)
    s_tile, h_tile = region(R_Q, TB, PANEL), region(R_Q + 1024, TB, PANEL)
    perm, spread = region(R_K, TB, T), region(R_K + 512, TB, T)
    w_pool = scratch(M_WPOOL, 4, P)
    later_sq = region(R_MEM, KT, T)
    mix = scratch(M_MIX, KT, T)
    p_tok, pooled = region(R_Q, TB, 4 * P), region(R_Q + 1024, 4, T)
    q2, k2, v2 = region(R_K, 4, T), region(R_K + 1024, GQA_KV, T), region(R_K + 1536, TB, P)
    logit2, e2, a2, at2 = (region(R_V, TB, T), region(R_V + 512, TB, T), region(R_V + 1024, TB, T),
                           region(R_V + 1536, TB, T))
    v_tok = region(R_Q, TB, D)
    ws_t = region(R_K, SG_G, P)
    w_s, sg_rows, bs_rows = scratch(M_WS, SG_G, P), scratch(M_ROWS, 2, D), scratch(M_BIAS, SG_G, P)
    out_tok = region(R_V, TB, D)

    def route(at, *shape):
        return region(R_TAIL + at, *shape)

    lg, top_v, top_e, top_1, top_2, sel, hot_g = (route(0, TB, G1 + N1), route(40, TB, N1), route(72, TB, N1),
                                                  route(104, TB, N1), route(136, TB, N1), route(168, TB, N1),
                                                  route(200, TB, G1))
    peak, peak_1, peak_2, ratio, wt_1, wt_2, p_top = (route(208 + 2 * k, TB) for k in range(7))
    desc = route(224, N1)
    ex_g = route(240, TB, G1)
    bn_s, bn_a = route(256, TB, 4 * 6), route(304, TB, 2)
    table = region(R_TAIL + 320, 2 * TB, N2 + 1)
    weights = region(R_TAIL + 360, TB, N1 + 4)
    mine, mine_w, own_w = route(400, 2 * TB), route(404, TB, 4), route(412, TB, 4)
    job_done = sem("job_done")
    bank_free = [sem(f"bank_free{b}") for b in range(BANKS)]
    slot_full = [sem(f"slot_full{s}") for s in range(SLOTS)]
    const_in, x_in, mem_in, vec_in, row_in = (sem("const_in"), sem("x_in"), sem("mem_in"), sem("vec_in"),
                                              sem("row_in"))
    phase_in = sem("phase_in")
    ones_set = sem("ones_set")
    dve_step, act_step = sem("dve_step"), sem("act_step")
    lam_summed, lam_exped, neg_lam_set, cond_set = (sem("lam_summed"), sem("lam_exped"), sem("neg_lam_set"),
                                                    sem("cond_set"))
    da_logits, da_exped, da_probs, da_squared, da_y = (sem("da_logits"), sem("da_exped"), sem("da_probs"),
                                                       sem("da_squared"), sem("da_y"))
    ret_scored, ret_centred, ret_squared, ret_normed, ret_scaled, ret_y = (
        sem("ret_scored"), sem("ret_centred"), sem("ret_squared"), sem("ret_normed"), sem("ret_scaled"), sem("ret_y"))
    mem_max, mem_probs = sem("mem_max"), sem("mem_probs")
    gated, merged_set = sem("gated"), sem("merged_set")
    ln_centred, ln_squared, ln_normed, ln_out = sem("ln_centred"), sem("ln_squared"), sem("ln_normed"), sem("ln_out")
    ada_summed = sem("ada_summed")
    router_in, small_in, modp1_set, modulated, acc_scaled = (sem("router_in"), sem("small_in"), sem("modp1_set"),
                                                             sem("modulated"), sem("acc_scaled"))
    route_diff, route_exp, masks_set, counts_set = sem("route_diff"), sem("route_exp"), sem("masks_set"), sem("counts_set")
    gqa_logits, gqa_exped, gqa_probs = sem("gqa_logits"), sem("gqa_exped"), sem("gqa_probs")
    v_normed, sg_gated, z_set = sem("v_normed"), sem("sg_gated"), sem("z_set")
    mine_set = sem("mine_set")
    perm_set, x_hi_set, x_lo_set, spread_set = sem("perm_set"), sem("x_hi_set"), sem("x_lo_set"), sem("spread_set")
    chunk_hi, chunk_lo = sem("chunk_hi"), sem("chunk_lo")
    silu_set, h_set, h_hi_set, h_lo_set = sem("silu_set"), sem("h_set"), sem("h_hi_set"), sem("h_lo_set")
    y_copied, added = sem("y_copied"), sem("added")
    out_staged, out_stored = sem("out_staged"), sem("out_stored")

    plans = (mixer1_steps(), mixer2_steps(), mixer3_steps(), last_steps())
    def unit_steps(pairs, routed, first):
        chunk = lambda side, p: [("chunk", side, p, c) for c in range(4 if side != "D" else pairs[p] // P)]
        last = len(pairs) - 1
        s = [("gather_first", i) for i in range(4)] if routed and first else []
        s += chunk("G", 0)
        s += [("scatter", i) for i in range(4)] if routed and not first else []
        s += [("spread",)] if routed else []
        s += chunk("U", 0)
        for p in range(last):
            g = chunk("G", p + 1)
            n = 4 if routed else 1
            s += g[:n] + [("turn", p)] + g[n:] + chunk("U", p + 1) + chunk("D", p)
        s += [("turn", last)]
        s += [("gather", i) for i in range(4)] if routed else []
        return s + chunk("D", last)

    FFN_P = [min(PANEL, FFN - c) for c in range(0, FFN, PANEL)]
    feeds = [dict(pairs=[FF1] * E1, n=G1, routed=True, gain=None, weights=E1),
             dict(pairs=FFN_P, n=1, routed=False, gain=(0, 5), weights=0),
             dict(pairs=[PANEL] * (FF2 // PANEL), n=N2, routed=True, gain=(1, 5), weights=1)]
    chunks_before = pairs_before = routed_before = units_before = filled_before = 0
    for f in feeds:
        f["steps"] = [unit_steps(f["pairs"], f["routed"], first) for first in (False, True)]
        assert len(f["steps"][0]) == len(f["steps"][1])
        f["jobs"] = len(f["steps"][0])
        f["pos"] = [{q: n + 1 for n, q in enumerate(steps)} for steps in f["steps"]]
        f["order"] = [q for q in f["steps"][0] if q[0] == "chunk"]
        f["chunks"] = len(f["order"])
        f["count"] = {q: n for n, q in enumerate(f["order"])}
        f["c0"], f["p0"], f["r0"], f["u0"] = chunks_before, pairs_before, routed_before, units_before
        chunks_before += f["chunks"] * f["n"]
        pairs_before += len(f["pairs"]) * f["n"]
        routed_before += f["n"] if f["routed"] else 0
        units_before += f["n"]
        f["x0"] = filled_before
        filled_before += f["n"] + 1 if f["routed"] else 1
    index, done, plan_end = {}, {}, []
    at = 0
    for n, plan in enumerate(plans):
        for s in plan:
            at += 1
            index[s], done[s] = len(index), at
        plan_end.append(at)
        if n < 3:
            feeds[n]["at"] = at
            at += feeds[n]["jobs"] * feeds[n]["n"] + 4
    def job_bank(s):
        return index[s] % BANKS

    def bank_through(s):
        return bank_free[index[s] % BANKS], index[s] // BANKS + 1

    gemm_src = {}
    at = 0
    for name, cols in (("da_q", 1024), ("da_k", 1024), ("da_v", 1024), ("r_q", 512), ("r_k", 512), ("r_v", 1024),
                       ("r_g", 1024), ("m_q", 1024), ("gate0", 1024), ("gate1", 1024), ("gate2", 1024)):
        gemm_src[name] = (w["w_in"][0], at)
        at += cols
    gemm_src["m_k"], gemm_src["m_v"] = (w["w_mem_kv"][0], 0), (w["w_mem_kv"][0], D)
    for n in range(3):
        gemm_src[f"branch{n}"] = (w["w_branch"][0, n], 0)
    gemm_src["w_o"] = (w["w_o"][0], 0)
    gemm_src["ev_p"], gemm_src["ev_q"] = (w["ev_w_in_2"][0], 0), (w["ev_w_in_2"][0], 512)
    gemm_src["ev_o"] = (w["ev_w_out_2"][0], 0)
    gemm_src["od_u"], gemm_src["od_v"] = (w["od_w_in_2"][0], 0), (w["od_w_in_2"][0], D)
    gemm_src["od_o"] = (w["od_w_out_2"][0], 0)
    token_major = ("da_v", "r_v", "m_v", "ev_p", "od_v")

    def cols(src, c0, n=PANEL):
        return src[:, c0:c0 + n].rearrange("(k p) n -> p k n", p=P)

    fills = [0] * SLOTS
    freed = [None] * SLOTS
    loads = {0: [], 1: [], 2: []}
    panel = {}

    def fill_slot(where, key, s, words, src, free):
        loads[where].append((s, words, src, freed[s]))
        fills[s] += 1
        freed[s] = free
        panel[key] = (s, fills[s])

    def plan_loads(n, count, start=0):
        at = start
        for s in plans[n]:
            key, words = s, SLOT
            if s[0] == "gemm" and s[2] % 2 == 0:
                src, c0 = gemm_src[s[1]]
                src, free = cols(src, c0 + s[2] // 2 * PANEL), (job_done, done[("gemm", s[1], s[2] + 1)])
            elif s[0] == "ev_k":
                src, words = cols(w["ev_w_in_2"][0], 1024, 256), KT * 256
                free = (job_done, done[("ev_v", 0, 0)])
            elif s == ("da_score", 0, 0) or s[0] == "ada" and s != ("ada", 1, 11):
                m = 0 if s[0] == "da_score" else 12 * s[1] + s[2] + 1
                key = ("ada", m // 12, m % 12)
                src, free = cols(w["ada_w_2"][m // 12], m % 12 * PANEL), (ada_summed, m + 1)
            else:
                continue
            fill_slot(n, key, at % count, words, src, free)
            at += 1
        return at

    def panel_order(f):
        return [q[1:3] for q in f["order"] if q[3] == 0]

    for n in range(3):
        plan_loads(n, SLOTS)
        f = feeds[n]
        f["freed"], f["base"] = freed[:FF_SLOTS], fills[:FF_SLOTS]
        order = panel_order(f)
        for k in range(len(order)):
            fills[k % FF_SLOTS] += f["n"]
            if k >= len(order) - FF_SLOTS:
                last = ("chunk", *order[k], 3 if order[k][0] != "D" else f["pairs"][order[k][1]] // P - 1)
                freed[k % FF_SLOTS] = (chunk_lo, f["c0"] + f["chunks"] * (f["n"] - 1) + f["count"][last] + 1)
        for k in range(FF_SLOTS, SLOTS):
            freed[k] = (job_done, f["at"] + f["jobs"] * f["n"] + 4)

    def panel_of(s):
        return panel[("gemm", s[1], s[2] - s[2] % 2) if s[0] == "gemm" else s]

    def layer_norm_scalar(act, n, z, z_sq, sq_done, sq_bank, sq_free, gain_bias, dst):
        for part in range(4):
            act.wait_ge(ln_centred, 4 * n + part + 1)
            act.activation(z_sq[:, 2 * part:2 * part + 2, :], z[:, 2 * part:2 * part + 2, :],
                           ACT.Square).then_inc(ln_squared, 1)
        act.wait_ge(job_done, sq_done)
        act.activation(ln_stat, psum[:, sq_bank, 0:T], ACT.Sqrt, bias=eps, scale=1.0 / D).then_inc(sq_free, 1)
        for k in range(KT):
            if k % 2 == 0:
                act.wait_ge(ln_normed, 4 * n + k // 2 + 1)
            g, b = gain_bias(k)
            act.activation(dst[:, k, :], z[:, k, :], ACT.Identity, bias=b, scale=g).then_inc(ln_out, 1)

    def layer_norm_vector(dve, settle, n, z, sum_done, sum_bank, sum_free, sq_read, modulate):
        dve.wait_ge(job_done, sum_done)
        dve.tensor_scalar(ln_stat, psum[:, sum_bank, 0:T], 1.0 / D, None, ALU.mult).then_inc(sum_free[0], 1)
        dve.wait_ge(*sum_free)
        for part in range(4):
            zp = z[:, 2 * part:2 * part + 2, :]
            dve.tensor_tensor(zp, zp, over(ln_stat, 2), ALU.subtract).then_inc(ln_centred, 1)
        dve.wait_ge(ln_centred, 4 * n + 4)
        dve.wait_ge(*sq_read)
        settle(dve.reciprocal(ln_stat, ln_stat))
        for part in range(4):
            zp = z[:, 2 * part:2 * part + 2, :]
            dve.wait_ge(ln_squared, 4 * n + part + 1)
            dve.tensor_tensor(zp, zp, over(ln_stat, 2), ALU.mult).then_inc(ln_normed, 1)
            if part:
                modulate(part - 1)
        modulate(3)

    def by_width(eng, count, body):
        with eng.If(count < P + 1):
            body(P)
        with eng.Else():
            body(T)

    def units(eng, f, body, tail):
        if not f["routed"]:
            body(0, T, None, None)
            tail(T)
            return

        def count(u):
            return eng.value_load(counts_i[0:1, bass.ds(u, 1)], min_val=0, max_val=T)

        count_0, count_1 = count(0), count(1)
        by_width(eng, count_0, lambda width: body(0, width, None, count_1))
        with eng.Fori(1, f["n"]) as u:
            before, own, after = count(u - 1), count(u), count(u + 1)
            by_width(eng, own, lambda width: body(u, width, before, after))
        by_width(eng, count(f["n"] - 1), tail)

    def at_unit(u, per_unit, value):
        return u * per_unit + value

    def chunk_view(tensor, f, side, p, c):
        n = f["count"][("chunk", side, p, c)] % STAGES
        rows, width = (2, f["pairs"][p]) if side != "D" else (1, D)
        return tensor[:, n, 0:rows * width].rearrange("p (a b) -> p a b", b=width)

    def chunk_source(f, side, p, c):
        k = panel_order(f).index((side, p)) % FF_SLOTS
        rows, width = (2, f["pairs"][p]) if side != "D" else (1, D)
        words = KT * f["pairs"][p]
        return slot(k, words // width, words)[:, rows * c:rows * (c + 1), :]

    def h_point(f, width):
        make, split = {}, {}
        order, count, last = f["order"], f["count"], len(f["pairs"]) - 1
        for p in range(last + 1):
            make[order[count[("chunk", "U", p, 3)] + STAGES - 1]] = p
            before_turn = count[("chunk", "G", p + 1, 3 if f["routed"] else 0) if p < last
                                else ("chunk", "D", p - 1, 3)]
            at = max(before_turn + (STAGES if width == P else 2), count[("chunk", "U", p, 3)] + STAGES - 1)
            split[order[min(at, len(order) - 1)]] = p
        return make, split

    def gather_bank(width, own, i):
        b = 2 if width == P else 4
        if own == P:
            return bank(b + i // 2, 4, P)[:, i % 2 * 2:i % 2 * 2 + 2, :]
        return bank(b + i % 2, 2, T)

    def when(eng, sem, value):
        if not isinstance(value, int) or value > 0:
            eng.wait_ge(sem, value)

    def mod_cols(tile, layer, part, k):
        at = layer * 48 + part * KT + k
        return tile[:, at:at + 1]

    block = ctx.enter_context(nc.Block())

    @block.sync
    def _(sp):
        sp.dma_start(x_tok, w["x"][0].rearrange("(b p) d -> p b d", p=P)).then_inc(x_in, 16)
        sp.dma_start(arena[:, 0:C_COMMON], w["consts"][:, 0:C_COMMON]).then_inc(const_in, 16)

        def load(s, words, src, wait):
            if wait:
                sp.wait_ge(*wait)
            sp.dma_start(slot(s, src.shape[1], words), src).then_inc(slot_full[s], 16)

        def source(f, n, u, side, p):
            if n == 0:
                gate_w, up_w, down_w = w["w1"][0][u * E1 + p], w["w3"][0][u * E1 + p], w["w2"][0][u * E1 + p]
                c0 = 0
            elif n == 1:
                gate_w, up_w, down_w = w["ffn_w_gate_2"][0], w["ffn_w_up_2"][0], w["ffn_w_down_2"][0]
                c0 = p * PANEL
            else:
                gate_w, up_w, down_w = w["moe_w_gate_2"][0][u], w["moe_w_up_2"][0][u], w["moe_w_down_2"][0][u]
                c0 = p * PANEL
            width = f["pairs"][p]
            if side == "D":
                return down_w[c0:c0 + width, :].rearrange("(j p) d -> p j d", p=P)
            return cols(gate_w if side == "G" else up_w, c0, width)

        def unit_loads(f, n, u):
            for k, (side, p) in enumerate(panel_order(f)):
                wait = (chunk_lo, at_unit(u, f["chunks"], f["c0"] + 4 * (k - FF_SLOTS + 1)))
                if isinstance(u, int) and k < FF_SLOTS:
                    wait = f["freed"][k]
                load(k % FF_SLOTS, KT * f["pairs"][p], source(f, n, u, side, p), wait)

        def small_loads():
            for table, tile, names in ((VEC_A, vec_a, {"b_gate": w["b_gate"], "gn_g": w["ret_gn_g"], "gn_b": w["ret_gn_b"],
                                                       "ln1_g": w["ln1_g"], "ln1_b": w["ln1_b"], "da_g": w["da_norm_g"],
                                                       "ln2_g": w["ln2_g"], "ln2_b": w["ln2_b"], "lng_2": w["ln_g_2"],
                                                       "c": w["c_2"], "pool_scale": w["ev_pool_scale_2"]}),
                                       (VEC_B, vec_b, {"ada_b": w["ada_b_2"], "lnb_2": w["ln_b_2"]})):
                for name, src in names.items():
                    r0, n = table[name]
                    flat = src.rearrange("a b c -> (a b c)") if len(src.shape) == 3 else src.rearrange("a b -> (a b)")
                    sp.dma_start(tile[r0:r0 + n, :], flat.rearrange("(k p) -> k p", p=P)).then_inc(vec_in, 16)
            for dst, src in ((lam_rows, w["da_lambda"][0].rearrange("a b -> (a b)")), (sink, w["ev_sink_2"][0]),
                             (bias_r1[:, 0:G1], w["b_rg"][0]), (bias_r1[:, G1:G1 + N1], w["b_re"][0])):
                sp.dma_start(dst, src.partition_broadcast(P)).then_inc(row_in, 16)
            for dst, src in ((router[0][:, :, 0:G1], w["w_rg"][0]), (router[0][:, :, G1:], w["w_re"][0]),
                             (router[1], w["moe_w_router_2"][0])):
                sp.dma_start(dst, src.rearrange("(k p) e -> p k e", p=P)).then_inc(router_in, 16)

        for n, f in enumerate(feeds):
            for k, one in enumerate(loads[n]):
                if n == 0 and k == SLOTS:
                    small_loads()
                load(*one)
            unit_loads(f, n, 0)
            if f["n"] > 1:
                with sp.Fori(1, f["n"]) as u:
                    unit_loads(f, n, u)
        for i in range(4):
            sp.wait_ge(*bank_through(("turn_out", i, 0)))
            c = slice(i % 2 * 4 * P, (i % 2 + 1) * 4 * P)
            sp.dma_start(out[i // 2 * P:(i // 2 + 1) * P, c], out_tok[:, i // 2, c]).then_inc(out_stored, 16)
        sp.wait_ge(out_stored, 4 * 16)

    @block.gpsimd
    def _(pool):
        nc.gpsimd.memset(ones, 1.0).then_inc(ones_set, 1)
        nc.gpsimd.memset(eps, EPS).then_inc(ones_set, 1)

    @block.scalar
    def _(act):
        step = [0]

        def settle(ins):
            step[0] += 1
            ins.then_inc(act_step, 1)
            act.wait_ge(act_step, step[0])

        def full(s):
            act.wait_ge(job_done, done[s])
            return job_bank(s)

        def evacuated(s):
            act.wait_ge(*bank_through(s))

        def copy(out_, s, view, scale=1.0):
            b = full(s)
            act.activation(out_, view(b), ACT.Copy, scale=scale).then_inc(bank_free[b], 1)

        as_blocks = lambda b: bank(b, 2, T)

        def walk(plan):
            for s in plan:
                kind, a, i = s
                if kind == "vec":
                    n = vec_rows[a]
                    copy((cols_a, cols_b)[a][:, 0:n], s, lambda b: psum[:, b, 0:n])
                    if a == 0:
                        evacuated(s)
                        act.activation(cond, cols_a[:, VEC_A["c"][0]:VEC_A["c"][0] + KT], ACT.Silu).then_inc(cond_set, 1)
                    else:
                        act.wait_ge(lam_summed, 1)
                        act.activation(lam_exp, lam_sum, ACT.Exp).then_inc(lam_exped, 1)
                elif kind == "turn_x":
                    copy(xT[:, 2 * a:2 * a + 2, :], s, as_blocks)
                    if kind == "turn_x" and a == 3:
                        mixer_loads()
                elif kind == "turn_mem":
                    copy(memT[:, 2 * a:2 * a + 2, :], s, as_blocks)
                elif kind == "gemm" and a in ("da_v", "r_v", "m_v"):
                    if a == "r_v":
                        act.wait_ge(job_done, done[("turn_mem", 3, 0)])
                    dst = {"da_v": dav, "r_v": rv, "m_v": mv}[a]
                    copy(dst[:, i % 2, i // 2 * PANEL:(i // 2 + 1) * PANEL], s, bank)
                elif kind == "gemm" and a in ("da_q", "da_k", "m_q", "m_k", "r_q", "r_k"):
                    dst = {"da_q": daq, "da_k": dak, "m_q": mq, "m_k": mk, "r_q": rq, "r_k": rk}[a]
                    scale = {"da_q": (D // (2 * DA_H)) ** -0.5, "m_q": (D // MEM_H) ** -0.5}.get(a, 1.0)
                    copy(dst[:, 2 * i:2 * i + 2, :], s, as_blocks, scale)
                elif kind == "gemm" and a == "r_g":
                    b = full(s)
                    act.activation(rg[:, 2 * i:2 * i + 2, :], bank(b, 2, T), ACT.Silu).then_inc(bank_free[b], 1)
                elif kind == "gemm" and a.startswith("gate"):
                    n = int(a[-1])
                    if n:
                        evacuated(("gemm", f"branch{n - 1}", i))
                    b = full(s)
                    for k in range(2):
                        ins = act.activation(gate[:, 2 * i + k, :], bank(b, 2, T)[:, k, :], ACT.Sigmoid,
                                             bias=col_a("b_gate", n * KT + 2 * i + k))
                    ins.then_inc(bank_free[b], 1)
                elif kind == "da_score":
                    u = 2 * a + i
                    act.wait_ge(da_logits, u + 1)
                    if u:
                        act.wait_ge(da_probs, u)
                    for c in range(2):
                        ins = act.activation(e_prob[:, c, :], logit[:, c, :], ACT.Exp, bias=dmax[:, c:c + 1],
                                             accum_out=dsum[:, c:c + 1])
                    ins.then_inc(da_exped, 1)
                elif kind == "da_turn":
                    copy(a_turn, s, as_blocks)
                elif kind == "da_out":
                    b = full(s)
                    if a:
                        act.wait_ge(job_done, done[("da_norm", a - 1, 0)])
                    act.activation(osq, psum[:, b, 0:T], ACT.Square).then_inc(da_squared, 1)
                elif kind == "da_norm":
                    b = full(s)
                    if a:
                        evacuated(("da_out", a - 1, 0))
                    act.activation(rstd, psum[:, b, 0:T], ACT.Sqrt, bias=eps, scale=1.0 / P).then_inc(bank_free[b], 1)
                elif kind == "ret_out":
                    if a:
                        act.wait_ge(ret_y, a)
                    copy(ret_o, s, as_blocks)
                elif kind == "ret_mean":
                    act.wait_ge(ret_centred, a + 1)
                    act.activation(ret_sq, ret_o, ACT.Square).then_inc(ret_squared, 1)
                elif kind == "ret_var":
                    b = full(s)
                    act.activation(ret_stat, psum[:, b, 0:T], ACT.Sqrt, bias=eps, scale=1.0 / 256)\
                       .then_inc(bank_free[b], 1)
                    act.wait_ge(ret_normed, a + 1)
                    for k in range(2):
                        n = 2 * a + k
                        ins = act.activation(ret_o[:, k, :], ret_o[:, k, :], ACT.Identity, bias=col_a("gn_b", n),
                                             scale=col_a("gn_g", n))
                    ins.then_inc(ret_scaled, 1)
                elif kind == "mem_score":
                    b = full(s)
                    act.wait_ge(mem_max, a + 1)
                    if a:
                        act.wait_ge(mem_probs, a)
                    for c in range(TB):
                        ins = act.activation(e_prob[:, c, :], bank(b, 2, T)[:, c, :], ACT.Exp, bias=dmax[:, c:c + 1],
                                             accum_out=dsum[:, c:c + 1])
                    ins.then_inc(bank_free[b], 1)
                elif kind == "mem_turn":
                    copy(a_turn, s, as_blocks)
                elif kind == "mem_out":
                    copy(ymem[:, 2 * a:2 * a + 2, :], s, as_blocks)
                elif kind == "turn_tok":
                    copy(tok[:, i // 2, i % 2 * PANEL:(i % 2 + 1) * PANEL], s, bank)
                    if a == 0 and i == 3:
                        later_loads()
                elif kind == "logits":
                    for n in range(2 - a):
                        act.wait_ge(route_diff, 2 * a + n + 1)
                        t = ex_g if (a, n) == (0, 0) else ratio
                        act.activation(t, t, ACT.Exp).then_inc(route_exp, 1)
                elif kind == "gemm" and a == "ev_p":
                    copy(p_tok[:, i, :], s, bank)
                elif kind == "gemm" and a == "ev_q":
                    copy(q2[:, 2 * i:2 * i + 2, :], s, as_blocks, GQA_D ** -0.5)
                elif kind == "ev_k":
                    b = full(s)
                    for g in range(GQA_KV):
                        for half in range(2):
                            ins = act.activation(k2[64 * half:64 * half + 64, g, :], psum[64 * g:64 * g + 64, b, 0:T],
                                                 ACT.Copy)
                    ins.then_inc(bank_free[b], 1)
                elif kind == "ev_v":
                    copy(v2, s, lambda b: psum[:, b, 0:T].rearrange("p (t c) -> p t c", c=P))
                elif kind == "pool":
                    copy(pooled[:, 2 * a:2 * a + 2, :], s, as_blocks)
                elif kind == "pool_map":
                    b = full(s)
                    for k in range(2):
                        ins = act.activation(mix[:, 2 * a + k, :], bank(b, 2, T)[:, k, :], ACT.Identity,
                                             scale=col_a("pool_scale", 2 * a + k))
                    ins.then_inc(bank_free[b], 1)
                elif kind == "gqa_score":
                    act.wait_ge(gqa_logits, a + 1)
                    if a:
                        act.wait_ge(gqa_probs, a)
                    for t in range(TB):
                        act.activation(e2[:, t, :], logit2[:, t, :], ACT.Exp, bias=dmax[:, t:t + 1],
                                       accum_out=dsum[:, t:t + 1])
                    act.activation(esink, dmax, ACT.Exp, bias=sink[:, a:a + 1]).then_inc(gqa_exped, 1)
                elif kind == "gqa_turn":
                    copy(at2, s, as_blocks)
                elif kind == "gqa_out":
                    p0 = 64 * (a % 2)
                    copy(mix[p0:p0 + 64, 4 + a // 2, :], s, lambda b: psum[p0:p0 + 64, b, 0:T])
                elif kind == "turn_ws":
                    copy(ws_t[:, 4 * a:4 * a + 4, :], s, lambda b: bank(b, 4, P))
                elif kind == "gemm" and a in ("od_u", "od_v"):
                    b = full(s)
                    if a == "od_u":
                        act.activation(mix[:, 2 * i:2 * i + 2, :], bank(b, 2, T), ACT.Gelu_apprx_tanh)\
                           .then_inc(bank_free[b], 1)
                    else:
                        act.activation(v_tok[:, i % 2, i // 2 * PANEL:(i // 2 + 1) * PANEL], bank(b),
                                       ACT.Gelu_apprx_tanh).then_inc(bank_free[b], 1)
                        if i == 3:
                            act.wait_ge(v_normed, 1)
                            act.activation(bn_a[:, :, 1:2], bn_a[:, :, 1:2], ACT.Sqrt, bias=eps).then_inc(v_normed, 1)
                elif kind == "turn_out":
                    copy(out_tok[:, a // 2, a % 2 * PANEL:(a % 2 + 1) * PANEL], s, bank)
                elif kind == "ln_sum":
                    sq = ("ln_sq", a, 0)
                    gain_bias = ((lambda k: (col_a("ln1_g", k), col_a("ln1_b", k))),
                                 (lambda k: (col_a("ln2_g", k), col_a("ln2_b", k))),
                                 *((lambda k, n=n: (col_a("lng_2", 8 * n + k), col_b("lnb_2", 8 * n + k)))
                                   for n in range(4)))[a]
                    src, squares = (z, z_sq) if a == 0 else (acc, later_sq)
                    layer_norm_scalar(act, a, src, squares, done[sq], job_bank(sq), bank_free[job_bank(sq)], gain_bias, acc)

        def mixer_loads():
            act.wait_ge(slot_full[0], 16)
            act.dma_start(region(A_PHASE, C_PHASE), w["consts"][:, C_COMMON:C_COMMON + C_PHASE]).then_inc(phase_in, 16)
            act.dma_start(mem_tok, w["mem"][0].rearrange("(b p) d -> p b d", p=P)).then_inc(mem_in, 16)

        def later_loads():
            act.wait_ge(da_probs, 2 * DA_H)
            act.wait_ge(ret_y, RET_H)
            act.dma_start(region(A_PHASE, C_PHASE), w["consts"][:, C_COMMON + C_PHASE:]).then_inc(small_in, 16)

        def pool_loads():
            act.dma_start(w_pool, w["ev_pool_w_2"][0].rearrange("g c d -> c g d")).then_inc(small_in, 16)

        def gate_loads():
            act.dma_start(w_s, w["od_w_s_2"][0].rearrange("g t s -> t g s")).then_inc(small_in, 16)
            for dst, src in ((sg_rows[:, 0, :], w["od_sg_ln_g_2"][0]), (sg_rows[:, 1, :], w["od_sg_ln_b_2"][0]),
                             (bs_rows.rearrange("p g t -> p (g t)"), w["od_b_s_2"][0].rearrange("g t -> (g t)"))):
                act.dma_start(dst, src.partition_broadcast(P)).then_inc(small_in, 16)

        def unit(f):
            pairs, count = f["pairs"], f["count"]

            def split_chunk(q, pos, jobs, u):
                _, side, p, c = q
                n = count[q]
                if c == 0:
                    k = panel_order(f).index((side, p))
                    act.wait_ge(slot_full[k % FF_SLOTS],
                                at_unit(u, 16 * len(pairs), 16 * (f["base"][k % FF_SLOTS] + k // FF_SLOTS + 1)))
                if n >= STAGES:
                    act.wait_ge(job_done, jobs + pos[f["order"][n - STAGES]])
                elif not isinstance(u, int):
                    act.wait_ge(job_done, jobs + (pos[f["order"][n - STAGES]] - f["jobs"]))
                act.activation(chunk_view(stage_hi, f, side, p, c), chunk_source(f, side, p, c), ACT.Copy)\
                   .then_inc(chunk_hi, 1)

            def take_tokens(jobs, pos, name, width, own):
                for i in range(4):
                    if f["routed"]:
                        act.wait_ge(job_done, jobs + pos[(name, i | 1 if own == P else i)])
                        src = gather_bank(width, own, i)[:, :, 0:own]
                    else:
                        src = hT[:, 2 * i:2 * i + 2, :]
                    act.activation(x_hi[:, 2 * i:2 * i + 2, 0:own], src, ACT.Copy).then_inc(x_hi_set, 1)

            def copy_output(value, width):
                act.wait_ge(job_done, value)
                for t in range(width // P):
                    ins = act.activation(y_tok[:, t, :].rearrange("p (a b) -> p a b", a=2),
                                         psum[:, 2 * t:2 * t + 2, :], ACT.Copy)
                ins.then_inc(y_copied, 1)

            def body(u, width, before, after):
                nt = width // P
                pos = f["pos"][isinstance(u, int)]
                make, split = h_point(f, width)
                jobs, p0 = at_unit(u, f["jobs"], f["at"]), at_unit(u, len(pairs), f["p0"])
                for q in f["order"]:
                    if count[q] == STAGES - 1 and before is not None:
                        by_width(act, before, lambda own: copy_output(jobs, own))
                    split_chunk(q, pos, jobs, u)
                    if count[q] == (2 if f["routed"] else 0) and before is None:
                        take_tokens(jobs, pos, "gather_first", P, width)
                    if q in make:
                        p = make[q]
                        act.wait_ge(job_done, jobs + pos[("chunk", "U", p, 3)])
                        when(act, h_set, p0 + p)
                        g0 = 4 if width == T else 4 + p % 2
                        act.activation(s_tile[:, 0:nt, 0:pairs[p]], psum[:, g0:g0 + nt, 0:pairs[p]], ACT.Silu)\
                           .then_inc(silu_set, 1)
                    if q in split:
                        p = split[q]
                        act.wait_ge(job_done, jobs + pos[("turn", p)])
                        t0, blocks = (6 if width == T else 7), pairs[p] // P
                        for t in range(nt):
                            ins = act.activation(h_hi[:, 0:blocks, t * P:(t + 1) * P],
                                                 bank(t0 + t, 4, P)[:, 0:blocks, :], ACT.Copy)
                        ins.then_inc(h_hi_set, 1)
                if after is not None:
                    by_width(act, after, lambda own: take_tokens(jobs, pos, "gather", width, own))

            def tail(width):
                copy_output(f["at"] + f["jobs"] * f["n"], width)

            return body, tail

        for n in range(3):
            if n == 1:
                pool_loads()
            elif n == 2:
                gate_loads()
            walk(plans[n])
            act.wait_ge(job_done, plan_end[n])
            act.wait_ge(ada_summed, 24)
            if feeds[n]["routed"]:
                evacuated(("rank", n // 2, 0))
            else:
                act.wait_ge(modulated, 2 * KT)
            units(act, feeds[n], *unit(feeds[n]))
        walk(plans[3])

    @block.vector
    def _(dve):
        step = [0]

        def settle(ins):
            step[0] += 1
            ins.then_inc(dve_step, 1)
            dve.wait_ge(dve_step, step[0])

        def full(s):
            dve.wait_ge(job_done, done[s])
            return job_bank(s)

        def evacuated(s):
            dve.wait_ge(*bank_through(s))

        dve.wait_ge(row_in, 4 * 16)
        lam4 = lam_rows.rearrange("p (a b) -> p a b", b=64)
        settle(dve.tensor_tensor(lam_prod, lam4[:, 0:4:2, :], lam4[:, 1:4:2, :], ALU.mult))
        dve.tensor_reduce(lam_sum, lam_prod, AX.X, ALU.add).then_inc(lam_summed, 1)
        dve.wait_ge(lam_exped, 1)
        settle(dve.tensor_tensor(neg_lam, lam_exp[:, 1:2], lam_exp[:, 0:1], ALU.subtract))
        settle(dve.tensor_scalar(neg_lam, neg_lam, -LAMBDA_INIT, None, ALU.add))
        evacuated(("vec", 0, 0))
        settle(dve.tensor_scalar(da_gain, col_a("da_g"), 1.0 - LAMBDA_INIT, None, ALU.mult))
        dve.wait_ge(const_in, 16)
        dve.wait_ge(phase_in, 16)
        def sum_modulation(n):
            layer, p = n // 12, n % 12
            at, fill = panel[("ada", layer, p)]
            dve.wait_ge(slot_full[at], 16 * fill)
            if n >= 2:
                dve.wait_ge(job_done, done[("ada", (n - 2) // 12, (n - 2) % 12)])
            tile, wt = ada_sum[:, n % 2, :], slot(at, KT)
            settle(dve.tensor_scalar(tile, wt[:, 0, :], cond[:, 0:1], None, ALU.mult))
            for k in range(1, KT):
                ins = dve.scalar_tensor_tensor(tile, wt[:, k, :], cond[:, k:k + 1], tile, ALU.mult, ALU.add)
                if k < KT - 1:
                    settle(ins)
            ins.then_inc(ada_summed, 1)

        def add_modulation_bias(s):
            b = full(s)
            at = s[1] * 48 + s[2] * 4
            c = VEC_B["ada_b"][0] + at
            dve.tensor_tensor(mod[:, at:at + 4], psum[:, b, 0:4], cols_b[:, c:c + 4], ALU.add)\
               .then_inc(bank_free[b], 1)

        def settled_max_one_hot(values, out_, n, m):
            settle(dve.tensor_reduce(m, values, AX.X, ALU.max))
            settle(dve.tensor_tensor(top_e[:, :, 0:n], values, along(m, n), ALU.is_equal))
            settle(dve.tensor_tensor(top_e[:, :, 0:n], top_e[:, :, 0:n], over(desc[:, 0:n], TB), ALU.mult))
            settle(dve.tensor_reduce(peak, top_e[:, :, 0:n], AX.X, ALU.max))
            settle(dve.tensor_tensor(out_, top_e[:, :, 0:n], along(peak, n), ALU.is_equal))

        def top_two(values, n, told):
            settled_max_one_hot(values, top_1[:, :, 0:n], n, peak_1)
            settle(dve.scalar_tensor_tensor(top_v[:, :, 0:n], top_1[:, :, 0:n], -1e38, values, ALU.mult, ALU.add))
            settled_max_one_hot(top_v[:, :, 0:n], top_2[:, :, 0:n], n, peak_2)
            dve.tensor_tensor(ratio, peak_2, peak_1, ALU.subtract).then_inc(route_diff, 1)
            dve.wait_ge(route_exp, told)
            settle(dve.tensor_scalar(wt_2, ratio, 1.0, None, ALU.add))
            settle(dve.reciprocal(wt_1, wt_2))
            settle(dve.tensor_tensor(wt_2, wt_1, ratio, ALU.mult))

        def routing(m, b, s):
            n = (N1, N2)[m]
            settle(dve.memset(region(R_TAIL + 320, 96), 0.0))
            settle(dve.tensor_copy(counts_i[:, :], region(R_TAIL + 320, N1)))
            settle(dve.tensor_scalar(desc, iota[:, 0:N1], -1.0, float(N1), ALU.mult, ALU.add))
            logits = psum[:, b, 0:TB * (G1 + N1 if m == 0 else N2)].rearrange("p (t e) -> p t e", t=TB)
            if m == 0:
                dve.tensor_tensor(lg, logits, over(bias_r1, TB), ALU.add).then_inc(bank_free[b], 1)
                evacuated(s)
                group, each = lg[:, :, 0:G1], lg[:, :, G1:].rearrange("p t (g e) -> p t g e", e=E1)
                settled_max_one_hot(group, hot_g, G1, peak_1)
                dve.tensor_tensor(ex_g, group, along(peak_1, G1), ALU.subtract).then_inc(route_diff, 1)
                dve.wait_ge(route_exp, 1)
                settle(dve.tensor_reduce(p_top, ex_g, AX.X, ALU.add))
                settle(dve.reciprocal(p_top, p_top))
                hot4 = hot_g.unsqueeze(3).to_broadcast([P, TB, G1, E1])
                four = lambda v: v.rearrange("p t (g e) -> p t g e", e=E1)
                for t in range(TB):
                    settle(dve.tensor_tensor(four(top_v)[:, t], each[:, t], hot4[:, t], ALU.mult))
                    settle(dve.tensor_reduce(sel[:, t, 0:E1], top_v[:, t, :].rearrange("p (g e) -> p e g", e=E1),
                                             AX.X, ALU.add))
                top_two(sel[:, :, 0:E1], E1, 2)
                settle(dve.tensor_tensor(wt_1, wt_1, p_top, ALU.mult))
                settle(dve.tensor_tensor(wt_2, wt_2, p_top, ALU.mult))
            else:
                dve.tensor_copy(lg[:, :, 0:n], logits).then_inc(bank_free[b], 1)
                evacuated(s)
                top_two(lg[:, :, 0:n], n, 3)
            k = E1 if m == 0 else n
            one, two = top_1[:, :, 0:k], top_2[:, :, 0:k]
            w_k, m_k = sel[:, :, 0:k], table[:, TB:2 * TB, 0:k]
            if m == 1:
                settle(dve.tensor_tensor(m_k, one, two, ALU.add))
            else:
                settle(dve.tensor_copy(table[:, TB:2 * TB, 0:G1], hot_g))
            settle(dve.tensor_tensor(one, one, along(wt_1, k), ALU.mult))
            settle(dve.tensor_tensor(two, two, along(wt_2, k), ALU.mult))
            if m == 1:
                dve.tensor_tensor(weights[:, :, 0:k], one, two, ALU.add).then_inc(masks_set, 1)
            else:
                settle(dve.tensor_tensor(w_k, one, two, ALU.add))
                for t in range(TB):
                    ins = dve.tensor_tensor(weights[:, t, 0:n].rearrange("p (g e) -> p g e", e=E1),
                                            along(hot_g[:, t, :], E1), over(w_k[:, t, :], G1), ALU.mult)
                ins.then_inc(masks_set, 1)

        def add_to_result(i, gain, settled):
            if gain is None:
                dve.tensor_tensor(acc[:, 2 * i:2 * i + 2, :], bank(i, 2, T), acc[:, 2 * i:2 * i + 2, :],
                                  ALU.add).then_inc(settled, 1)
                return
            for k in range(2):
                ins = dve.scalar_tensor_tensor(acc[:, 2 * i + k, :], bank(i, 2, T)[:, k, :],
                                               mod_cols(modp1, *gain, 2 * i + k), acc[:, 2 * i + k, :],
                                               ALU.mult, ALU.add)
            ins.then_inc(settled, 1)

        owed = []

        def walk(plan):
            for s in plan:
                kind, a, i = s
                if owed and index[s] >= index[owed[0]] + 2:
                    add_modulation_bias(owed.pop())
                if kind == "da_score":
                    u = 2 * a + i
                    b = full(s)
                    if u:
                        dve.wait_ge(da_exped, u)
                    dve.scalar_tensor_tensor(logit, causal, 2.0 ** -(a + 1), bank(b, 2, T), ALU.mult,
                                             ALU.add).then_inc(bank_free[b], 1)
                    evacuated(s)
                    dve.tensor_reduce(dmax, logit, AX.X, ALU.max, negate=True).then_inc(da_logits, 1)
                    dve.wait_ge(da_exped, u + 1)
                    settle(dve.reciprocal(drec, dsum))
                    if i == 0:
                        if a:
                            dve.wait_ge(job_done, done[("da_turn", a - 1, 0)])
                        dve.tensor_tensor(a_prob, e_prob, along(drec, T), ALU.mult).then_inc(da_probs, 1)
                    else:
                        settle(dve.tensor_scalar(drec, drec, neg_lam, None, ALU.mult))
                        settle(dve.tensor_tensor(e_prob, e_prob, along(drec, T), ALU.mult))
                        dve.wait_ge(da_probs, u)
                        dve.tensor_tensor(a_prob, a_prob, e_prob, ALU.add).then_inc(da_probs, 1)
                elif kind == "da_norm":
                    evacuated(s)
                    settle(dve.reciprocal(rstd, rstd))
                    bo = job_bank(("da_out", a, 0))
                    dve.scalar_tensor_tensor(yda[:, a, :], psum[:, bo, 0:T], da_gain, rstd, ALU.mult,
                                             ALU.mult).then_inc(bank_free[bo], 1)
                elif kind == "ret_score":
                    b = full(s)
                    if a:
                        dve.wait_ge(job_done, done[("ret_out", a - 1, 0)])
                    dve.tensor_tensor(ret_s, bank(b, 2, T), decay[:, 2 * a:2 * a + 2, :], ALU.mult).then_inc(bank_free[b], 1)
                elif kind == "ret_mean":
                    b = full(s)
                    dve.tensor_scalar(ret_stat, psum[:, b, 0:T], 1.0 / 256, None, ALU.mult).then_inc(bank_free[b], 1)
                    evacuated(s)
                    evacuated(("ret_out", a, 0))
                    dve.tensor_tensor(ret_o, ret_o, over(ret_stat, 2), ALU.subtract).then_inc(ret_centred, 1)
                elif kind == "ret_var":
                    evacuated(s)
                    settle(dve.reciprocal(ret_stat, ret_stat))
                    dve.tensor_tensor(ret_o, ret_o, over(ret_stat, 2), ALU.mult).then_inc(ret_normed, 1)
                    dve.wait_ge(ret_scaled, a + 1)
                    for k in range(1):
                        evacuated(("gemm", "r_g", a))
                        dve.tensor_tensor(yret[:, 2 * a:2 * a + 2, :], ret_o, rg[:, 2 * a:2 * a + 2, :],
                                          ALU.mult).then_inc(ret_y, 1)
                elif kind == "mem_score":
                    b = full(s)
                    dve.tensor_reduce(dmax, bank(b, 2, T), AX.X, ALU.max, negate=True).then_inc(mem_max, 1)
                    evacuated(s)
                    settle(dve.reciprocal(drec, dsum))
                    if a:
                        dve.wait_ge(job_done, done[("mem_turn", a - 1, 0)])
                    dve.tensor_tensor(a_prob, e_prob, along(drec, T), ALU.mult).then_inc(mem_probs, 1)
                elif kind == "gemm" and a.startswith("branch"):
                    n = int(a[-1])
                    b = full(s)
                    evacuated(("gemm", f"gate{n}", i))
                    mg = merged[:, 2 * i:2 * i + 2, :]
                    gt = gate[:, 2 * i:2 * i + 2, :]
                    if n == 0:
                        dve.tensor_tensor(mg, gt, bank(b, 2, T), ALU.mult).then_inc(bank_free[b], 1)
                    else:
                        dve.tensor_tensor(gtmp, gt, bank(b, 2, T), ALU.mult).then_inc(bank_free[b], 1)
                        evacuated(s)
                        evacuated(("gemm", f"branch{n - 1}", i))
                        settle(dve.tensor_tensor(mg, mg, gtmp, ALU.add))
                        if n == 2 and i == 3:
                            dve.sem_inc(merged_set, 1)
                elif kind == "gemm" and a == "w_o":
                    b = full(s)
                    dve.scalar_tensor_tensor(z[:, 2 * i:2 * i + 2, :], xT[:, 2 * i:2 * i + 2, :], ALPHA1, bank(b, 2, T),
                                             ALU.mult, ALU.add).then_inc(bank_free[b], 1)
                elif kind == "ada":
                    owed.append(s)
                    n = 12 * a + i + 1
                    if n < 24:
                        sum_modulation(n)
                    else:
                        add_modulation_bias(owed.pop())
                        evacuated(s)
                        evacuated(("ada", 1, 10))
                        dve.tensor_scalar(modp1, mod, 1.0, None, ALU.add).then_inc(modp1_set, 1)
                elif kind == "gemm" and a in ("ev_o", "od_o"):
                    b = full(s)
                    dve.wait_ge(acc_scaled, 2 if a == "ev_o" else 4)
                    for k in range(2):
                        n = 2 * i + k
                        ins = dve.scalar_tensor_tensor(acc[:, n, :], bank(b, 2, T)[:, k, :],
                                                       mod_cols(modp1, 0 if a == "ev_o" else 1, 2, n), acc[:, n, :],
                                                       ALU.mult, ALU.add)
                    ins.then_inc(bank_free[b], 1)
                elif kind == "gqa_score":
                    b = full(s)
                    if a == 0:
                        dve.wait_ge(small_in, 2 * 16)
                    if a:
                        dve.wait_ge(gqa_exped, a)
                    dve.scalar_tensor_tensor(logit2, wbias, 2.0 ** -(a + 1), bank(b, 2, T), ALU.mult,
                                             ALU.add).then_inc(bank_free[b], 1)
                    evacuated(s)
                    settle(dve.tensor_reduce(dmax, logit2, AX.X, ALU.max))
                    dve.tensor_scalar(dmax, dmax, sink[:, a:a + 1], -1.0, ALU.max, ALU.mult).then_inc(gqa_logits, 1)
                    dve.wait_ge(gqa_exped, a + 1)
                    settle(dve.tensor_tensor(dsum, dsum, esink, ALU.add))
                    settle(dve.reciprocal(drec, dsum))
                    if a:
                        dve.wait_ge(job_done, done[("gqa_turn", a - 1, 0)])
                    dve.tensor_tensor(a2, e2, along(drec, T), ALU.mult).then_inc(gqa_probs, 1)
                elif s == ("gemm", "od_v", 3):
                    dve.wait_ge(small_in, 6 * 16)
                    for n in range(4):
                        evacuated(("gemm", "od_v", n))
                    for t in range(TB):
                        for c in range(2):
                            settle(dve.bn_stats(bn_s[:, t, 6 * c:6 * c + 6], v_tok[:, t, c * 512:(c + 1) * 512]))
                        ins = dve.bn_aggr(bn_a[:, t, :], bn_s[:, t, 0:12])
                        if t == 0:
                            settle(ins)
                    ins.then_inc(v_normed, 1)
                    dve.wait_ge(v_normed, 2)
                    settle(dve.reciprocal(bn_a[:, :, 1:2], bn_a[:, :, 1:2]))
                    for t in range(TB):
                        settle(dve.tensor_scalar(v_tok[:, t, :], v_tok[:, t, :], bn_a[:, t, 0:1], bn_a[:, t, 1:2],
                                                 ALU.subtract, ALU.mult))
                    settle(dve.tensor_tensor(v_tok, v_tok, over(sg_rows[:, 0, :], TB), ALU.mult))
                    dve.tensor_tensor(v_tok, v_tok, over(sg_rows[:, 1, :], TB), ALU.add).then_inc(v_normed, 1)
                elif kind == "gate_s":
                    b = full(s)
                    evacuated(("gemm", "od_u", a))
                    for k in range(2):
                        ins = dve.tensor_tensor(e2[:, k, :].rearrange("p (c t) -> p c t", t=P), bank(b, 4, P)[:, 2 * k:2 * k + 2, :],
                                                over(bs_rows[:, 2 * a + k, :], 2), ALU.add)
                    ins.then_inc(bank_free[b], 1)
                    evacuated(s)
                    dve.tensor_tensor(mix[:, 2 * a:2 * a + 2, :], mix[:, 2 * a:2 * a + 2, :], e2,
                                      ALU.mult).then_inc(sg_gated, 1)
                    dve.wait_ge(sg_gated, a + 1)
                elif kind == "logits":
                    routing(a, full(s), s)
                elif kind == "turn_tok" and i == 3:
                    if a == 0:
                        dve.wait_ge(job_done, done[s])
                        dve.tensor_scalar(acc, acc, ALPHA1, None, ALU.mult).then_inc(acc_scaled, 1)
                elif kind == "rank":
                    b = full(s)
                    n = (G1, N2)[a]
                    settle(dve.tensor_copy(table[:, 0:2, 0:n], psum[:, b, 0:2 * n].rearrange("p (t e) -> p t e", e=n)))
                    dve.tensor_copy(counts_i[:, 0:n], psum[:, b, 2 * n:3 * n]).then_inc(bank_free[b], 1)
                elif kind == "ln_sum":
                    if a == 0:
                        for k in range(4):
                            evacuated(("gemm", "w_o", k))
                    src = z if a == 0 else acc

                    def modulate(part):
                        if 1 <= a <= 4:
                            layer, third = (a - 1) // 2, 3 * ((a - 1) % 2)
                            for k in (2 * part, 2 * part + 1):
                                dve.wait_ge(ln_out, KT * a + k + 1)
                                dve.tensor_scalar(hT[:, k, :], acc[:, k, :], mod_cols(modp1, layer, third + 1, k),
                                                  mod_cols(mod, layer, third, k), ALU.mult, ALU.add)\
                                   .then_inc(modulated, 1)

                    if a == 1:
                        dve.wait_ge(modp1_set, 1)
                    layer_norm_vector(dve, settle, a, src, done[s], job_bank(s), bank_through(s),
                                      bank_through(("ln_sq", a, 0)), modulate)
                    if 1 <= a <= 4:
                        dve.wait_ge(modulated, KT * a)
                        dve.tensor_scalar(acc, acc, ALPHA2, None, ALU.mult).then_inc(acc_scaled, 1)
                        dve.wait_ge(acc_scaled, a + 1)

        def own_tokens(f, u):
            k = f["weights"]
            dve.tensor_copy(mine.unsqueeze(2), table[:, :, bass.ds(u, 1)]).then_inc(mine_set, 1)
            dve.tensor_copy(mine_w[:, :, 0:k], weights[:, :, bass.ds(u * k, k)]).then_inc(mine_set, 1)
            dve.wait_ge(mine_set, u * 2 + 2 * (f["r0"] + (f["u0"] > 0) + 1))
            for t in range(TB):
                ins = dve.tensor_scalar(perm[:, t, :], iota, mine[:, t:t + 1], mine[:, TB + t:TB + t + 1],
                                        ALU.is_equal, ALU.mult)
            ins.then_inc(perm_set, 1)

        def unit(f):
            pairs, count = f["pairs"], f["count"]

            def take_tokens(fill, width, own):
                for i in range(4):
                    dve.wait_ge(x_hi_set, fill + ((i | 1 if own == P else i) + 1))
                    src = gather_bank(width, own, i)[:, :, 0:own] if f["routed"] else hT[:, 2 * i:2 * i + 2, :]
                    dve.tensor_tensor(x_lo[:, 2 * i:2 * i + 2, 0:own], src, x_hi[:, 2 * i:2 * i + 2, 0:own].bitcast(F32),
                                      ALU.subtract).then_inc(x_lo_set, 1)

            def add_output(value):
                for i in range(4):
                    dve.wait_ge(job_done, value + (i + 1))
                    add_to_result(i, f["gain"], added)

            def body(u, width, before, after):
                nt = width // P
                pos = f["pos"][isinstance(u, int)]
                make, split = h_point(f, width)
                jobs, c0, p0 = (at_unit(u, f["jobs"], f["at"]), at_unit(u, f["chunks"], f["c0"]),
                                at_unit(u, len(pairs), f["p0"]))
                fill = at_unit(u, 4, 4 * f["x0"])
                for q in f["order"]:
                    _, side, p, c = q
                    n = count[q]
                    dve.wait_ge(chunk_hi, c0 + (n + 1))
                    dve.tensor_tensor(chunk_view(stage_lo, f, side, p, c), chunk_source(f, side, p, c),
                                      chunk_view(stage_hi, f, side, p, c).bitcast(F32), ALU.subtract)\
                       .then_inc(chunk_lo, 1)
                    if n == (2 if f["routed"] else 0) and before is None:
                        take_tokens(fill, P, width)
                    if n == STAGES + 3:
                        if before is not None:
                            add_output(jobs + (pos[("scatter", 0)] - 1))
                        if f["routed"]:
                            dve.wait_ge(job_done, jobs + pos[("spread",)])
                            b, w_b = (7, 7) if width == P else (6, 7)
                            dve.tensor_copy(spread[:, 0:nt, :], bank(b, 2, T)[:, 0:nt, :])
                            dve.tensor_copy(own_w[:, 0:nt, 0:f["weights"]],
                                            bank(w_b, 16, 32)[:, 8:8 + nt, 0:f["weights"]]).then_inc(spread_set, 1)
                    if q in make:
                        p = make[q]
                        dve.wait_ge(silu_set, p0 + (p + 1))
                        if p:
                            dve.wait_ge(job_done, jobs + pos[("turn", p - 1)])
                        elif f["routed"]:
                            dve.wait_ge(spread_set, at_unit(u, 1, f["r0"] + 1))
                        for t in range(nt):
                            s_t, u_t, h_t = (s_tile[:, t, 0:pairs[p]], psum[:, 6 + t, 0:pairs[p]],
                                             h_tile[:, t, 0:pairs[p]])
                            if f["routed"]:
                                e = p if f["weights"] > 1 else 0
                                ins = dve.scalar_tensor_tensor(h_t, s_t, own_w[:, t, e:e + 1], u_t, ALU.mult,
                                                               ALU.mult)
                            else:
                                ins = dve.tensor_tensor(h_t, s_t, u_t, ALU.mult)
                        ins.then_inc(h_set, 1)
                        if p == 0 and f["routed"]:
                            dve.wait_ge(perm_set, at_unit(u, 1, f["r0"] + (f["u0"] > 0) + 1))
                            own_tokens(f, u + 1)
                    if q in split:
                        p = split[q]
                        dve.wait_ge(h_hi_set, p0 + (p + 1))
                        t0, blocks = (6 if width == T else 7), pairs[p] // P
                        for t in range(nt):
                            ins = dve.tensor_tensor(h_lo[:, 0:blocks, t * P:(t + 1) * P],
                                                    bank(t0 + t, 4, P)[:, 0:blocks, :],
                                                    h_hi[:, 0:blocks, t * P:(t + 1) * P].bitcast(F32), ALU.subtract)
                        ins.then_inc(h_lo_set, 1)
                if after is not None:
                    by_width(dve, after, lambda own: take_tokens(fill + 4, width, own))

            def tail(width):
                add_output(f["at"] + f["jobs"] * f["n"])

            return body, tail

        dve.wait_ge(cond_set, 1)
        sum_modulation(0)
        for n in range(3):
            f = feeds[n]
            walk(plans[n])
            dve.wait_ge(acc_scaled, (1, 3, 5)[n])
            if f["routed"]:
                evacuated(("rank", n // 2, 0))
                own_tokens(f, 0)
            units(dve, f, *unit(f))
            dve.wait_ge(added, 4 * (f["u0"] + f["n"]))
        walk(plans[3])

    @block.tensor
    def _(pe):
        def open_bank(s):
            n = index[s]
            if n >= BANKS:
                pe.wait_ge(bank_free[n % BANKS], n // BANKS)
            return n % BANKS

        def evacuated(s):
            pe.wait_ge(*bank_through(s))

        def turn4(s, pairs):
            b = open_bank(s)
            for n, (src, col) in enumerate(pairs):
                ins = pe.transpose(psum[0:src.shape[1], b, col:col + src.shape[0]], src,
                                   ident[0:src.shape[0], 0:src.shape[0]])
            ins.then_inc(job_done, 1)

        rhs_of = {"m_k": memT, "m_v": memT, "branch0": yda, "branch1": yret, "branch2": ymem, "w_o": merged,
                  "ev_p": hT, "ev_q": hT, "ev_o": mix, "od_u": hT, "od_v": hT, "od_o": mix}
        pe.wait_ge(const_in, 16)
        pe.wait_ge(ones_set, 2)
        def walk(plan):
            for s in plan:
                kind, a, i = s
                if kind == "vec":
                    pe.wait_ge(vec_in, 16 * 13)
                    rows = (vec_a, vec_b)[a]
                    n = vec_rows[a]
                    b = open_bank(s)
                    pe.transpose(psum[:, b, 0:n], rows[0:n, :], ident[0:n, 0:n]).then_inc(job_done, 1)
                elif kind in ("turn_x", "turn_mem"):
                    pe.wait_ge(*((x_in, 16) if kind == "turn_x" else (mem_in, 16)))
                    src = x_tok if kind == "turn_x" else mem_tok
                    turn4(s, [(src[:, t, (2 * a + k) * P:(2 * a + k + 1) * P], k * T + t * P)
                              for k in range(2) for t in range(TB)])
                elif kind == "gemm":
                    at, fills = panel_of(s)
                    if i == 0:
                        if a == "da_q":
                            for n in range(4):
                                evacuated(("turn_x", n, 0))
                        elif a == "m_k":
                            for n in range(4):
                                evacuated(("turn_mem", n, 0))
                        elif a == "branch0":
                            evacuated(("da_out", DA_H - 1, 0))
                            for n in range(DA_H):
                                evacuated(("da_out", n, 0))
                        elif a == "branch1":
                            pe.wait_ge(ret_y, RET_H)
                        elif a == "branch2":
                            for n in range(MEM_H):
                                evacuated(("mem_out", n, 0))
                        elif a == "w_o":
                            pe.wait_ge(merged_set, 1)
                        elif a == "ev_o":
                            evacuated(("pool_map", 0, 0))
                            evacuated(("pool_map", 1, 0))
                            for n in range(GQA_H):
                                evacuated(("gqa_out", n, 0))
                        elif a == "od_o":
                            pe.wait_ge(sg_gated, 4)
                    pe.wait_ge(slot_full[at], 16 * fills)
                    rhs = rhs_of.get(a, xT)
                    b = open_bank(s)
                    wt = slot(at, KT)
                    if a in token_major:
                        for k in range(KT):
                            if i == 0 and a == "od_v":
                                pe.wait_ge(modulated, 2 * KT + k + 1)
                            ins = pe.matmul(bank(b), rhs[:, k, i % 2 * P:(i % 2 + 1) * P], wt[:, k, :],
                                            start=(k == 0), stop=(k == KT - 1))
                    else:
                        for m in range(2):
                            c = (i % 2 * 2 + m) * P
                            for k in range(KT):
                                if i == 0 and m == 0 and a == "ev_q":
                                    pe.wait_ge(modulated, k + 1)
                                ins = pe.matmul(bank(b, 2, T)[:, m, :], wt[:, k, c:c + P], rhs[:, k, :],
                                                start=(k == 0), stop=(k == KT - 1))
                    ins.then_inc(job_done, 1)
                elif kind == "da_score":
                    b = open_bank(s)
                    if a % 2 == 0 and i == 0:
                        evacuated(("gemm", "da_q", a // 2))
                        evacuated(("gemm", "da_k", a // 2))
                    for t in range(TB):
                        ins = pe.matmul(bank(b, 2, T)[:, t, :], daq[64 * i:64 * i + 64, a, t * P:(t + 1) * P],
                                        dak[64 * i:64 * i + 64, a, :], start=True, stop=True)
                    ins.then_inc(job_done, 1)
                elif kind == "da_turn":
                    pe.wait_ge(da_probs, 2 * a + 2)
                    turn4(s, [(a_prob[:, t, k * P:(k + 1) * P], k * T + t * P) for k in range(2) for t in range(TB)])
                elif kind == "da_out":
                    evacuated(("da_turn", a, 0))
                    if a == 0:
                        for n in range(4):
                            evacuated(("gemm", "da_v", n))
                    b = open_bank(s)
                    for k in range(TB):
                        ins = pe.matmul(psum[:, b, 0:T], dav[:, k, a * P:(a + 1) * P], a_turn[:, k, :], start=(k == 0),
                                        stop=(k == TB - 1))
                    ins.then_inc(job_done, 1)
                elif kind == "da_norm":
                    pe.wait_ge(da_squared, a + 1)
                    b = open_bank(s)
                    pe.matmul(psum[:, b, 0:T], ones, osq, start=True, stop=True).then_inc(job_done, 1)
                elif kind == "ret_score":
                    if a == 0:
                        for n, k in (("r_q", 2), ("r_k", 2), ("r_v", 4)):
                            for m in range(k):
                                evacuated(("gemm", n, m))
                    b = open_bank(s)
                    for k in range(TB):
                        ins = pe.matmul(bank(b, 2, T)[:, k, :], rk[:, a, k * P:(k + 1) * P], rq[:, a, :], start=True,
                                        stop=True)
                    ins.then_inc(job_done, 1)
                elif kind == "ret_out":
                    evacuated(("ret_score", a, 0))
                    b = open_bank(s)
                    for m in range(2):
                        for k in range(TB):
                            c = (2 * a + m) * P
                            ins = pe.matmul(bank(b, 2, T)[:, m, :], rv[:, k, c:c + P], ret_s[:, k, :], start=(k == 0),
                                            stop=(k == TB - 1))
                    ins.then_inc(job_done, 1)
                elif kind in ("ret_mean", "ret_var"):
                    if kind == "ret_mean":
                        evacuated(("ret_out", a, 0))
                    else:
                        pe.wait_ge(ret_squared, a + 1)
                    src = ret_o if kind == "ret_mean" else ret_sq
                    b = open_bank(s)
                    for k in range(2):
                        ins = pe.matmul(psum[:, b, 0:T], ones, src[:, k, :], start=(k == 0), stop=(k == 1))
                    ins.then_inc(job_done, 1)
                elif kind == "mem_score":
                    if a == 0:
                        for n in ("m_q", "m_k"):
                            for m in range(4):
                                evacuated(("gemm", n, m))
                    b = open_bank(s)
                    for t in range(TB):
                        for k in range(2):
                            ins = pe.matmul(bank(b, 2, T)[:, t, :], mq[:, 2 * a + k, t * P:(t + 1) * P],
                                            mk[:, 2 * a + k, :], start=(k == 0), stop=(k == 1))
                    ins.then_inc(job_done, 1)
                elif kind == "mem_turn":
                    pe.wait_ge(mem_probs, a + 1)
                    turn4(s, [(a_prob[:, t, k * P:(k + 1) * P], k * T + t * P) for k in range(2) for t in range(TB)])
                elif kind == "mem_out":
                    evacuated(("mem_turn", a, 0))
                    if a == 0:
                        for n in range(4):
                            evacuated(("gemm", "m_v", n))
                    b = open_bank(s)
                    for m in range(2):
                        for k in range(TB):
                            c = (2 * a + m) * P
                            ins = pe.matmul(bank(b, 2, T)[:, m, :], mv[:, k, c:c + P], a_turn[:, k, :], start=(k == 0),
                                            stop=(k == TB - 1))
                    ins.then_inc(job_done, 1)
                elif kind in ("ln_sum", "ln_sq"):
                    b = open_bank(s)
                    src = (z if a == 0 else acc) if kind == "ln_sum" else (z_sq if a == 0 else later_sq)
                    for k in range(KT):
                        if kind == "ln_sq" and k % 2 == 0:
                            pe.wait_ge(ln_squared, 4 * a + k // 2 + 1)
                        elif k % 2 == 0 and a in (0, 2, 4):
                            evacuated(("gemm", ("w_o", "ev_o", "od_o")[a // 2], k // 2))
                        elif k % 2 == 0:
                            pe.wait_ge(added, 4 * (feeds[a // 2]["u0"] + feeds[a // 2]["n"]) - 3 + k // 2)
                        ins = pe.matmul(psum[:, b, 0:T], ones, src[:, k, :], start=(k == 0), stop=(k == KT - 1))
                    ins.then_inc(job_done, 1)
                elif kind == "ada":
                    pe.wait_ge(ada_summed, 12 * a + i + 1)
                    b = open_bank(s)
                    for m in range(4):
                        ins = pe.matmul(psum[:, b, m:m + 1], ada_sum[:, (12 * a + i) % 2, m * P:(m + 1) * P],
                                        ones[:, 0:1], start=True, stop=True)
                    ins.then_inc(job_done, 1)
                elif kind == "logits":
                    if a == 0:
                        pe.wait_ge(router_in, 3 * 16)
                    b = open_bank(s)
                    n = router[a].shape[2]
                    for t in range(TB):
                        for k in range(KT):
                            if t == 0:
                                pe.wait_ge(*((ln_out, k + 1) if a == 0 else (modulated, 3 * KT + k + 1)))
                            ins = pe.matmul(psum[:, b, t * n:(t + 1) * n], (acc, hT)[a][:, k, t * P:(t + 1) * P],
                                            router[a][:, k, :], start=(k == 0), stop=(k == KT - 1))
                    ins.then_inc(job_done, 1)
                elif kind == "turn_tok":
                    src, t, k0 = (acc, hT)[a], i // 2, i % 2 * 4
                    turn4(s, [(src[:, k0 + k, t * P:(t + 1) * P], k * P) for k in range(4)])
                elif kind == "turn_out":
                    t, k0 = a // 2, a % 2 * 4
                    pe.wait_ge(ln_out, 5 * KT + k0 + 4)
                    turn4(s, [(acc[:, k0 + k, t * P:(t + 1) * P], k * P) for k in range(4)])
                elif kind == "rank":
                    pe.wait_ge(masks_set, a + 1)
                    b = open_bank(s)
                    n = (G1, N2)[a]
                    mask = [table[:, 2 + t, 0:n] for t in range(TB)]
                    for c, terms in enumerate((((ustrict, 0),), ((ustrict, 1), (ones, 0)), ((ones, 0), (ones, 1)))):
                        for k, (lhs, t) in enumerate(terms):
                            ins = pe.matmul(psum[:, b, c * n:(c + 1) * n], lhs, mask[t], start=(k == 0),
                                            stop=(k == len(terms) - 1))
                    ins.then_inc(job_done, 1)
                elif kind in ("ev_k", "ev_v"):
                    at, fill = panel[("ev_k", 0, 0)]
                    pe.wait_ge(slot_full[at], 16 * fill)
                    wt = slot(at, KT, KT * 256)
                    b = open_bank(s)
                    if kind == "ev_k":
                        for k in range(KT):
                            ins = pe.matmul(psum[:, b, 0:T], wt[:, k, 0:P], hT[:, k, :], start=(k == 0),
                                            stop=(k == KT - 1))
                    else:
                        for t in range(TB):
                            for k in range(KT):
                                ins = pe.matmul(psum[:, b, t * P:(t + 1) * P], hT[:, k, t * P:(t + 1) * P],
                                                wt[:, k, P:2 * P], start=(k == 0), stop=(k == KT - 1))
                    ins.then_inc(job_done, 1)
                elif kind in ("pool", "pool_map"):
                    if kind == "pool":
                        pe.wait_ge(small_in, 2 * 16)
                        evacuated(("gemm", "ev_p", 0))
                        evacuated(("gemm", "ev_p", 1))
                    else:
                        evacuated(("pool", a, 0))
                    b = open_bank(s)
                    for m in range(2):
                        g = 2 * a + m
                        if kind == "pool":
                            for t in range(TB):
                                ins = pe.matmul(bank(b, 2, T)[:, m, :], p_tok[:, t, g * P:(g + 1) * P],
                                                pool_m[:, 2 * g + t, :], start=(t == 0), stop=(t == 1))
                        else:
                            ins = pe.matmul(bank(b, 2, T)[:, m, :], w_pool[:, g, :], pooled[:, g, :], start=True,
                                            stop=True)
                    ins.then_inc(job_done, 1)
                elif kind == "gqa_score":
                    if a == 0:
                        for n in (("gemm", "ev_q", 0), ("gemm", "ev_q", 1), ("ev_k", 0, 0)):
                            evacuated(n)
                    b = open_bank(s)
                    p0 = 64 * (a % 2)
                    for t in range(TB):
                        ins = pe.matmul(bank(b, 2, T)[:, t, :], q2[p0:p0 + 64, a // 2, t * P:(t + 1) * P],
                                        k2[p0:p0 + 64, a // 4, :], start=True, stop=True)
                    ins.then_inc(job_done, 1)
                elif kind == "gqa_turn":
                    pe.wait_ge(gqa_probs, a + 1)
                    turn4(s, [(a2[:, t, k * P:(k + 1) * P], k * T + t * P) for k in range(2) for t in range(TB)])
                elif kind == "gqa_out":
                    evacuated(("gqa_turn", a, 0))
                    if a == 0:
                        evacuated(("ev_v", 0, 0))
                    b = open_bank(s)
                    p0, c0 = 64 * (a % 2), 64 * (a // 4)
                    for k in range(TB):
                        ins = pe.matmul(psum[p0:p0 + 64, b, 0:T], v2[:, k, c0:c0 + 64], at2[:, k, :],
                                        start=(k == 0), stop=(k == TB - 1))
                    ins.then_inc(job_done, 1)
                elif kind == "turn_ws":
                    pe.wait_ge(small_in, 6 * 16)
                    turn4(s, [(w_s[:, 4 * a + k, :], k * P) for k in range(4)])
                elif kind == "gate_s":
                    if a == 0:
                        pe.wait_ge(v_normed, 3)
                        evacuated(("turn_ws", 0, 0))
                        evacuated(("turn_ws", 1, 0))
                    b = open_bank(s)
                    for m in range(2):
                        for t in range(TB):
                            g = 2 * a + m
                            ins = pe.matmul(bank(b, 4, P)[:, 2 * m + t, :], v_tok[:, t, g * P:(g + 1) * P],
                                            ws_t[:, g, :], start=True, stop=True)
                    ins.then_inc(job_done, 1)

        def unit(f):
            pairs, count = f["pairs"], f["count"]

            def products(dsts, lhs, rhs, first, last):
                (lhs_hi, lhs_lo), terms = lhs, []
                for n, (dst, (rhs_hi, rhs_lo)) in enumerate(zip(dsts, rhs)):
                    terms += [(dst, lhs_hi, rhs_hi, first, False), (dst, lhs_hi, rhs_lo, False, False)]
                for dst, (rhs_hi, _) in zip(dsts, rhs):
                    terms.append((dst, lhs_lo, rhs_hi, False, last))
                for dst, a, b, start, stop in terms:
                    ins = pe.matmul(dst, a, b, start=start, stop=stop)
                return ins

            def gather(width, own, table, fill):
                pe.wait_ge(perm_set, table)
                for i in range(4):
                    if own == T and i >= 2:
                        pe.wait_ge(x_lo_set, fill + (i - 1))
                    for k in range(2):
                        for t in range(TB):
                            c = (2 * i + k) * P
                            ins = pe.matmul(gather_bank(width, own, i)[:, k, 0:own], tok[:, t, c:c + P],
                                            perm[:, t, 0:own], start=(t == 0), stop=(t == TB - 1))
                    ins.then_inc(job_done, 1)

            def scatter(width, value):
                pe.wait_ge(y_copied, value)
                for i in range(4):
                    for k in range(2):
                        at = (2 * i + k) * P
                        for c in range(width // P):
                            src = y_tok[:, c, at:at + P]
                            if f["routed"]:
                                ins = pe.matmul(bank(i, 2, T)[:, k, :], src, spread[:, c, :], start=(c == 0),
                                                stop=(c == width // P - 1))
                            else:
                                ins = pe.transpose(bank(i, 2, T)[:, k, c * P:(c + 1) * P], src, ident)
                    ins.then_inc(job_done, 1)

            def turn_table(nt):
                b, w_b = (7, 7) if nt == 1 else (6, 7)
                for c in range(nt):
                    for t in range(TB):
                        pe.transpose(bank(b, 2, T)[:, c, t * P:(t + 1) * P], perm[:, t, c * P:(c + 1) * P], ident)
                for c in range(nt):
                    for t in range(TB):
                        ins = pe.matmul(bank(w_b, 16, 32)[:, 8 + c, 0:f["weights"]], perm[:, t, c * P:(c + 1) * P],
                                        mine_w[:, t, 0:f["weights"]], start=(t == 0), stop=(t == TB - 1))
                ins.then_inc(job_done, 1)

            def body(u, width, before, after):
                nt = width // P
                first = isinstance(u, int)
                c0, p0 = at_unit(u, f["chunks"], f["c0"]), at_unit(u, len(pairs), f["p0"])
                table, fill = at_unit(u, 1, f["r0"] + (f["u0"] > 0) + 1), at_unit(u, 4, 4 * f["x0"])
                if f["routed"] and first:
                    gather(P, width, table, fill)
                if not first:
                    pe.wait_ge(x_lo_set, fill + 4)
                for q in f["steps"][first]:
                    if q[0] == "chunk":
                        _, side, p, c = q
                        n = count[q]
                        if side == "D":
                            if c == 0:
                                pe.wait_ge(h_lo_set, p0 + (p + 1))
                                if p == 0 and not first:
                                    pe.wait_ge(added, at_unit(u, 4, 4 * f["u0"]))
                        elif c == 0 and p and (side == "U" or width == T):
                            pe.wait_ge(h_set, p0 + p)
                            if side == "U" and width == T:
                                pe.wait_ge(h_lo_set, p0 + p)
                        elif c == 0 and p > 1:
                            pe.wait_ge(h_set, p0 + (p - 1))
                        elif c == 0 and side == "U" and width == T and f["routed"]:
                            pe.wait_ge(spread_set, at_unit(u, 1, f["r0"] + 1))
                        if first and side == "G" and p == 0:
                            pe.wait_ge(x_lo_set, fill + (c + 1))
                        pe.wait_ge(chunk_lo, c0 + (n + 1))
                        hi, lo = chunk_view(stage_hi, f, side, p, c), chunk_view(stage_lo, f, side, p, c)
                        if side == "D":
                            for t in range(nt):
                                part = slice(t * P, (t + 1) * P)
                                ins = products([psum[:, 2 * t + m, :] for m in range(2)],
                                               (h_hi[:, c, part], h_lo[:, c, part]),
                                               [(hi[:, 0, m * PANEL:(m + 1) * PANEL],
                                                 lo[:, 0, m * PANEL:(m + 1) * PANEL]) for m in range(2)],
                                               p == 0 and c == 0, p == len(pairs) - 1 and c == pairs[p] // P - 1)
                        else:
                            b0 = 6 if side == "U" else 4 if width == T else 4 + p % 2
                            for k in range(2):
                                for t in range(nt):
                                    part = slice(t * P, (t + 1) * P)
                                    ins = products([psum[:, b0 + t, 0:pairs[p]]],
                                                   (x_hi[:, 2 * c + k, part], x_lo[:, 2 * c + k, part]),
                                                   [(hi[:, k, :], lo[:, k, :])], c == 0 and k == 0,
                                                   c == 3 and k == 1)
                        ins.then_inc(job_done, 1)
                    elif q[0] == "turn":
                        p = q[1]
                        pe.wait_ge(h_set, p0 + (p + 1))
                        if p == 0 and f["routed"]:
                            pe.wait_ge(spread_set, at_unit(u, 1, f["r0"] + 1))
                        t0 = 6 if width == T else 7
                        for t in range(nt):
                            for j in range(pairs[p] // P):
                                ins = pe.transpose(bank(t0 + t, 4, P)[:, j, :], h_tile[:, t, j * P:(j + 1) * P], ident)
                        ins.then_inc(job_done, 1)
                    elif q == ("scatter", 0):
                        by_width(pe, before, lambda own: scatter(own, at_unit(u, 1, f["u0"])))
                    elif q == ("spread",):
                        turn_table(nt)
                    elif q == ("gather", 0):
                        by_width(pe, after, lambda own: gather(width, own, table + 1, fill + 4))

            def tail(width):
                pe.wait_ge(x_lo_set, 4 * (f["x0"] + f["n"] + f["routed"]))
                scatter(width, f["u0"] + f["n"])

            return body, tail

        for n in range(3):
            walk(plans[n])
            if feeds[n]["routed"]:
                evacuated(("rank", n // 2, 0))
            for s in plans[n][-8:]:
                evacuated(s)
            units(pe, feeds[n], *unit(feeds[n]))
            if job_bank(plans[n + 1][0]) < 4:
                pe.wait_ge(added, 4 * (feeds[n]["u0"] + feeds[n]["n"]))
            pe.wait_ge(h_lo_set, feeds[n]["p0"] + len(feeds[n]["pairs"]) * feeds[n]["n"])
        walk(plans[3])

    ctx.close()


_OUT = (1, T, D)


def kernel(**inputs):
    import concourse.bacc as bacc
    from concourse.bass_utils import run_bass_kernel_spmd

    nc = bacc.Bacc("TRN2", target_bir_lowering=False, num_devices=1)
    arrays, w = {}, {}
    for name, value in {**inputs, "consts": shape_constants()}.items():
        a = np.ascontiguousarray(value)
        arrays[name + "_in"] = a
        w[name] = nc.dram_tensor(name + "_in", a.shape, mybir.dt.from_np(a.dtype), kind="ExternalInput").ap()
    out = nc.dram_tensor("out", (T, D), F32, kind="ExternalOutput").ap()
    build(nc, w, out)
    return run_bass_kernel_spmd(nc, [arrays], core_ids=[0]).results[0]["out"].reshape(_OUT)
```
